# Optimizing a Trainium2 kernel written in Bass

```python
import math
import jax, jax.numpy as jnp
from jax import lax
import numpy as np

D_MODEL = 1024
BATCH = 1
SEQ = 512
DEPTH = 2

HEAD_DIM = 64
N_A_LAYERS = DEPTH // 2
N_B_LAYERS = DEPTH - N_A_LAYERS
FOX_HEADS = D_MODEL // HEAD_DIM
SWA_Q_HEADS = D_MODEL // HEAD_DIM
SWA_KV_HEADS = SWA_Q_HEADS // 8
SWA_GROUP = SWA_Q_HEADS // SWA_KV_HEADS
WINDOW = 128
Q_BLOCK = 128
D_FF = 4 * D_MODEL
N_BUCKETS = 32
REL_MAX_DIST = 128
NORM_EPS = 1e-6

kernel_name = "yoco_fox_swa_sink_hybrid"

def _rmsnorm(x, g):
    xf = x.astype(jnp.float32)
    y = xf * lax.rsqrt(jnp.mean(xf * xf, axis=-1, keepdims=True) + NORM_EPS)
    return (y * g.astype(jnp.float32)).astype(x.dtype)

def _t5_causal_bucket(dist):
    n = np.maximum(dist, 0)
    max_exact = N_BUCKETS // 2
    large = max_exact + (np.log(np.maximum(n, 1) / max_exact)
                         / np.log(REL_MAX_DIST / max_exact)
                         * (N_BUCKETS - max_exact)).astype(np.int32)
    large = np.minimum(large, N_BUCKETS - 1)
    return np.where(n < max_exact, n, large).astype(np.int32)

def _sq_relu_mlp(h, w_up, w_down):
    u = h @ w_up
    return (jnp.square(jax.nn.relu(u))) @ w_down

def _fox_attention(h, w_in, b_f, g_q, g_k, w_out):
    bsz, seq, _ = h.shape
    hw = FOX_HEADS * HEAD_DIM
    proj = h @ w_in
    q = _rmsnorm(proj[..., :hw].reshape(bsz, seq, FOX_HEADS, HEAD_DIM), g_q)
    k = _rmsnorm(proj[..., hw:2 * hw].reshape(bsz, seq, FOX_HEADS, HEAD_DIM), g_k)
    v = proj[..., 2 * hw:3 * hw].reshape(bsz, seq, FOX_HEADS, HEAD_DIM)
    log_f = jax.nn.log_sigmoid(proj[..., 3 * hw:].astype(jnp.float32)
                               + b_f.astype(jnp.float32))
    c = jnp.cumsum(log_f, axis=1).transpose(0, 2, 1)
    scale = HEAD_DIM ** -0.5
    outs = []
    for blk in range(seq // Q_BLOCK):
        t0, t1 = blk * Q_BLOCK, (blk + 1) * Q_BLOCK
        s = jnp.einsum('bqhd,bkhd->bhqk', q[:, t0:t1], k[:, :t1]).astype(jnp.float32) * scale
        s = s + c[:, :, t0:t1, None] - c[:, :, None, :t1]
        mask = np.arange(t1)[None, :] <= np.arange(t0, t1)[:, None]
        s = jnp.where(mask, s, -jnp.inf)
        p = jax.nn.softmax(s, axis=-1).astype(v.dtype)
        outs.append(jnp.einsum('bhqk,bkhd->bqhd', p, v[:, :t1]))
    o = jnp.concatenate(outs, axis=1).reshape(bsz, seq, hw)
    return o @ w_out

def _shared_kv(h, g_kv, w_kv, g_k):
    bsz, seq, _ = h.shape
    kvw = SWA_KV_HEADS * HEAD_DIM
    kv = _rmsnorm(h, g_kv) @ w_kv
    k = _rmsnorm(kv[..., :kvw].reshape(bsz, seq, SWA_KV_HEADS, HEAD_DIM), g_k)
    v = kv[..., kvw:].reshape(bsz, seq, SWA_KV_HEADS, HEAD_DIM)
    return k, v

def _band(x):
    bsz, seq = x.shape[:2]
    xb = x.reshape(bsz, seq // WINDOW, WINDOW, *x.shape[2:])
    prev = jnp.pad(xb[:, :-1], ((0, 0), (1, 0), (0, 0), (0, 0), (0, 0)))
    return jnp.concatenate([prev, xb], axis=2)

def _swa_sink_attention(h, w_q, g_q, k_band, v_band, sinks, rel_bias, w_out):
    bsz, seq, _ = h.shape
    nblk = seq // WINDOW
    q = _rmsnorm((h @ w_q).reshape(bsz, seq, SWA_Q_HEADS, HEAD_DIM), g_q)
    qb = q.reshape(bsz, nblk, WINDOW, SWA_KV_HEADS, SWA_GROUP, HEAD_DIM)
    s = jnp.einsum('bnqkgd,bnjkd->bnkgqj', qb, k_band).astype(jnp.float32) * (HEAD_DIM ** -0.5)
    dist = np.arange(WINDOW)[:, None] + WINDOW - np.arange(2 * WINDOW)[None, :]
    bias = rel_bias.astype(jnp.float32)[_t5_causal_bucket(dist)]
    bias = bias.transpose(2, 0, 1).reshape(SWA_KV_HEADS, SWA_GROUP, WINDOW, 2 * WINDOW)
    s = s + bias[None, None]
    valid = (dist >= 0) & (dist < WINDOW)
    blk_ok = (np.arange(nblk)[:, None] > 0) | (np.arange(2 * WINDOW)[None, :] >= WINDOW)
    mask = valid[None, :, :] & blk_ok[:, None, :]
    s = jnp.where(mask[None, :, None, None], s, -jnp.inf)
    sink = jnp.broadcast_to(
        sinks.astype(jnp.float32).reshape(1, 1, SWA_KV_HEADS, SWA_GROUP, 1, 1),
        s.shape[:-1] + (1,))
    p = jax.nn.softmax(jnp.concatenate([s, sink], axis=-1), axis=-1)[..., :-1]
    o = jnp.einsum('bnkgqj,bnjkd->bnqkgd', p.astype(v_band.dtype), v_band)
    return o.reshape(bsz, seq, SWA_Q_HEADS * HEAD_DIM) @ w_out

def setup_inputs(seed: int = 0) -> dict:
    key = jax.random.key(seed)
    ks = jax.random.split(key, 20)
    f32 = jnp.float32
    hw = FOX_HEADS * HEAD_DIM
    qw = SWA_Q_HEADS * HEAD_DIM
    kvw = SWA_KV_HEADS * HEAD_DIM

    def nrm(k, shape, fan_in):
        return jax.random.normal(k, shape, f32) * (fan_in ** -0.5)

    def gain(k, shape):
        return 1.0 + 0.05 * jax.random.normal(k, shape, f32)

    return {
        "x": jax.random.normal(ks[0], (BATCH, SEQ, D_MODEL), f32),
        "g_attn": gain(ks[1], (DEPTH, D_MODEL)),
        "g_mlp": gain(ks[2], (DEPTH, D_MODEL)),
        "w_in_a": nrm(ks[3], (N_A_LAYERS, D_MODEL, 3 * hw + FOX_HEADS), D_MODEL),
        "b_f": 3.0 + 0.5 * jax.random.normal(ks[4], (N_A_LAYERS, FOX_HEADS), f32),
        "gq_a": gain(ks[5], (N_A_LAYERS, HEAD_DIM)),
        "gk_a": gain(ks[6], (N_A_LAYERS, HEAD_DIM)),
        "w_out_a": nrm(ks[7], (N_A_LAYERS, hw, D_MODEL), hw),
        "g_kv": gain(ks[8], (D_MODEL,)),
        "w_kv": nrm(ks[9], (D_MODEL, 2 * kvw), D_MODEL),
        "gk_b": gain(ks[10], (HEAD_DIM,)),
        "w_q_b": nrm(ks[11], (N_B_LAYERS, D_MODEL, qw), D_MODEL),
        "gq_b": gain(ks[12], (N_B_LAYERS, HEAD_DIM)),
        "sinks": 0.5 * jax.random.normal(ks[13], (N_B_LAYERS, SWA_Q_HEADS), f32),
        "rel_bias": 0.2 * jax.random.normal(ks[14], (N_BUCKETS, SWA_Q_HEADS), f32),
        "w_out_b": nrm(ks[15], (N_B_LAYERS, qw, D_MODEL), qw),
        "w_up": nrm(ks[16], (DEPTH, D_MODEL, D_FF), D_MODEL),
        "w_down": nrm(ks[17], (DEPTH, D_FF, D_MODEL), D_FF),
    }

def reference(x, g_attn, g_mlp, w_in_a, b_f, gq_a, gk_a, w_out_a, g_kv, w_kv, gk_b,
              w_q_b, gq_b, sinks, rel_bias, w_out_b, w_up, w_down):
    h = x
    k_band = None
    v_band = None
    for layer in range(DEPTH):
        if layer < N_A_LAYERS:
            a = layer
            h = h + _fox_attention(_rmsnorm(h, g_attn[layer]), w_in_a[a], b_f[a],
                                   gq_a[a], gk_a[a], w_out_a[a])
        else:
            b = layer - N_A_LAYERS
            if b == 0:
                k_sh, v_sh = _shared_kv(h, g_kv, w_kv, gk_b)
                k_band, v_band = _band(k_sh), _band(v_sh)
            h = h + _swa_sink_attention(_rmsnorm(h, g_attn[layer]), w_q_b[b], gq_b[b],
                                        k_band, v_band, sinks[b], rel_bias, w_out_b[b])
        h = h + _sq_relu_mlp(_rmsnorm(h, g_mlp[layer]), w_up[layer], w_down[layer])
    return h


_drawn_inputs = setup_inputs


def setup_inputs(seed=0):
    import zlib

    import numpy as np

    out = dict(_drawn_inputs(seed))
    spreads = {}
    factors = {'gq_a': 3.57,
     'gk_a': 3.5,
     'g_kv': 5.081,
     'gk_b': 8.0,
     'gq_b': 8.0,
     'sinks': 64.0,
     'rel_bias': 3.375}
    for name, (base, spread) in spreads.items():
        noise = np.random.default_rng([zlib.crc32(name.encode()), seed]).standard_normal(out[name].shape)
        drawn = base * np.exp(spread * noise) if base else spread * noise
        out[name] = __import__('jax').numpy.asarray(drawn.astype(out[name].dtype))
    for name, factor in factors.items():
        out[name] = (out[name] * factor).astype(out[name].dtype)
    return out
```

```python
from contextlib import ExitStack

import numpy as np

import concourse.bass as bass
from concourse import mybir

ALU = mybir.AluOpType
ACT = mybir.ActivationFunctionType
F32 = mybir.dt.float32
F32R = mybir.dt.float32r
AX_X = mybir.AxisListType.X

P = 128
D = 1024
T = 512
HD = 64
HEADS = 16
PAIRS = HEADS // 2
F = 4 * D
KC = D // P
TB = T // P
FH = F // 2 // P
WINDOW = 128
N_BUCKETS = 32
REL_MAX_DIST = 128
EPS = 1e-6
NEG = -1e30
UNIT = 2048

U_V = 0
U_PAIR = 4
U_OUT = [12, 53]
U_UP = [16, 32, 57, 73]
U_DOWN = [24, 40, 65, 81]
U_KV = 48
U_Q = 49
N_UNITS = 89

FILL_ATTN0, FILL_OUT_A, FILL_MLP0, FILL_KV, FILL_Q, FILL_OUT_B, FILL_MLP1 = range(7)
GAIN = {FILL_ATTN0: 0, FILL_MLP0: 1, FILL_KV: 2, FILL_Q: 3, FILL_MLP1: 4}
XF_ORDER = {FILL_ATTN0: 0, FILL_MLP0: 1, FILL_KV: 2, FILL_Q: 3, FILL_MLP1: 4}

C_IDENT, C_BLK, C_OND, C_SINK = 0, 128, 256, 384
C_TEMP = 576
C_ANTI, C_ONES, C_MASKA, C_MASKT, C_HOT, C_NEG = 576, 704, 832, 960, 1088, 1856
C_ALL = 2624


def shape_constants():
    c = np.zeros((P, C_ALL), np.float32)
    c[:, C_IDENT:C_IDENT + P] = np.eye(P)
    for b in range(2):
        c[64 * b:64 * b + 64, C_BLK + 64 * b:C_BLK + 64 * b + 64] = 1.0 / HD
    c[:, C_OND:C_OND + P] = 1.0 / D
    c[:, C_SINK + 64:C_SINK + 128] = 1.0 / P
    c[:, C_ANTI:C_ANTI + P] = np.eye(P)[::-1]
    c[:, C_ONES:C_ONES + P] = 1.0
    r = np.arange(P)
    c[:, C_MASKA:C_MASKA + P] = np.where(r[None, :] > r[:, None], NEG, 0.0)
    c[:, C_MASKT:C_MASKT + P] = np.where(r[:, None] > r[None, :], NEG, 0.0)
    d = np.arange(WINDOW)
    exact = N_BUCKETS // 2
    large = exact + (np.log(np.maximum(d, 1) / exact) / np.log(REL_MAX_DIST / exact)
                     * (N_BUCKETS - exact)).astype(np.int32)
    bucket = np.where(d < exact, d, np.minimum(large, N_BUCKETS - 1))
    c[:, C_NEG:C_NEG + 768] = NEG
    for dist in range(WINDOW):
        for col in (127 + dist, 384 + 255 - dist):
            c[bucket[dist], C_HOT + col] = 1.0
            c[:, C_NEG + col] = 0.0
    return c


def build(nc, x, g_attn, g_mlp, w_in_a, b_f, gq_a, gk_a, w_out_a, g_kv, w_kv, gk_b,
          w_q_b, gq_b, sinks, rel_bias, w_out_b, w_up, w_down, consts, out):
    with ExitStack() as ctx:
        base = nc.sbuf_base
        room = (nc.sbuf_bytes_remaining // 32) * 32
        ctx.enter_context(nc.sbuf_tensor("arena", [P, room // 4 - 8], F32))
        cursor = [(base + 31) // 32 * 32]
        limit = base + room - 32

        def at(name, shape, dt, offset):
            assert offset + 4 * int(np.prod(shape[1:])) <= limit, (name, offset, limit)
            return nc.alloc_sbuf_tensor_at(name, shape, dt, offset=offset)

        def sb(name, shape, dt=F32):
            t = at(name, shape, dt, cursor[0])
            cursor[0] += (4 * int(np.prod(shape[1:])) + 31) // 32 * 32
            return t

        def sem(name):
            return ctx.enter_context(nc.semaphore(name))

        hT = sb("hT", [P, KC, T])
        xn_hi = sb("xn_hi", [P, KC, T], F32R)
        xn_lo = sb("xn_lo", [P, KC, T], F32R)
        stage = sb("stage", [P, 2, UNIT])
        w_hi = sb("w_hi", [P, 2, UNIT], F32R)
        w_lo = sb("w_lo", [P, 2, UNIT], F32R)
        sq_off = cursor[0]
        sqt = sb("sqt", [P, 2, T])
        rst_off = cursor[0]
        rst = sb("rst", [P, 2, T])
        qkn = sb("qkn", [P, 2, T])
        kept = sb("kept", [P, C_TEMP])
        ident_r = sb("ident_r", [P, P], F32R)
        ones_r = sb("ones_r", [P, P], F32R)
        anti_r = sb("anti_r", [P, P], F32R)
        maskA_r = sb("maskA_r", [P, P], F32R)
        maskT_r = sb("maskT_r", [P, P], F32R)
        gains = sb("gains", [P, 44])
        gq8 = sb("gq8", [P, 2])
        bf = sb("bf", [P, 1])
        sinkb = sb("sinkb", [P, HEADS])
        nsink = sb("nsink", [P, HEADS])
        cc = sb("cc", [P, TB, HEADS])
        nm = sb("nm", [P, 2, TB])
        rel = sb("rel", [P, HEADS])
        area = cursor[0]
        KB = 1024

        o_t = at("o_t", [P, KC, T], F32, area + 78 * KB)
        hank = at("hank", [P, HEADS, 2 * WINDOW], F32, area + 78 * KB)
        r_hi = at("r_hi", [P, FH, T], F32R, area)
        r_lo = at("r_lo", [P, FH, T], F32R, area + 32 * KB)
        out_sb = at("out_sb", [P, 2, TB, P], F32, area + 64 * KB)
        x_in = at("x_in", [P, TB, D], F32, area)
        ctemp = at("ctemp", [P, C_ALL - C_TEMP], F32, area + 16 * KB)
        g_in = at("g_in", [44, P], F32, area + 25 * KB)
        ext_sb = at("ext_sb", [HEADS, 2, 384], F32, area + 46 * KB)
        v_all = at("v_all", [P, TB, D], F32, area)
        pT = at("pT", [P, 2, 1280], F32, area + 16 * KB)
        vx = at("vx", [P, TB, 192], F32, area + 27 * KB)
        qk_hi = at("qk_hi", [P, 2, T], F32R, area + 30 * KB)
        qk_lo = at("qk_lo", [P, 2, T], F32R, area + 34 * KB)
        diag = at("diag", [P, 2, T], F32R, area + 38 * KB)
        cm = at("cm", [P, 2, T], F32R, area + 42 * KB)
        ct = at("ct", [P, 4, T], F32, area + 46 * KB)
        wf = at("wf", [P, KC, P], F32, area + 54 * KB)
        wf_hi = at("wf_hi", [P, KC, P], F32R, area + 58 * KB)
        wf_lo = at("wf_lo", [P, KC, P], F32R, area + 62 * KB)
        hk_hi = at("hk_hi", [P, HEADS, 2 * WINDOW], F32R, area)
        hk_lo = at("hk_lo", [P, HEADS, 2 * WINDOW], F32R, area + 16 * KB)
        hka = at("hka", [P, HEADS, 2 * WINDOW], F32R, area + 32 * KB)
        sp_ = at("swa_p", [P, 2, 896], F32, area + 48 * KB)
        svx = at("swa_vx", [P, 2, TB, 192], F32, area + 55 * KB)
        sq_hi = at("swa_q_hi", [P, T], F32R, area + 61 * KB)
        sq_lo = at("swa_q_lo", [P, T], F32R, area + 63 * KB)
        kd_hi = at("kd_hi", [P, 2, T], F32R, area + 65 * KB)
        kd_lo = at("kd_lo", [P, 2, T], F32R, area + 69 * KB)
        sdiag = at("swa_diag", [P, 2, T], F32R, area + 73 * KB)
        psink = [at("psink0", [P, T], F32, sq_off + 2 * KB), at("psink1", [P, T], F32, rst_off + 2 * KB)]

        ident = kept[:, C_IDENT:C_IDENT + P]
        blk = kept[:, C_BLK:C_BLK + P]
        ones_d = kept[:, C_OND:C_OND + P]

        ps = ctx.enter_context(nc.psum_tensor("ps", [P, 8, T], F32))
        ext = nc.dram_tensor("ext", [2, HEADS, 384], F32, kind="Internal").ap()

        x_landed = sem("x_landed")
        consts_landed = sem("consts_landed")
        small_landed = sem("small_landed")
        landed = [sem("landed0"), sem("landed1")]
        w_hi_ready = sem("w_hi_ready")
        w_lo_ready = sem("w_lo_ready")
        w_used = sem("w_used")
        prep = sem("prep")
        gains_t = sem("gains_t")
        ext_ps = sem("ext_ps")
        ext_ready = sem("ext_ready")
        ext_stored = sem("ext_stored")
        hank_landed = sem("hank_landed")
        x_turned = sem("x_turned")
        h_written = sem("h_written")
        sq_ready = sem("sq_ready")
        sum_added = sem("sum_added")
        ln_done = sem("ln_done")
        rstd_ready = sem("rstd_ready")
        xf_ready = sem("xf_ready")
        xn_hi_ready = sem("xn_hi_ready")
        xn_ready = sem("xn_ready")
        v_stored = sem("v_stored")
        wf_zero = sem("wf_zero")
        wf_landed = sem("wf_landed")
        wf_split = sem("wf_split")
        gate_ps = sem("gate_ps")
        gate_step = sem("gate_step")
        gate_dve = sem("gate_dve")
        c_turned = sem("c_turned")
        cc_ready = sem("cc_ready")
        f_sq = sem("f_sq")
        f_sum = sem("f_sum")
        f_ln = sem("f_ln")
        f_rs = sem("f_rs")
        f_qkn = sem("f_qkn")
        f_hi = sem("f_hi")
        f_lo = sem("f_lo")
        f_cm = sem("f_cm")
        f_vx = sem("f_vx")
        f_ones = sem("f_ones")
        f_sa = sem("f_sa")
        f_nm = sem("f_nm")
        f_diag = sem("f_diag")
        f_st = sem("f_st")
        f_p = sem("f_p")
        f_o = sem("f_o")
        f_rec = sem("f_rec")
        f_ot = sem("f_ot")
        s_hank = sem("s_hank")
        s_hank_read = sem("s_hank_read")
        s_k = sem("s_k")
        s_sq = sem("s_sq")
        s_sum = sem("s_sum")
        s_ln = sem("s_ln")
        s_rs = sem("s_rs")
        s_qn = sem("s_qn")
        s_hi = sem("s_hi")
        s_lo = sem("s_lo")
        s_q = sem("s_q")
        s_ones = sem("s_ones")
        s_sa = sem("s_sa")
        s_nm = sem("s_nm")
        s_nms = sem("s_nms")
        s_diag = sem("s_diag")
        s_st = sem("s_st")
        s_p = sem("s_p")
        s_o = sem("s_o")
        s_rec = sem("s_rec")
        s_ot = sem("s_ot")
        relu_done = sem("relu_done")
        sqf_done = sem("sqf_done")
        r_hi_ready = sem("r_hi_ready")
        r_ready = sem("r_ready")
        fin_ready = sem("fin_ready")
        fin_turned = sem("fin_turned")
        out_copied = sem("out_copied")
        out_stored = [sem("out_stored0"), sem("out_stored1")]

        def after(eng, s, count):
            if not (isinstance(count, int) and count <= 0):
                eng.wait_ge(s, count)

        block = ctx.enter_context(nc.Block())

        @block.sync
        def _(sp):
            def slot_free(u):
                after(sp, w_lo_ready, u - 1)

            def load(u, s, src, **shape):
                slot_free(u)
                dst = stage[:, s, :].rearrange("p (k n) -> p k n", **shape)
                sp.dma_start(dst, src).then_inc(landed[s], 16)

            sp.dma_start(kept[:], consts[:, 0:C_TEMP]).then_inc(consts_landed, 16)
            for b in range(TB):
                sp.dma_start(x_in[:, b, :], x[0, b * P:(b + 1) * P, :]).then_inc(x_landed, 16)
            sp.dma_start(ctemp[:], consts[:, C_TEMP:C_ALL]).then_inc(consts_landed, 16)

            w_in = w_in_a[0].rearrange("(k p) n -> p k n", p=P)
            for v in range(4):
                load(U_V + v, (U_V + v) % 2, w_in[:, :, 2 * D + 256 * v:2 * D + 256 * v + 256], k=KC)

            def load_pair(i, s):
                slot_free(U_PAIR + i)
                dst = stage[:, s, :].rearrange("p (t k n) -> p t k n", t=2, k=KC)
                for t in range(2):
                    sp.dma_start(dst[:, t], w_in[:, :, bass.ds(i * P + t * D, P)]).then_inc(landed[s], 16)

            with sp.Fori(0, PAIRS // 2) as i:
                for j in range(2):
                    load_pair(2 * i + j, (U_PAIR + j) % 2)

            def load_out(which, w):
                src = w.rearrange("(k p) n -> p k n", p=P)
                with sp.Fori(0, 2) as i:
                    for j in range(2):
                        u = U_OUT[which] + j
                        load(u + 2 * i, u % 2, src[:, :, bass.ds(i * 512 + 256 * j, 256)], k=KC)

            def load_mlp(d):
                layer, half = d // 2, d % 2
                up = w_up[layer].rearrange("(k p) n -> p k n", p=P)
                with sp.Fori(0, 4) as i:
                    for j in range(2):
                        u = U_UP[d] + j
                        load(u + 2 * i, u % 2, up[:, :, bass.ds(i * 512 + 256 * j + half * (F // 2), 256)], k=KC)
                down = w_down[layer, half * (F // 2):(half + 1) * (F // 2), :].rearrange("(k p) n -> p k n", p=P)
                with sp.Fori(0, 4) as i:
                    for j in range(2):
                        u = U_DOWN[d] + j
                        load(u + 2 * i, u % 2, down[:, :, bass.ds(i * 256 + 128 * j, P)], k=FH)

            def load_hankel(which):
                src = bass.AP(ext.tensor, which * HEADS * 384, [[1, P], [384, HEADS], [1, 2 * WINDOW]])
                sp.dma_start(hank[:], src).then_inc(hank_landed, 16)

            load_out(0, w_out_a[0])
            load_mlp(0)
            sp.wait_ge(xn_ready, KC * (FILL_OUT_A + 1))
            sp.wait_ge(ext_stored, 16)
            load_hankel(0)
            load_mlp(1)
            load(U_KV, U_KV % 2, w_kv.rearrange("(k p) n -> p k n", p=P), k=KC)
            wq = w_q_b[0].rearrange("(k p) n -> p k n", p=P)
            load(U_Q, U_Q % 2, wq[:, :, 0:256], k=KC)
            sp.wait_ge(s_hank_read, 1)
            load_hankel(1)
            for v in range(1, 4):
                load(U_Q + v, (U_Q + v) % 2, wq[:, :, 256 * v:256 * v + 256], k=KC)
            load_out(1, w_out_b[0])
            load_mlp(2)
            load_mlp(3)
            dst = out[0].rearrange("(b p) n -> p b n", p=P)
            for n in range(KC):
                sp.wait_ge(out_copied, n + 1)
                sp.dma_start(dst[:, :, n * P:(n + 1) * P], out_sb[:, n % 2]).then_inc(out_stored[n % 2], 16)
            for s in range(2):
                sp.wait_ge(out_stored[s], 16 * KC // 2)

        @block.gpsimd
        def _(pool):
            nc.gpsimd.memset(wf[:], 0.0).then_inc(wf_zero, 1)

            def low(u, s):
                pool.wait_ge(w_hi_ready, u + 1)
                for q in range(4):
                    c = slice(q * UNIT // 4, (q + 1) * UNIT // 4)
                    ins = nc.gpsimd.tensor_tensor(w_lo[:, s, c], stage[:, s, c], w_hi[:, s, c].bitcast(F32),
                                                  ALU.subtract)
                ins.then_inc(w_lo_ready, 1)

            with pool.Fori(0, N_UNITS // 2) as i:
                low(2 * i, 0)
                low(2 * i + 1, 1)
            low(N_UNITS - 1, 0)

        @block.scalar
        def _(act):
            def split(count, u, s):
                act.wait_ge(landed[s], 16 * count)
                after(act, w_used, u - 1)
                nc.scalar.activation(w_hi[:, s, :], stage[:, s, :], ACT.Copy).then_inc(w_hi_ready, 1)

            act.dma_start(g_in[0:8, :], g_attn[0].rearrange("(k p) -> k p", p=P)).then_inc(small_landed, 16)
            act.dma_start(g_in[8:16, :], g_mlp[0].rearrange("(k p) -> k p", p=P)).then_inc(small_landed, 16)
            act.dma_start(g_in[16:24, :], g_kv.rearrange("(k p) -> k p", p=P)).then_inc(small_landed, 16)
            act.dma_start(g_in[24:32, :], g_attn[1].rearrange("(k p) -> k p", p=P)).then_inc(small_landed, 16)
            act.dma_start(g_in[32:40, :], g_mlp[1].rearrange("(k p) -> k p", p=P)).then_inc(small_landed, 16)
            for n, g in enumerate((gq_a[0], gk_a[0], gq_b[0], gk_b)):
                for half in range(2):
                    act.dma_start(g_in[40 + n:41 + n, 64 * half:64 * half + 64], g[None, :]).then_inc(small_landed, 16)
            act.dma_start(rel[0:N_BUCKETS, :], rel_bias).then_inc(small_landed, 16)
            act.dma_start(sinkb[:], sinks[0].partition_broadcast(P)).then_inc(small_landed, 16)
            act.wait_ge(wf_zero, 2)
            act.dma_start(bf[0:HEADS, :], b_f[0].rearrange("(h o) -> h o", o=1)).then_inc(wf_landed, 16)
            act.dma_start(wf[:, :, 0:HEADS], w_in_a[0].rearrange("(k p) n -> p k n", p=P)[:, :, 3 * D:3 * D + HEADS]
                          ).then_inc(wf_landed, 16)

            split(1, 0, 0)
            split(1, 1, 1)

            def norm_stats(q, h_base):
                for c in range(KC):
                    act.wait_ge(h_written, h_base + c + 1)
                    after(act, sum_added, KC * q + c - 1)
                    nc.scalar.activation(sqt[:, c % 2, :], hT[:, c, :], ACT.Square).then_inc(sq_ready, 1)
                act.wait_ge(sum_added, KC * (q + 1))
                nc.scalar.activation(rst[:, 0, :], ps[:, 7, :], ACT.Ln, bias=EPS).then_inc(ln_done, 1)
                act.wait_ge(ln_done, q + 1)
                nc.scalar.activation(rst[:, 0, :], rst[:, 0, :], ACT.Exp, scale=-0.5).then_inc(rstd_ready, 1)

            def norm_hi(fill, u_first):
                after(act, w_used, u_first)
                for c in range(KC):
                    act.wait_ge(xf_ready, KC * XF_ORDER[fill] + c + 1)
                    nc.scalar.activation(xn_hi[:, c, :], qkn[:, c % 2, :], ACT.Copy).then_inc(xn_hi_ready, 1)

            norm_stats(0, 0)
            act.wait_ge(ext_ready, 1)
            act.dma_start(ext.rearrange("w h n -> h w n"), ext_sb[:]).then_inc(ext_stored, 16)
            norm_hi(FILL_ATTN0, 0)
            for v in range(4):
                u = U_V + v + 2
                split(u // 2 + 1 if u < U_PAIR else 2 + 2, u, u % 2)

            act.wait_ge(gate_ps, 1)
            act.wait_ge(ext_stored, 16)
            nc.scalar.activation(ct[:, 0, :], ps[:, 6, :], ACT.Identity, bias=bf[:, 0:1]).then_inc(gate_step, 1)
            act.wait_ge(gate_step, 1)
            nc.scalar.activation(ct[:, 1, :], ct[:, 0, :], ACT.Abs).then_inc(gate_step, 1)
            act.wait_ge(gate_step, 2)
            nc.scalar.activation(ct[:, 1, :], ct[:, 1, :], ACT.Exp, scale=-1.0).then_inc(gate_step, 1)
            act.wait_ge(gate_step, 3)
            nc.scalar.activation(ct[:, 1, :], ct[:, 1, :], ACT.Ln, bias=1.0).then_inc(gate_step, 1)

            def fox_square(i):
                act.wait_ge(w_used, U_PAIR + i + 1)
                nc.scalar.activation(sqt[:], ps[:, 0:2, :], ACT.Square).then_inc(f_sq, 1)

            def fox_rstd(i):
                act.wait_ge(f_sum, i + 1)
                after(act, f_qkn, i)
                nc.scalar.activation(rst[:], ps[:, 2:4, :], ACT.Ln, bias=EPS).then_inc(f_ln, 1)
                act.wait_ge(f_ln, i + 1)
                nc.scalar.activation(rst[:], rst[:], ACT.Exp, scale=-0.5).then_inc(f_rs, 1)

            def fox_hi(i):
                act.wait_ge(f_qkn, i + 1)
                after(act, f_st, 2 * i)
                nc.scalar.activation(qk_hi[:], qkn[:], ACT.Copy).then_inc(f_hi, 1)

            def fox_exp(j):
                for e in range(2):
                    act.wait_ge(f_st, 2 * j + e + 1)
                    after(act, f_o, 2 * j - 1 + e)
                    b = 2 + 3 * e
                    tiles = ((0, b, 0, 512, 0), (1, b + 1, 0, 384, 512), (3, b + 1, 384, 128, 896),
                             (2, b + 2, 0, 256, 1024))
                    for kb, bank, c0, n, dst in tiles:
                        ins = nc.scalar.activation(pT[:, e, dst:dst + n], ps[:, bank, c0:c0 + n], ACT.Exp,
                                                   bias=cc[:, kb, bass.ds(2 * j + e, 1)])
                    ins.then_inc(f_p, 1)

            act.wait_ge(cc_ready, 1)
            fox_square(0)
            fox_rstd(0)
            fox_hi(0)
            split(2 + 4, U_PAIR + 2, 0)

            def fox_step(i, landed_count, s):
                fox_square(i)
                fox_exp(i - 1)
                fox_rstd(i)
                fox_hi(i)
                split(landed_count, U_PAIR + i + 2, s)

            fox_step(1, 2 + 4, 1)
            with act.Fori(1, 3) as t:
                fox_step(2 * t, 2 + 4 + 2 * t, 0)
                fox_step(2 * t + 1, 2 + 4 + 2 * t, 1)
            fox_step(6, 2 + 8 + 1, 0)
            fox_step(7, 2 + 8 + 1, 1)
            fox_exp(7)

            def out_hi(fill, ready, u_first):
                act.wait_ge(w_used, u_first)
                for c in range(KC):
                    act.wait_ge(ready, 2 * c + 2)
                    nc.scalar.activation(xn_hi[:, c, :], o_t[:, c, :], ACT.Copy).then_inc(xn_hi_ready, 1)

            SLOT = 5

            def split_units(u0, n):
                with act.Fori(0, n // 2) as t:
                    for j in range(2):
                        u = u0 + j
                        split(u // 2 + SLOT + t, u + 2 * t, u % 2)

            out_hi(FILL_OUT_A, f_ot, U_OUT[0])
            split_units(U_OUT[0] + 2, 4)

            def mlp_up(d):
                def unit(i, s, count):
                    act.wait_ge(w_used, U_UP[d] + i + 1)
                    after(act, sqf_done, 8 * d + i)
                    after(act, r_hi_ready, 8 * d + i)
                    b = 2 * s
                    nc.scalar.activation(sqt[:], ps[:, b:b + 2, :], ACT.Relu).then_inc(relu_done, 1)
                    act.wait_ge(relu_done, 8 * d + i + 1)
                    nc.scalar.activation(r_hi[:, bass.ds(2 * i, 2), :], sqt[:], ACT.Square).then_inc(r_hi_ready, 1)
                    split(count, U_UP[d] + i + 2, (U_UP[d] + s) % 2)

                c = [(U_UP[d] + j + 2) // 2 + SLOT for j in range(2)]
                unit(0, 0, c[0])
                unit(1, 1, c[1])
                with act.Fori(1, 4) as t:
                    for j in range(2):
                        unit(2 * t + j, j, c[j] + t)

            norm_stats(1, 8)
            norm_hi(FILL_MLP0, U_UP[0])
            for d in range(2):
                mlp_up(d)
                split_units(U_DOWN[d] + 2, 8)

            norm_stats(2, 24)
            norm_hi(FILL_KV, U_KV)
            act.wait_ge(s_k, 1)
            nc.scalar.activation(sqt[:, 0, :], ps[:, 0, :], ACT.Square).then_inc(s_sq, 1)
            split((U_Q + 1) // 2 + SLOT, U_Q + 1, (U_Q + 1) % 2)
            norm_hi(FILL_Q, U_Q)
            act.wait_ge(s_sum, 1)
            nc.scalar.activation(rst[:, 1, :], ps[:, 1, :], ACT.Ln, bias=EPS).then_inc(s_ln, 1)
            act.wait_ge(s_ln, 1)
            nc.scalar.activation(rst[:, 1, :], rst[:, 1, :], ACT.Exp, scale=-0.5).then_inc(s_rs, 1)
            act.wait_ge(s_qn, 1)
            for g in range(2):
                for half in range(2):
                    ins = nc.scalar.activation(kd_hi[64 * half:64 * half + 64, g, :], qkn[64 * g:64 * g + 64, 1, :],
                                               ACT.Copy)
            ins.then_inc(s_hi, 1)

            def swa_square(i):
                if i % 2 == 0:
                    act.wait_ge(s_q, i // 2 + 1)
                else:
                    act.wait_ge(w_used, U_Q + i // 2 + 1)
                nc.scalar.activation(sqt[:, 0, :], ps[:, 0, :], ACT.Square).then_inc(s_sq, 1)

            def swa_rstd(i):
                act.wait_ge(s_sum, i + 2)
                act.wait_ge(s_qn, i + 1)
                nc.scalar.activation(rst[:, 0, :], ps[:, 1, :], ACT.Ln, bias=EPS).then_inc(s_ln, 1)
                act.wait_ge(s_ln, i + 2)
                nc.scalar.activation(rst[:, 0, :], rst[:, 0, :], ACT.Exp, scale=-0.5).then_inc(s_rs, 1)

            def swa_hi(i):
                act.wait_ge(s_qn, i + 2)
                after(act, s_st, 2 * i)
                nc.scalar.activation(sq_hi[:], qkn[:, 0, :], ACT.Copy).then_inc(s_hi, 1)

            def swa_exp(j):
                for e in range(2):
                    act.wait_ge(s_st, 2 * j + e + 1)
                    after(act, s_o, 2 * j - 1 + e)
                    b = 2 + 2 * e
                    nc.scalar.activation(psink[e][:], ps[:, 6 + e, :], ACT.Exp,
                                         bias=sinkb[:, bass.ds(2 * j + e, 1)])
                    nc.scalar.activation(sp_[:, e, 0:512], ps[:, b, :], ACT.Exp)
                    nc.scalar.activation(sp_[:, e, 512:896], ps[:, b + 1, 0:384], ACT.Exp).then_inc(s_p, 1)

            def swa_step(i, split_unit, count, s):
                swa_square(i)
                swa_exp(i - 1)
                swa_rstd(i)
                swa_hi(i)
                if split_unit is not None:
                    split(count, split_unit, s)

            swa_square(0)
            swa_rstd(0)
            swa_hi(0)
            swa_step(1, U_Q + 2, (U_Q + 2) // 2 + SLOT, (U_Q + 2) % 2)
            for v in range(1, 4):
                swa_step(2 * v, None, None, None)
                u = U_Q + v + 2
                swa_step(2 * v + 1, u, u // 2 + SLOT, u % 2)
            swa_exp(7)
            out_hi(FILL_OUT_B, s_ot, U_OUT[1])
            split_units(U_OUT[1] + 2, 4)

            norm_stats(3, 32)
            norm_hi(FILL_MLP1, U_UP[2])
            mlp_up(2)
            split_units(U_DOWN[2] + 2, 8)
            mlp_up(3)
            for n in range(KC):
                if n + 2 < KC:
                    u = U_DOWN[3] + n + 2
                    split(u // 2 + SLOT, u, u % 2)
                if n >= 1:
                    turn_out = n - 1
                    act.wait_ge(fin_turned, turn_out + 1)
                    after(act, out_stored[turn_out % 2], 16 * (turn_out // 2))
                    nc.scalar.activation(out_sb[:, turn_out % 2], ps[:, 6 + turn_out % 2, :].rearrange(
                        "p (b n) -> p b n", b=TB), ACT.Copy).then_inc(out_copied, 1)
            act.wait_ge(fin_turned, KC)
            act.wait_ge(out_stored[1], 16 * (KC // 2 - 1))
            nc.scalar.activation(out_sb[:, 1], ps[:, 7, :].rearrange("p (b n) -> p b n", b=TB),
                                 ACT.Copy).then_inc(out_copied, 1)

        @block.vector
        def _(dve):
            V = nc.vector

            nc.vector.memset(bf[:], 0.0).then_inc(wf_zero, 1)
            dve.wait_ge(consts_landed, 32)
            for dst, col in ((ident_r, None), (anti_r, C_ANTI), (ones_r, C_ONES), (maskA_r, C_MASKA), (maskT_r, C_MASKT)):
                src = ident if col is None else ctemp[:, col - C_TEMP:col - C_TEMP + P]
                ins = V.tensor_copy(dst[:], src)
            ins.then_inc(prep, 1)
            dve.wait_ge(gains_t, 1)
            V.tensor_copy(gains[:], ps[:, 7, 0:44]).then_inc(prep, 1)
            dve.wait_ge(prep, 2)
            V.tensor_scalar(gq8[:, 0:1], gains[:, 40:41], float(HD) ** -0.5, None, ALU.mult)
            V.tensor_scalar(gq8[:, 1:2], gains[:, 42:43], float(HD) ** -0.5, None, ALU.mult)
            V.tensor_scalar(nsink[:], sinkb[:], -1.0, None, ALU.mult).then_inc(prep, 1)
            for c in range(KC):
                dve.wait_ge(x_turned, c + 1)
                V.tensor_copy(hT[:, c, :], ps[:, c % 4, :]).then_inc(h_written, 1)
            dve.wait_ge(ext_ps, 1)
            for w in range(2):
                ins = V.tensor_tensor(ext_sb[:, w, :], ps[0:HEADS, 4 + w, 0:384],
                                      ctemp[0:HEADS, C_NEG - C_TEMP + 384 * w:C_NEG - C_TEMP + 384 * w + 384], ALU.add)
            ins.then_inc(ext_ready, 1)

            def norm_apply(fill, q, u_first):
                g = 8 * GAIN[fill]
                dve.wait_ge(rstd_ready, q + 1)
                after(dve, w_used, u_first)

                def full(c):
                    if c >= 2:
                        dve.wait_ge(xn_ready, KC * fill + c - 1)
                    V.scalar_tensor_tensor(out=qkn[:, c % 2, :], in0=hT[:, c, :], scalar=gains[:, g + c:g + c + 1],
                                           in1=rst[:, 0, :], op0=ALU.mult, op1=ALU.mult).then_inc(xf_ready, 1)

                full(0)
                full(1)
                for c in range(KC):
                    dve.wait_ge(xf_ready, KC * XF_ORDER[fill] + c + 1)
                    dve.wait_ge(xn_hi_ready, KC * fill + c + 1)
                    V.tensor_tensor(xn_lo[:, c, :], qkn[:, c % 2, :], xn_hi[:, c, :].bitcast(F32),
                                    ALU.subtract).then_inc(xn_ready, 1)
                    if c + 2 < KC:
                        full(c + 2)

            def out_lo(fill):
                for c in range(KC):
                    dve.wait_ge(xn_hi_ready, KC * fill + c + 1)
                    V.tensor_tensor(xn_lo[:, c, :], o_t[:, c, :], xn_hi[:, c, :].bitcast(F32),
                                    ALU.subtract).then_inc(xn_ready, 1)

            norm_apply(FILL_ATTN0, 0, 0)
            dve.wait_ge(wf_landed, 32)
            V.tensor_copy(wf_hi[:], wf[:]).then_inc(wf_split, 1)
            dve.wait_ge(wf_split, 1)
            V.tensor_tensor(wf_lo[:], wf[:], wf_hi[:].bitcast(F32), ALU.subtract).then_inc(wf_split, 1)
            V.memset(vx[:, :, HD:2 * HD], 1.0).then_inc(f_ones, 1)
            for v in range(4):
                dve.wait_ge(w_used, U_V + v + 1)
                b = 4 * (v % 2)
                V.tensor_copy(v_all[:, :, 256 * v:256 * v + 256], ps[:, b:b + 4, 0:256]).then_inc(v_stored, 1)
            dve.wait_ge(ext_stored, 16)
            V.memset(ct[:, 3, :], 1.0).then_inc(gate_dve, 1)
            dve.wait_ge(gate_step, 4)
            V.scalar_tensor_tensor(out=ct[:, 1, :], in0=ct[:, 0, :], scalar=0.0, in1=ct[:, 1, :],
                                   op0=ALU.min, op1=ALU.subtract).then_inc(gate_dve, 1)
            dve.wait_ge(gate_dve, 2)
            V.tensor_tensor_scan(out=ct[:, 2, :], data0=ct[:, 3, :], data1=ct[:, 1, :], initial=0.0,
                                 op0=ALU.mult, op1=ALU.subtract).then_inc(gate_dve, 1)
            dve.wait_ge(c_turned, 1)
            V.tensor_copy(cc[:], ps[:, 7, 0:TB * HEADS].rearrange("p (b h) -> p b h", b=TB)).then_inc(cc_ready, 1)

            def fox_cm(i):
                after(dve, f_sa, 2 * i)
                for e in range(2):
                    ins = V.tensor_scalar(cm[:, e, :], ct[:, 2, :], kept[:, bass.ds(2 * i + e, 1)], None, ALU.mult)
                ins.then_inc(f_cm, 1)

            def fox_vx(i):
                after(dve, f_o, 2 * i)
                for e in range(2):
                    ins = V.tensor_copy(vx[:, :, 2 * HD * e:2 * HD * e + HD], v_all[:, :, bass.ds(i * P + HD * e, HD)])
                ins.then_inc(f_vx, 1)

            def fox_norm(i):
                dve.wait_ge(f_rs, i + 1)
                V.scalar_tensor_tensor(out=qkn[:, 0, :], in0=ps[:, 0, :], scalar=gq8[:, 0:1], in1=rst[:, 0, :],
                                       op0=ALU.mult, op1=ALU.mult)
                V.scalar_tensor_tensor(out=qkn[:, 1, :], in0=ps[:, 1, :], scalar=gains[:, 41:42], in1=rst[:, 1, :],
                                       op0=ALU.mult, op1=ALU.mult).then_inc(f_qkn, 1)
                dve.wait_ge(f_hi, i + 1)
                after(dve, f_st, 2 * i)
                V.tensor_tensor(qk_lo[:], qkn[:], qk_hi[:].bitcast(F32), ALU.subtract).then_inc(f_lo, 1)

            def fox_max(j):
                for e in range(2):
                    dve.wait_ge(f_sa, 2 * j + e + 1)
                    after(dve, f_diag, 2 * j - 1 + e)
                    b = 2 + 3 * e
                    for qb, bank, c0, n in ((3, b, 0, 512), (2, b + 1, 0, 384), (0, b + 1, 384, 128), (1, b + 2, 0, 256)):
                        ins = V.tensor_reduce(nm[:, e, qb:qb + 1], ps[:, bank, c0:c0 + n], AX_X, ALU.max, negate=True)
                    ins.then_inc(f_nm, 1)
                    dve.wait_ge(f_nm, 2 * j + e + 1)
                    after(dve, f_st, 2 * j - 1 + e)
                    V.tensor_tensor(diag[:, e, :].rearrange("p (b n) -> p b n", b=TB),
                                    ident[:, None, :].to_broadcast([P, TB, P]),
                                    nm[:, e, :, None].to_broadcast([P, TB, P]), ALU.mult).then_inc(f_diag, 1)

            def fox_out(j):
                for e in range(2):
                    dve.wait_ge(f_o, 2 * j + e + 1)
                    own, other = slice(64 * e, 64 * e + 64), slice(64 - 64 * e, 128 - 64 * e)
                    V.reciprocal(ct[own, 3, :], ps[other, 4 + e, :]).then_inc(f_rec, 1)
                    dve.wait_ge(f_rec, 2 * j + e + 1)
                    dst = o_t[own, bass.ds(j, 1), :].rearrange("p a n -> p (a n)")
                    V.tensor_tensor(dst, ps[own, 4 + e, :], ct[own, 3, :], ALU.mult).then_inc(f_ot, 1)

            def fox_step(i):
                fox_max(i - 1)
                fox_norm(i)
                fox_cm(i)
                fox_out(i - 1)
                fox_vx(i)

            dve.wait_ge(gate_dve, 3)
            fox_cm(0)
            fox_vx(0)
            fox_norm(0)
            fox_step(1)
            with dve.Fori(1, 4) as t:
                fox_step(2 * t)
                fox_step(2 * t + 1)
            fox_max(7)
            fox_out(7)
            out_lo(FILL_OUT_A)

            def add_chunk(bank, c):
                dst = hT[:, bass.ds(c, 1), :].rearrange("p a n -> p (a n)")
                V.tensor_tensor(dst, dst, ps[:, bank, :], ALU.add).then_inc(h_written, 1)

            def add_out(which):
                with dve.Fori(0, 2) as t:
                    for j in range(2):
                        dve.wait_ge(w_used, U_OUT[which] + 2 * t + j + 1)
                        for n in range(2):
                            add_chunk(2 * j + n, 4 * t + 2 * j + n)

            def mlp_up(d):
                with dve.Fori(0, 4) as t:
                    for j in range(2):
                        i = 2 * t + j
                        dve.wait_ge(relu_done, 8 * d + i + 1)
                        V.tensor_tensor(qkn[:], sqt[:], sqt[:], ALU.mult).then_inc(sqf_done, 1)
                        dve.wait_ge(sqf_done, 8 * d + i + 1)
                        dve.wait_ge(r_hi_ready, 8 * d + i + 1)
                        V.tensor_tensor(r_lo[:, bass.ds(2 * i, 2), :], qkn[:],
                                        r_hi[:, bass.ds(2 * i, 2), :].bitcast(F32), ALU.subtract).then_inc(r_ready, 1)
                        dve.wait_ge(r_ready, 8 * d + i + 1)

            def mlp_down(d):
                with dve.Fori(0, 4) as t:
                    for j in range(2):
                        dve.wait_ge(w_used, U_DOWN[d] + 2 * t + j + 1)
                        add_chunk(4 + j, 2 * t + j)

            add_out(0)
            norm_apply(FILL_MLP0, 1, U_UP[0])
            for d in range(2):
                mlp_up(d)
                mlp_down(d)

            norm_apply(FILL_KV, 2, U_KV)
            dve.wait_ge(hank_landed, 16)
            V.tensor_copy(hk_hi[:], hank[:]).then_inc(s_hank, 1)
            dve.wait_ge(s_hank, 1)
            V.tensor_tensor(hk_lo[:], hank[:], hk_hi[:].bitcast(F32), ALU.subtract).then_inc(s_hank_read, 1)
            norm_apply(FILL_Q, 2, U_Q)
            V.memset(svx[:, :, :, HD:2 * HD], 1.0)
            dve.wait_ge(w_used, U_KV + 1)
            for g in range(2):
                for half in range(2):
                    ins = V.tensor_copy(svx[:, g, :, 2 * HD * half:2 * HD * half + HD],
                                        ps[:, 2, :].rearrange("p (b n) -> p b n", b=TB)[:, :, HD * g:HD * g + HD])
            ins.then_inc(s_ones, 1)
            dve.wait_ge(s_rs, 1)
            dve.wait_ge(xn_ready, KC * (FILL_Q + 1))
            V.scalar_tensor_tensor(out=qkn[:, 1, :], in0=ps[:, 0, :], scalar=gains[:, 43:44], in1=rst[:, 1, :],
                                   op0=ALU.mult, op1=ALU.mult).then_inc(s_qn, 1)
            dve.wait_ge(s_hi, 1)
            dve.wait_ge(s_qn, 1)
            for g in range(2):
                for half in range(2):
                    V.tensor_tensor(kd_lo[64 * half:64 * half + 64, g, :], qkn[64 * g:64 * g + 64, 1, :],
                                    kd_hi[64 * g:64 * g + 64, g, :].bitcast(F32), ALU.subtract)
            dve.wait_ge(hank_landed, 32)
            V.tensor_copy(hka[:], hank[:]).then_inc(s_lo, 1)

            def swa_norm(i):
                dve.wait_ge(s_rs, i + 2)
                dve.wait_ge(s_lo, i + 1)
                V.scalar_tensor_tensor(out=qkn[:, 0, :], in0=ps[:, 0, :], scalar=gq8[:, 1:2], in1=rst[:, 0, :],
                                       op0=ALU.mult, op1=ALU.mult).then_inc(s_qn, 1)
                dve.wait_ge(s_hi, i + 2)
                after(dve, s_st, 2 * i)
                V.tensor_tensor(sq_lo[:], qkn[:, 0, :], sq_hi[:].bitcast(F32), ALU.subtract).then_inc(s_lo, 1)

            def swa_max(j):
                for e in range(2):
                    dve.wait_ge(s_sa, 2 * j + e + 1)
                    after(dve, s_diag, 2 * j - 1 + e)
                    b = 2 + 2 * e
                    V.tensor_reduce(nm[:, e, 1:3], ps[:, b, :].rearrange("p (b n) -> p b n", b=2), AX_X, ALU.max,
                                    negate=True)
                    V.tensor_reduce(nm[:, e, 3:4], ps[:, b + 1, 0:256], AX_X, ALU.max, negate=True)
                    V.tensor_reduce(nm[:, e, 0:1], ps[:, b + 1, 256:384], AX_X, ALU.max, negate=True).then_inc(s_nm, 1)
                    dve.wait_ge(s_nm, 2 * j + e + 1)
                    V.tensor_scalar(nm[:, e, :], nm[:, e, :], nsink[:, bass.ds(2 * j + e, 1)], None,
                                    ALU.min).then_inc(s_nms, 1)
                    dve.wait_ge(s_nms, 2 * j + e + 1)
                    after(dve, s_st, 2 * j - 1 + e)
                    V.tensor_tensor(sdiag[:, e, :].rearrange("p (b n) -> p b n", b=TB),
                                    ident[:, None, :].to_broadcast([P, TB, P]),
                                    nm[:, e, :, None].to_broadcast([P, TB, P]), ALU.mult).then_inc(s_diag, 1)

            def swa_out(j):
                for e in range(2):
                    dve.wait_ge(s_o, 2 * j + e + 1)
                    own, other = slice(64 * e, 64 * e + 64), slice(64 - 64 * e, 128 - 64 * e)
                    V.reciprocal(qkn[own, 1, :], ps[other, 6 + e, :]).then_inc(s_rec, 1)
                    dve.wait_ge(s_rec, 2 * j + e + 1)
                    V.tensor_tensor(o_t[own, j, :], ps[own, 6 + e, :], qkn[own, 1, :], ALU.mult).then_inc(s_ot, 1)

            swa_norm(0)
            for i in range(1, PAIRS):
                swa_max(i - 1)
                swa_norm(i)
                swa_out(i - 1)
            swa_max(7)
            swa_out(7)
            out_lo(FILL_OUT_B)
            add_out(1)
            norm_apply(FILL_MLP1, 3, U_UP[2])
            mlp_up(2)
            mlp_down(2)
            mlp_up(3)
            for n in range(KC):
                dve.wait_ge(w_used, U_DOWN[3] + n + 1)
                after(dve, fin_turned, n - 1)
                V.tensor_tensor(rst[:, n % 2, :], hT[:, n, :], ps[:, 4 + n % 2, :], ALU.add).then_inc(fin_ready, 1)

        @block.tensor
        def _(pe):
            mm = nc.tensor.matmul

            def three(out_, s_hi, s_lo, m_hi, m_lo, start, stop):
                mm(out_, s_hi, m_hi, start=start, stop=False)
                mm(out_, s_hi, m_lo, start=False, stop=False)
                return mm(out_, s_lo, m_hi, start=False, stop=stop)

            pe.wait_ge(consts_landed, 32)
            pe.wait_ge(small_landed, 16 * 15)
            nc.tensor.transpose(ps[:, 7, 0:44], g_in[:], ident[0:44, 0:44]).then_inc(gains_t, 1)
            for w in range(2):
                ins = mm(ps[0:HEADS, 4 + w, 0:384], rel[0:N_BUCKETS, :],
                         ctemp[0:N_BUCKETS, C_HOT - C_TEMP + 384 * w:C_HOT - C_TEMP + 384 * w + 384],
                         start=True, stop=True)
            ins.then_inc(ext_ps, 1)
            pe.wait_ge(x_landed, 16 * TB)
            for c in range(KC):
                after(pe, h_written, c - 3)
                for b in range(TB):
                    ins = nc.tensor.transpose(ps[:, c % 4, b * P:(b + 1) * P], x_in[:, b, c * P:(c + 1) * P], ident)
                ins.then_inc(x_turned, 1)

            def norm_sum(q):
                if q == 0:
                    pe.wait_ge(prep, 2)
                for c in range(KC):
                    pe.wait_ge(sq_ready, KC * q + c + 1)
                    mm(ps[:, 7, :], ones_d, sqt[:, c % 2, :], start=(c == 0), stop=(c == KC - 1)).then_inc(sum_added, 1)

            norm_sum(0)

            pe.wait_ge(h_written, KC)
            pe.wait_ge(ext_ready, 1)
            for v in range(4):
                u = U_V + v
                s = u % 2
                pe.wait_ge(w_lo_ready, u + 1)
                after(pe, v_stored, v - 1)
                if v == 1:
                    pe.wait_ge(rstd_ready, 1)
                wh = w_hi[:, s, :].rearrange("p (k n) -> p k n", k=KC)
                wl = w_lo[:, s, :].rearrange("p (k n) -> p k n", k=KC)
                for k in range(KC):
                    if v == 0:
                        pe.wait_ge(xn_ready, k + 1)
                    for b in range(TB):
                        o = ps[:, 4 * (v % 2) + b, 0:256]
                        xs = slice(b * P, (b + 1) * P)
                        ins = three(o, xn_hi[:, k, xs], xn_lo[:, k, xs], wh[:, k, :], wl[:, k, :], k == 0, k == KC - 1)
                ins.then_inc(w_used, 1)

            def chunk(bank, wh, wl, k_of, m_hi, m_lo, kc):
                for k in range(kc):
                    ins = three(ps[:, bank, :], k_of(wh, k), k_of(wl, k), m_hi[:, k, :], m_lo[:, k, :], k == 0, k == kc - 1)
                return ins

            pe.wait_ge(v_stored, 4)
            pe.wait_ge(wf_split, 2)
            chunk(6, wf_hi, wf_lo, lambda w, k: w[:, k, :], xn_hi, xn_lo, KC).then_inc(gate_ps, 1)

            def proj_pair(i, s, t):
                if t == 0:
                    pe.wait_ge(w_lo_ready, U_PAIR + i + 1)
                    after(pe, f_qkn, i)
                wh = w_hi[:, s, :].rearrange("p (t k n) -> p t k n", t=2, k=KC)
                wl = w_lo[:, s, :].rearrange("p (t k n) -> p t k n", t=2, k=KC)
                return chunk(t, wh[:, t], wl[:, t], lambda w, k: w[:, k, :], xn_hi, xn_lo, KC)

            def fox_sum(i):
                pe.wait_ge(f_sq, i + 1)
                for t in range(2):
                    ins = mm(ps[:, 2 + t, :], blk, sqt[:, t, :], start=True, stop=True)
                ins.then_inc(f_sum, 1)

            def fox_max_scores(j):
                pe.wait_ge(f_hi, j + 1)
                pe.wait_ge(f_cm, j + 1)
                for e in range(2):
                    after(pe, f_ot, 2 * j - 1 + e)
                    b = 2 + 3 * e
                    h = slice(64 * e, 64 * e + 64)
                    for qb, bank, c0 in ((3, b, 0), (2, b + 1, 0), (0, b + 1, 384), (1, b + 2, 0)):
                        n = (qb + 1) * P
                        o = ps[:, bank, c0:c0 + n]
                        mm(o, qk_hi[h, 0, qb * P:(qb + 1) * P], qk_hi[h, 1, 0:n], start=True, stop=False)
                        mm(o, ones_r[:], cm[:, e, 0:n], start=False, stop=False)
                        ins = mm(ps[:, bank, c0 + qb * P:c0 + n], ident_r[:], maskA_r[:], start=False, stop=True)
                    ins.then_inc(f_sa, 1)

            def fox_scores(j):
                pe.wait_ge(f_lo, j + 1)
                for e in range(2):
                    pe.wait_ge(f_diag, 2 * j + e + 1)
                    b = 2 + 3 * e
                    h = slice(64 * e, 64 * e + 64)
                    for kb, bank, c0 in ((0, b, 0), (1, b + 1, 0), (3, b + 1, 384), (2, b + 2, 0)):
                        n = (TB - kb) * P
                        o = ps[:, bank, c0:c0 + n]
                        ks, qs = slice(kb * P, (kb + 1) * P), slice(kb * P, T)
                        mm(o, qk_hi[h, 1, ks], qk_hi[h, 0, qs], start=True, stop=False)
                        mm(o, qk_hi[h, 1, ks], qk_lo[h, 0, qs], start=False, stop=False)
                        mm(o, qk_lo[h, 1, ks], qk_hi[h, 0, qs], start=False, stop=False)
                        mm(o, ones_r[:], diag[:, e, qs], start=False, stop=False)
                        ins = mm(ps[:, bank, c0:c0 + P], ident_r[:], maskT_r[:], start=False, stop=True)
                    ins.then_inc(f_st, 1)

            def fox_pv(j):
                pe.wait_ge(f_vx, j + 1)
                for e in range(2):
                    pe.wait_ge(f_p, 2 * j + e + 1)
                    for kb, src in ((0, 0), (1, 512), (2, 1024), (3, 896)):
                        n = (TB - kb) * P
                        ins = mm(ps[:, 4 + e, kb * P:T], vx[:, kb, HD * e:HD * e + P], pT[:, e, src:src + n],
                                 start=(kb == 0), stop=(kb == TB - 1))
                    ins.then_inc(f_o, 1)

            pe.wait_ge(f_ones, 1)
            proj_pair(0, 0, 0)
            pe.wait_ge(gate_dve, 3)
            for b in range(TB):
                ins = nc.tensor.transpose(ps[:, 7, b * HEADS:(b + 1) * HEADS], ct[0:HEADS, 2, b * P:(b + 1) * P],
                                          ident[0:HEADS, 0:HEADS])
            ins.then_inc(c_turned, 1)
            proj_pair(0, 0, 1).then_inc(w_used, 1)
            fox_sum(0)

            def fox_step(i, s):
                proj_pair(i, s, 0)
                fox_max_scores(i - 1)
                proj_pair(i, s, 1).then_inc(w_used, 1)
                fox_scores(i - 1)
                pe.wait_ge(f_p, 2 * i - 1)
                fox_sum(i)
                fox_pv(i - 1)

            pe.wait_ge(cc_ready, 1)
            fox_step(1, 1)
            with pe.Fori(1, 4) as t:
                fox_step(2 * t, 0)
                fox_step(2 * t + 1, 1)
            fox_max_scores(7)
            fox_scores(7)
            fox_pv(7)

            def unit_d(u, s, banks, fill=None, k_waits=False):
                pe.wait_ge(w_lo_ready, u + 1)
                wh = w_hi[:, s, :].rearrange("p (k n) -> p k n", k=KC)
                wl = w_lo[:, s, :].rearrange("p (k n) -> p k n", k=KC)
                for k in range(KC):
                    if k_waits:
                        pe.wait_ge(xn_ready, KC * fill + k + 1)
                    for n in range(2):
                        ins = three(ps[:, banks + n, :], wh[:, k, n * P:(n + 1) * P], wl[:, k, n * P:(n + 1) * P],
                                    xn_hi[:, k, :], xn_lo[:, k, :], k == 0, k == KC - 1)
                ins.then_inc(w_used, 1)

            def proj_out(which, fill):
                h_base = [8, 32][which]
                u = U_OUT[which]
                unit_d(u, u % 2, 0, fill, True)
                unit_d(u + 1, (u + 1) % 2, 2)
                for j in range(2, 4):
                    pe.wait_ge(h_written, h_base + 2 * (j - 1))
                    unit_d(u + j, (u + j) % 2, 2 * (j % 2))

            def mlp_up(d, fill, k_waits):
                u = U_UP[d]
                unit_d(u, u % 2, 0, fill, k_waits)
                unit_d(u + 1, (u + 1) % 2, 2)
                with pe.Fori(1, 4) as t:
                    for j in range(2):
                        pe.wait_ge(relu_done, 8 * d + 2 * t + j - 1)
                        unit_d(u + j + 2 * t, (u + j) % 2, 2 * j)

            def down_unit(u, s, bank, d=None):
                pe.wait_ge(w_lo_ready, u + 1)
                wh = w_hi[:, s, :].rearrange("p (k n) -> p k n", k=FH)
                wl = w_lo[:, s, :].rearrange("p (k n) -> p k n", k=FH)
                for k in range(FH):
                    if d is not None and k % 2 == 0:
                        pe.wait_ge(r_ready, 8 * d + k // 2 + 1)
                    ins = three(ps[:, bank, :], wh[:, k, :], wl[:, k, :], r_hi[:, k, :], r_lo[:, k, :],
                                k == 0, k == FH - 1)
                ins.then_inc(w_used, 1)

            H_BASE = [16, 24, 40, 48]

            def mlp_down(d):
                u = U_DOWN[d]
                pe.wait_ge(h_written, H_BASE[d])
                down_unit(u, u % 2, 4, d)
                down_unit(u + 1, (u + 1) % 2, 5)
                with pe.Fori(1, 4) as t:
                    for j in range(2):
                        pe.wait_ge(h_written, H_BASE[d] + 2 * t + j - 1)
                        down_unit(u + j + 2 * t, (u + j) % 2, 4 + j)

            proj_out(0, FILL_OUT_A)
            norm_sum(1)
            mlp_up(0, FILL_MLP0, True)
            mlp_down(0)
            mlp_up(1, FILL_MLP0, False)
            mlp_down(1)

            norm_sum(2)
            s = U_KV % 2
            pe.wait_ge(w_lo_ready, U_KV + 1)
            wh = w_hi[:, s, :].rearrange("p (k n) -> p k n", k=KC)
            wl = w_lo[:, s, :].rearrange("p (k n) -> p k n", k=KC)
            for k in range(KC):
                pe.wait_ge(xn_ready, KC * FILL_KV + k + 1)
                ins = three(ps[:, 0, :], wh[:, k, 0:P], wl[:, k, 0:P], xn_hi[:, k, :], xn_lo[:, k, :],
                            k == 0, k == KC - 1)
            ins.then_inc(s_k, 1)
            for b in range(TB):
                xs = slice(b * P, (b + 1) * P)
                for k in range(KC):
                    ins = three(ps[:, 2, xs], xn_hi[:, k, xs], xn_lo[:, k, xs], wh[:, k, P:2 * P], wl[:, k, P:2 * P],
                                k == 0, k == KC - 1)
            ins.then_inc(w_used, 1)
            pe.wait_ge(s_sq, 1)
            mm(ps[:, 1, :], blk, sqt[:, 0, :], start=True, stop=True).then_inc(s_sum, 1)

            def swa_proj(i, k_waits=False):
                v, n = i // 2, i % 2
                u = U_Q + v
                s = u % 2
                if n == 0:
                    pe.wait_ge(w_lo_ready, u + 1)
                pe.wait_ge(s_qn, i + 1)
                wh = w_hi[:, s, :].rearrange("p (k n) -> p k n", k=KC)
                wl = w_lo[:, s, :].rearrange("p (k n) -> p k n", k=KC)
                for k in range(KC):
                    if k_waits:
                        pe.wait_ge(xn_ready, KC * FILL_Q + k + 1)
                    ins = three(ps[:, 0, :], wh[:, k, n * P:(n + 1) * P], wl[:, k, n * P:(n + 1) * P],
                                xn_hi[:, k, :], xn_lo[:, k, :], k == 0, k == KC - 1)
                ins.then_inc(w_used if n else s_q, 1)

            def swa_sum(i):
                pe.wait_ge(s_sq, i + 2)
                ins = mm(ps[:, 1, :], blk, sqt[:, 0, :], start=True, stop=True)
                ins.then_inc(s_sum, 1)

            def swa_max_scores(j):
                g = j // (PAIRS // 2)
                pe.wait_ge(s_hi, j + 2)
                for e in range(2):
                    b = 2 + 2 * e
                    h = slice(64 * e, 64 * e + 64)
                    bias = hka[:, 2 * j + e, :]
                    for qb, bank, c0 in ((1, b, 0), (2, b, 256), (3, b + 1, 0), (0, b + 1, 256)):
                        n = 2 * P if qb else P
                        o = ps[:, bank, c0:c0 + n]
                        k0 = max(qb - 1, 0) * P
                        mm(o, sq_hi[h, qb * P:(qb + 1) * P], kd_hi[h, g, k0:k0 + n], start=True, stop=False)
                        ins = mm(o, anti_r[:], bias[:, 2 * P - n:2 * P], start=False, stop=True)
                    ins.then_inc(s_sa, 1)

            def swa_scores(j):
                g = j // (PAIRS // 2)
                pe.wait_ge(s_lo, j + 2)
                for e in range(2):
                    pe.wait_ge(s_diag, 2 * j + e + 1)
                    after(pe, s_ot, 2 * j - 1 + e)
                    b = 2 + 2 * e
                    h = slice(64 * e, 64 * e + 64)
                    mm(ps[:, 6 + e, :], ones_r[:], sdiag[:, e, :], start=True, stop=True)
                    for kb, bank, c0 in ((0, b, 0), (1, b, 256), (2, b + 1, 0), (3, b + 1, 256)):
                        n = 2 * P if kb < TB - 1 else P
                        o = ps[:, bank, c0:c0 + n]
                        ks, qs = slice(kb * P, (kb + 1) * P), slice(kb * P, kb * P + n)
                        mm(o, kd_hi[h, g, ks], sq_hi[h, qs], start=True, stop=False)
                        mm(o, kd_hi[h, g, ks], sq_lo[h, qs], start=False, stop=False)
                        mm(o, kd_lo[h, g, ks], sq_hi[h, qs], start=False, stop=False)
                        mm(o, ones_r[:], sdiag[:, e, qs], start=False, stop=False)
                        mm(o, anti_r[:], hk_lo[:, 2 * j + e, 0:n], start=False, stop=False)
                        ins = mm(o, anti_r[:], hk_hi[:, 2 * j + e, 0:n], start=False, stop=True)
                    ins.then_inc(s_st, 1)

            def swa_pv(j):
                g = j // (PAIRS // 2)
                for e in range(2):
                    pe.wait_ge(s_p, 2 * j + e + 1)
                    mm(ps[:, 6 + e, :], kept[:, C_SINK + HD * e:C_SINK + HD * e + P], psink[e][:], start=True, stop=False)
                    for kb in range(TB):
                        n = 2 * P if kb < TB - 1 else P
                        ins = mm(ps[:, 6 + e, kb * P:kb * P + n], svx[:, g, kb, HD * e:HD * e + P],
                                 sp_[:, e, kb * 256:kb * 256 + n], start=False, stop=(kb == TB - 1))
                    ins.then_inc(s_o, 1)

            swa_proj(0, True)
            swa_sum(0)
            pe.wait_ge(s_ones, 1)
            for i in range(1, PAIRS):
                swa_max_scores(i - 1)
                swa_proj(i)
                swa_scores(i - 1)
                swa_sum(i)
                swa_pv(i - 1)
            swa_max_scores(7)
            swa_scores(7)
            swa_pv(7)
            proj_out(1, FILL_OUT_B)
            norm_sum(3)
            mlp_up(2, FILL_MLP1, True)
            mlp_down(2)
            mlp_up(3, FILL_MLP1, False)
            pe.wait_ge(h_written, H_BASE[3])

            def turn_out(n):
                pe.wait_ge(fin_ready, n + 1)
                after(pe, out_copied, n - 1)
                for b in range(TB):
                    ins = nc.tensor.transpose(ps[:, 6 + n % 2, b * P:(b + 1) * P], rst[:, n % 2, b * P:(b + 1) * P], ident)
                ins.then_inc(fin_turned, 1)

            for n in range(KC):
                after(pe, fin_ready, n - 1)
                down_unit(U_DOWN[3] + n, (U_DOWN[3] + n) % 2, 4 + n % 2, 3 if n == 0 else None)
                if n >= 1:
                    turn_out(n - 1)
            turn_out(KC - 1)


_INS = ["x", "g_attn", "g_mlp", "w_in_a", "b_f", "gq_a", "gk_a", "w_out_a", "g_kv", "w_kv", "gk_b",
        "w_q_b", "gq_b", "sinks", "rel_bias", "w_out_b", "w_up", "w_down"]


def kernel(**inputs):
    import numpy as _np
    import concourse.bacc as _bacc
    from concourse import mybir as _mybir
    from concourse.bass_utils import run_bass_kernel_spmd as _run

    nc = _bacc.Bacc("TRN2", target_bir_lowering=False, num_devices=1)
    arrays, args = {}, []
    for name in _INS + ["shape_consts"]:
        a = shape_constants() if name == "shape_consts" else _np.ascontiguousarray(inputs[name])
        arrays[f"in_{name}"] = a
        args.append(nc.dram_tensor(f"in_{name}", a.shape, _mybir.dt.from_np(a.dtype), kind="ExternalInput").ap())
    out = nc.dram_tensor("out", (1, T, D), _mybir.dt.float32, kind="ExternalOutput").ap()
    build(nc, *args, out)
    r = _run(nc, [arrays], core_ids=[0])
    return r.results[0]["out"]
```

```python
from contextlib import ExitStack

import numpy as np

import concourse.bass as bass
from concourse import mybir

ALU = mybir.AluOpType
ACT = mybir.ActivationFunctionType
F32 = mybir.dt.float32
F32R = mybir.dt.float32r
AX_X = mybir.AxisListType.X

P = 128
D = 1024
T = 512
HD = 64
HEADS = 16
PAIRS = HEADS // 2
F = 4 * D
KC = D // P
TB = T // P
FH = F // 2 // P
WINDOW = 128
N_BUCKETS = 32
REL_MAX_DIST = 128
EPS = 1e-6
NEG = -1e30
UNIT = 2048

U_V = 0
U_PAIR = 4
U_OUT = [12, 53]
U_UP = [16, 32, 57, 73]
U_DOWN = [24, 40, 65, 81]
U_KV = 48
U_Q = 49
N_UNITS = 89

FILL_ATTN0, FILL_OUT_A, FILL_MLP0, FILL_KV, FILL_Q, FILL_OUT_B, FILL_MLP1 = range(7)
GAIN = {FILL_ATTN0: 0, FILL_MLP0: 1, FILL_KV: 2, FILL_Q: 3, FILL_MLP1: 4}
XF_ORDER = {FILL_ATTN0: 0, FILL_MLP0: 1, FILL_KV: 2, FILL_Q: 3, FILL_MLP1: 4}

C_IDENT, C_BLK, C_OND = 0, 128, 256
C_TEMP = 384
C_ANTI, C_ONES, C_MASKA, C_MASKT, C_HOT, C_NEG = 384, 512, 640, 768, 896, 1280
C_ALL = 1664


def shape_constants():
    c = np.zeros((P, C_ALL), np.float32)
    c[:, C_IDENT:C_IDENT + P] = np.eye(P)
    for b in range(2):
        c[64 * b:64 * b + 64, C_BLK + 64 * b:C_BLK + 64 * b + 64] = 1.0 / HD
    c[:, C_OND:C_OND + P] = 1.0 / D
    c[:, C_ANTI:C_ANTI + P] = np.eye(P)[::-1]
    c[:, C_ONES:C_ONES + P] = 1.0
    r = np.arange(P)
    c[:, C_MASKA:C_MASKA + P] = np.where(r[None, :] > r[:, None], NEG, 0.0)
    c[:, C_MASKT:C_MASKT + P] = np.where(r[:, None] > r[None, :], NEG, 0.0)
    d = np.arange(WINDOW)
    exact = N_BUCKETS // 2
    large = exact + (np.log(np.maximum(d, 1) / exact) / np.log(REL_MAX_DIST / exact)
                     * (N_BUCKETS - exact)).astype(np.int32)
    bucket = np.where(d < exact, d, np.minimum(large, N_BUCKETS - 1))
    c[:, C_NEG:C_NEG + 384] = NEG
    for dist in range(WINDOW):
        c[bucket[dist], C_HOT + 127 + dist] = 1.0
        c[:, C_NEG + 127 + dist] = 0.0
    return c


def build(nc, x, g_attn, g_mlp, w_in_a, b_f, gq_a, gk_a, w_out_a, g_kv, w_kv, gk_b,
          w_q_b, gq_b, sinks, rel_bias, w_out_b, w_up, w_down, consts, out):
    with ExitStack() as ctx:
        base = nc.sbuf_base
        room = (nc.sbuf_bytes_remaining // 32) * 32
        ctx.enter_context(nc.sbuf_tensor("arena", [P, room // 4 - 8], F32))
        cursor = [(base + 31) // 32 * 32]
        limit = base + room - 32

        def at(name, shape, dt, offset):
            assert offset + 4 * int(np.prod(shape[1:])) <= limit, (name, offset, limit)
            return nc.alloc_sbuf_tensor_at(name, shape, dt, offset=offset)

        def sb(name, shape, dt=F32):
            t = at(name, shape, dt, cursor[0])
            cursor[0] += (4 * int(np.prod(shape[1:])) + 31) // 32 * 32
            return t

        def sem(name):
            return ctx.enter_context(nc.semaphore(name))

        hT = sb("hT", [P, KC, T])
        xn_hi = sb("xn_hi", [P, KC, T], F32R)
        xn_lo = sb("xn_lo", [P, KC, T], F32R)
        stage = sb("stage", [P, 2, UNIT])
        w_hi = sb("w_hi", [P, 2, UNIT], F32R)
        w_lo = sb("w_lo", [P, 2, UNIT], F32R)
        sq_off = cursor[0]
        sqt = sb("sqt", [P, 2, T])
        rst_off = cursor[0]
        rst = sb("rst", [P, 2, T])
        acc = rst[:, 1, :]
        qkn = sb("qkn", [P, 2, T])
        kept = sb("kept", [P, C_TEMP])
        ident_r = sb("ident_r", [P, P], F32R)
        ones_r = sb("ones_r", [P, P], F32R)
        anti_r = sb("anti_r", [P, P], F32R)
        maskA_r = sb("maskA_r", [P, P], F32R)
        maskT_r = sb("maskT_r", [P, P], F32R)
        gains = sb("gains", [P, 44])
        half_gains = sb("half_gains", [P, 4])
        bf = sb("bf", [P, 1])
        sinkb = sb("sinkb", [P, HEADS])
        nsink = sb("nsink", [P, HEADS])
        nm = sb("nm", [P, 2, TB])
        rel = sb("rel", [P, HEADS])
        area = cursor[0]
        KB = 1024

        o_t = at("o_t", [P, KC, T], F32, area + 78 * KB)
        hank = at("hank", [P, HEADS, 2 * WINDOW], F32, area + 78 * KB)
        x_hat = at("x_hat", [P, KC, T], F32, area)
        o_hi = [at("oa_hi", [P, KC, T], F32R, area), at("ob_hi", [P, KC, T], F32R, area)]
        o_lo = [at("oa_lo", [P, KC, T], F32R, area + 54 * KB), at("ob_lo", [P, KC, T], F32R, area + 16 * KB)]
        r_hi = at("r_hi", [P, FH, T], F32R, area)
        r_lo = at("r_lo", [P, FH, T], F32R, area + 32 * KB)
        out_sb = at("out_sb", [P, 2, TB, P], F32, area + 64 * KB)
        x_in = at("x_in", [P, TB, D], F32, area)
        ctemp = at("ctemp", [P, C_ALL - C_TEMP], F32, area + 16 * KB)
        g_in = at("g_in", [44, P], F32, area + 25 * KB)
        ext_sb = at("ext_sb", [HEADS, 384], F32, area + 46 * KB)
        v_all = at("v_all", [P, TB, D], F32, area)
        pT = at("pT", [P, 2, 1280], F32, area + 16 * KB)
        vx = at("vx", [P, TB, 192], F32, area + 27 * KB)
        qk_hi = at("qk_hi", [P, 2, 2, T], F32R, area + 30 * KB)
        qk_lo = at("qk_lo", [P, 2, T], F32R, area + 38 * KB)
        diag = at("diag", [P, 2, T], F32R, area + 42 * KB)
        c_split = at("c_split", [64, T], F32R, area + 74 * KB)
        pick = at("pick", [64, HEADS], F32, area + 76 * KB)
        ct = at("ct", [P, 4, T], F32, area + 46 * KB)
        raw = at("raw", [P, 2, T], F32, area + 70 * KB)
        wf = at("wf", [P, KC, P], F32, area + 54 * KB)
        wf_hi = at("wf_hi", [P, KC, P], F32R, area + 58 * KB)
        wf_lo = at("wf_lo", [P, KC, P], F32R, area + 62 * KB)
        hk_hi = at("hk_hi", [P, HEADS, 2 * WINDOW], F32R, area)
        hk_lo = at("hk_lo", [P, HEADS, 2 * WINDOW], F32R, area + 16 * KB)
        q_rst = at("q_rst", [P, T], F32, area + 32 * KB)
        q_raw = at("q_raw", [P, 2, T], F32, area + 34 * KB)
        v_rst = at("v_rst", [P, TB], F32, area + 38 * KB)
        sp_ = at("swa_p", [P, 2, 896], F32, area + 48 * KB)
        svx = at("swa_vx", [P, 2, TB, 192], F32, area + 55 * KB)
        sq_hi = at("swa_q_hi", [P, T], F32R, area + 61 * KB)
        sq_lo = at("swa_q_lo", [P, T], F32R, area + 63 * KB)
        kd_hi = at("kd_hi", [P, 2, T], F32R, area + 65 * KB)
        kd_lo = at("kd_lo", [P, 2, T], F32R, area + 69 * KB)
        sdiag = at("swa_diag", [P, 2, T], F32R, area + 73 * KB)
        psink = [at("psink0", [P, T], F32, sq_off + 2 * KB), at("psink1", [P, T], F32, rst_off + 2 * KB)]

        ident = kept[:, C_IDENT:C_IDENT + P]
        blk = kept[:, C_BLK:C_BLK + P]
        ones_d = kept[:, C_OND:C_OND + P]

        ps = ctx.enter_context(nc.psum_tensor("ps", [P, 8, T], F32))
        ext = nc.dram_tensor("ext", [HEADS, 384], F32, kind="Internal").ap()

        x_landed = [sem(f"x_landed{b}") for b in range(TB)]
        consts_landed = sem("consts_landed")
        ctemp_landed = sem("ctemp_landed")
        small_landed = sem("small_landed")
        landed = [sem("landed0"), sem("landed1")]
        w_hi_ready = sem("w_hi_ready")
        w_lo_ready = sem("w_lo_ready")
        w_used = sem("w_used")
        prep = sem("prep")
        gains_t = sem("gains_t")
        ext_ps = sem("ext_ps")
        ext_ready = sem("ext_ready")
        ext_stored = sem("ext_stored")
        hank_landed = sem("hank_landed")
        x_turned = sem("x_turned")
        h_written = sem("h_written")
        sq_ready = sem("sq_ready")
        acc_added = sem("acc_added")
        sum_added = sem("sum_added")
        n_refined = sem("n_refined")
        ln_done = sem("ln_done")
        rstd_ready = sem("rstd_ready")
        xhat_ready = sem("xhat_ready")
        xn_hi_ready = sem("xn_hi_ready")
        xn_ready = sem("xn_ready")
        v_stored = sem("v_stored")
        wf_zero = sem("wf_zero")
        wf_landed = sem("wf_landed")
        wf_split = sem("wf_split")
        gate_ps = sem("gate_ps")
        gate_step = sem("gate_step")
        gate_dve = sem("gate_dve")
        f_sq = sem("f_sq")
        f_sum = sem("f_sum")
        f_ln = sem("f_ln")
        f_rs = sem("f_rs")
        f_refined = sem("f_refined")
        f_proj = sem("f_proj")
        f_den = sem("f_den")
        f_qkn = sem("f_qkn")
        f_hi = sem("f_hi")
        f_lo = sem("f_lo")
        f_c = sem("f_c")
        f_vx = sem("f_vx")
        f_ones = sem("f_ones")
        f_sa = sem("f_sa")
        f_nm = sem("f_nm")
        f_diag = sem("f_diag")
        f_st = sem("f_st")
        f_p = sem("f_p")
        f_o = sem("f_o")
        f_rec = sem("f_rec")
        f_ot = sem("f_ot")
        s_hank = sem("s_hank")
        s_hank_read = sem("s_hank_read")
        s_kv = sem("s_kv")
        s_raw = sem("s_raw")
        s_vps = sem("s_vps")
        s_sq = sem("s_sq")
        s_sum = sem("s_sum")
        s_ln = sem("s_ln")
        s_rs = sem("s_rs")
        s_refined = sem("s_refined")
        s_qn = sem("s_qn")
        s_hi = sem("s_hi")
        s_lo = sem("s_lo")
        s_q = sem("s_q")
        s_sa = sem("s_sa")
        s_nm = sem("s_nm")
        s_nms = sem("s_nms")
        s_diag = sem("s_diag")
        s_st = sem("s_st")
        s_p = sem("s_p")
        s_o = sem("s_o")
        s_den = sem("s_den")
        s_rec = sem("s_rec")
        s_v = sem("s_v")
        s_ot = sem("s_ot")
        u_ready = sem("u_ready")
        sqf_done = sem("sqf_done")
        r_hi_ready = sem("r_hi_ready")
        r_ready = sem("r_ready")
        fin_ready = sem("fin_ready")
        fin_turned = sem("fin_turned")
        out_copied = sem("out_copied")
        out_stored = [sem("out_stored0"), sem("out_stored1")]

        def after(eng, s, count):
            if not (isinstance(count, int) and count <= 0):
                eng.wait_ge(s, count)

        SCORE_BANKS = ((2, 3, 4), (5, 6, 7))

        block = ctx.enter_context(nc.Block())

        @block.sync
        def _(sp):
            def slot_free(u):
                after(sp, w_lo_ready, u - 1)

            def load(u, s, src, **shape):
                slot_free(u)
                dst = stage[:, s, :].rearrange("p (k n) -> p k n", **shape)
                sp.dma_start(dst, src).then_inc(landed[s], 16)

            sp.dma_start(kept[:], consts[:, 0:C_TEMP]).then_inc(consts_landed, 16)
            for b in range(TB):
                sp.dma_start(x_in[:, b, :], x[0, b * P:(b + 1) * P, :]).then_inc(x_landed[b], 16)

            w_in = w_in_a[0].rearrange("(k p) n -> p k n", p=P)
            for v in range(4):
                if v == 2:
                    sp.dma_start(ctemp[:], consts[:, C_TEMP:C_ALL]).then_inc(ctemp_landed, 16)
                load(U_V + v, (U_V + v) % 2, w_in[:, :, 2 * D + 256 * v:2 * D + 256 * v + 256], k=KC)

            def load_pair(i, s):
                slot_free(U_PAIR + i)
                dst = stage[:, s, :].rearrange("p (t k n) -> p t k n", t=2, k=KC)
                for t in range(2):
                    sp.dma_start(dst[:, t], w_in[:, :, bass.ds(i * P + t * D, P)]).then_inc(landed[s], 16)

            with sp.Fori(0, PAIRS // 2) as i:
                for j in range(2):
                    load_pair(2 * i + j, (U_PAIR + j) % 2)

            def load_out(which, w):
                src = w.rearrange("(k p) n -> p k n", p=P)
                with sp.Fori(0, 2) as i:
                    for j in range(2):
                        u = U_OUT[which] + j
                        load(u + 2 * i, u % 2, src[:, :, bass.ds(i * 512 + 256 * j, 256)], k=KC)

            def load_mlp(d):
                layer, half = d // 2, d % 2
                up = w_up[layer].rearrange("(k p) n -> p k n", p=P)
                with sp.Fori(0, 4) as i:
                    for j in range(2):
                        u = U_UP[d] + j
                        load(u + 2 * i, u % 2, up[:, :, bass.ds(i * 512 + 256 * j + half * (F // 2), 256)], k=KC)
                down = w_down[layer, half * (F // 2):(half + 1) * (F // 2), :].rearrange("(k p) n -> p k n", p=P)
                with sp.Fori(0, 4) as i:
                    for j in range(2):
                        u = U_DOWN[d] + j
                        load(u + 2 * i, u % 2, down[:, :, bass.ds(i * 256 + 128 * j, P)], k=FH)

            load_out(0, w_out_a[0])
            load_mlp(0)
            sp.wait_ge(xn_ready, KC * (FILL_OUT_A + 1))
            sp.wait_ge(ext_stored, 16)
            hank_src = bass.AP(ext.tensor, 0, [[1, P], [384, HEADS], [1, 2 * WINDOW]])
            sp.dma_start(hank[:], hank_src).then_inc(hank_landed, 16)
            load_mlp(1)
            load(U_KV, U_KV % 2, w_kv.rearrange("(k p) n -> p k n", p=P), k=KC)
            wq = w_q_b[0].rearrange("(k p) n -> p k n", p=P)
            for v in range(4):
                load(U_Q + v, (U_Q + v) % 2, wq[:, :, 256 * v:256 * v + 256], k=KC)
            load_out(1, w_out_b[0])
            load_mlp(2)
            load_mlp(3)
            dst = out[0].rearrange("(b p) n -> p b n", p=P)
            for n in range(KC):
                sp.wait_ge(out_copied, n + 1)
                sp.dma_start(dst[:, :, n * P:(n + 1) * P], out_sb[:, n % 2]).then_inc(out_stored[n % 2], 16)
            for s in range(2):
                sp.wait_ge(out_stored[s], 16 * KC // 2)

        @block.gpsimd
        def _(pool):
            nc.gpsimd.memset(wf[:], 0.0).then_inc(wf_zero, 1)

            def low(u, s):
                pool.wait_ge(w_hi_ready, u + 1)
                for q in range(4):
                    c = slice(q * UNIT // 4, (q + 1) * UNIT // 4)
                    ins = nc.gpsimd.tensor_tensor(w_lo[:, s, c], stage[:, s, c], w_hi[:, s, c].bitcast(F32),
                                                  ALU.subtract)
                ins.then_inc(w_lo_ready, 1)

            with pool.Fori(0, N_UNITS // 2) as i:
                low(2 * i, 0)
                low(2 * i + 1, 1)
            low(N_UNITS - 1, 0)

        @block.scalar
        def _(act):
            def split(count, u, s):
                act.wait_ge(landed[s], 16 * count)
                after(act, w_used, u - 1)
                nc.scalar.activation(w_hi[:, s, :], stage[:, s, :], ACT.Copy).then_inc(w_hi_ready, 1)

            act.preload_act_table_set("natural_log_exp_and_others")
            act.dma_start(g_in[0:8, :], g_attn[0].rearrange("(k p) -> k p", p=P)).then_inc(small_landed, 16)
            act.dma_start(g_in[8:16, :], g_mlp[0].rearrange("(k p) -> k p", p=P)).then_inc(small_landed, 16)
            act.dma_start(g_in[16:24, :], g_kv.rearrange("(k p) -> k p", p=P)).then_inc(small_landed, 16)
            act.dma_start(g_in[24:32, :], g_attn[1].rearrange("(k p) -> k p", p=P)).then_inc(small_landed, 16)
            act.dma_start(g_in[32:40, :], g_mlp[1].rearrange("(k p) -> k p", p=P)).then_inc(small_landed, 16)
            for n, g in enumerate((gq_a[0], gk_a[0], gq_b[0], gk_b)):
                for half in range(2):
                    act.dma_start(g_in[40 + n:41 + n, 64 * half:64 * half + 64], g[None, :]).then_inc(small_landed, 16)
            act.dma_start(rel[0:N_BUCKETS, :], rel_bias).then_inc(small_landed, 16)
            act.dma_start(sinkb[:], sinks[0].partition_broadcast(P)).then_inc(small_landed, 16)
            act.wait_ge(wf_zero, 2)
            act.dma_start(bf[0:HEADS, :], b_f[0].rearrange("(h o) -> h o", o=1)).then_inc(wf_landed, 16)
            act.dma_start(wf[:, :, 0:HEADS], w_in_a[0].rearrange("(k p) n -> p k n", p=P)[:, :, 3 * D:3 * D + HEADS]
                          ).then_inc(wf_landed, 16)

            split(1, 0, 0)
            split(1, 1, 1)

            def norm_square(q, h_base, c, slot):
                act.wait_ge(h_written, h_base + c + 1)
                after(act, acc_added, 9 * q + c if not (q == 0 and isinstance(c, int) and c < 2) else 0)
                src = hT[:, bass.ds(c, 1), :].rearrange("p a n -> p (a n)")
                nc.scalar.activation(sqt[:, slot, :], src, ACT.Square).then_inc(sq_ready, 1)

            def norm_rstd(q):
                act.wait_ge(sum_added, q + 1)
                nc.scalar.activation(rst[:, 0, :], ps[:, 7, :], ACT.Ln, bias=EPS).then_inc(ln_done, 1)
                act.wait_ge(ln_done, 2 * q + 1)
                nc.scalar.activation(rst[:, 0, :], rst[:, 0, :], ACT.Exp, scale=-0.5).then_inc(ln_done, 1)
                act.wait_ge(ln_done, 2 * q + 2)
                nc.scalar.activation(sqt[:, 0, :], rst[:, 0, :], ACT.Square).then_inc(rstd_ready, 1)

            def fill_hi():
                for c in range(KC):
                    act.wait_ge(xhat_ready, c + 1)
                    nc.scalar.activation(xn_hi[:, c, :], x_hat[:, c, :], ACT.Identity,
                                         scale=gains[:, c:c + 1]).then_inc(xn_hi_ready, 1)

            def h_hi(fill, h_base, c):
                act.wait_ge(h_written, h_base + c + 1)
                src = hT[:, bass.ds(c, 1), :].rearrange("p a n -> p (a n)")
                dst = xn_hi[:, bass.ds(c, 1), :].rearrange("p a n -> p (a n)")
                nc.scalar.activation(dst, src, ACT.Identity,
                                     scale=gains[:, bass.ds(8 * GAIN[fill] + c, 1)]).then_inc(xn_hi_ready, 1)

            for c in range(KC):
                norm_square(0, 0, c, c % 2)
            norm_rstd(0)
            act.wait_ge(prep, 1)
            fill_hi()
            for v in range(4):
                u = U_V + v + 2
                split(u // 2 + 1 if u < U_PAIR else 2 + 2, u, u % 2)
                if v == 1:
                    act.wait_ge(ext_ready, 1)
                    act.dma_start(ext, ext_sb[:]).then_inc(ext_stored, 16)

            act.wait_ge(gate_ps, 1)
            act.wait_ge(ext_stored, 16)
            nc.scalar.activation(ct[:, 0, :], ps[:, 6, :], ACT.Identity, bias=bf[:, 0:1]).then_inc(gate_step, 1)
            act.wait_ge(gate_step, 1)
            nc.scalar.activation(ct[:, 1, :], ct[:, 0, :], ACT.Abs).then_inc(gate_step, 1)
            act.wait_ge(gate_step, 2)
            nc.scalar.activation(ct[:, 1, :], ct[:, 1, :], ACT.Exp, scale=-1.0).then_inc(gate_step, 1)
            act.wait_ge(gate_step, 3)
            nc.scalar.activation(ct[:, 1, :], ct[:, 1, :], ACT.Ln, bias=1.0).then_inc(gate_step, 1)

            def fox_square(i, t):
                if t == 0:
                    act.wait_ge(f_proj, i + 1)
                else:
                    act.wait_ge(w_used, U_PAIR + i + 1)
                after(act, f_qkn, 2 * i - 1 + t)
                nc.scalar.activation(raw[:, t, :], ps[:, t, :], ACT.Copy)
                nc.scalar.activation(sqt[:, t, :], ps[:, t, :], ACT.Square).then_inc(f_sq, 1)

            def fox_rstd(i, t):
                act.wait_ge(f_sum, 2 * i + t + 1)
                nc.scalar.activation(rst[:, t, :], ps[:, t, :], ACT.Ln, bias=EPS).then_inc(f_ln, 1)
                act.wait_ge(f_ln, 4 * i + 2 * t + 1)
                nc.scalar.activation(rst[:, t, :], rst[:, t, :], ACT.Exp, scale=-0.5).then_inc(f_ln, 1)
                act.wait_ge(f_ln, 4 * i + 2 * t + 2)
                nc.scalar.activation(sqt[:, t, :], rst[:, t, :], ACT.Square).then_inc(f_rs, 1)

            def fox_hi(i):
                act.wait_ge(f_qkn, 2 * i + 2)
                for e in range(2):
                    after(act, f_st, 2 * i - 1 + e)
                    own = slice(64 * e, 64 * e + 64)
                    nc.scalar.activation(qk_hi[own, :, e, :], qkn[own], ACT.Copy).then_inc(f_hi, 1)

            def fox_exp(j, e):
                act.wait_ge(f_st, 2 * j + e + 1)
                after(act, f_o, 2 * j - 1 + e)
                b0, b1, b2 = SCORE_BANKS[e]
                for bank, n, dst in ((b0, 512, 0), (b1, 512, 512), (b2, 256, 1024)):
                    ins = nc.scalar.activation(pT[:, e, dst:dst + n], ps[:, bank, 0:n], ACT.Exp)
                ins.then_inc(f_p, 1)

            for t in range(2):
                fox_square(0, t)
                fox_rstd(0, t)
            fox_hi(0)
            split(2 + 4, U_PAIR + 2, 0)

            def fox_den(j):
                for e in range(2):
                    act.wait_ge(f_o, 2 * j + e + 1)
                    own, other = slice(64 * e, 64 * e + 64), slice(64 - 64 * e, 128 - 64 * e)
                    after(act, f_ot, 2 * j)
                    ins = nc.scalar.activation(ct[own, 3, :], ps[other, 4 + 3 * e, :], ACT.Copy)
                ins.then_inc(f_den, 1)

            def fox_step(i, landed_count, s):
                fox_square(i, 0)
                fox_rstd(i, 0)
                fox_square(i, 1)
                fox_exp(i - 1, 0)
                fox_rstd(i, 1)
                fox_exp(i - 1, 1)
                fox_hi(i)
                fox_den(i - 1)
                split(landed_count, U_PAIR + i + 2, s)

            fox_step(1, 2 + 4, 1)
            with act.Fori(1, 3) as t:
                fox_step(2 * t, 2 + 4 + 2 * t, 0)
                fox_step(2 * t + 1, 2 + 4 + 2 * t, 1)
            fox_step(6, 2 + 8 + 1, 0)
            fox_step(7, 2 + 8 + 1, 1)
            def out_hi(which, ready, c):
                act.wait_ge(ready, 2 * c + 2)
                nc.scalar.activation(o_hi[which][:, c, :], o_t[:, c, :], ACT.Copy).then_inc(xn_hi_ready, 1)

            SLOT = 5

            def split_units(u0, n):
                with act.Fori(0, n // 2) as t:
                    for j in range(2):
                        u = u0 + j
                        split(u // 2 + SLOT + t, u + 2 * t, u % 2)

            act.wait_ge(f_vx, PAIRS)
            for c in range(2):
                out_hi(0, f_ot, c)
            fox_exp(7, 0)
            for c in range(2, 4):
                out_hi(0, f_ot, c)
            fox_exp(7, 1)
            for c in range(4, KC - 1):
                out_hi(0, f_ot, c)
            fox_den(7)
            out_hi(0, f_ot, KC - 1)

            def out_units(which, q, fill, h_base):
                with act.Fori(0, 2) as t:
                    for j in range(2):
                        u = U_OUT[which] + 2 + j
                        split(u // 2 + SLOT + t, u + 2 * t, u % 2)
                        for n in range(2):
                            c = 4 * t + 2 * j + n
                            norm_square(q, h_base, c, n)
                            h_hi(fill, h_base, c)
                norm_rstd(q)

            out_units(0, 1, FILL_MLP0, 8)

            def mlp_up(d):
                def unit(i, s, count):
                    split(count, U_UP[d] + i + 2, (U_UP[d] + s) % 2)
                    act.wait_ge(u_ready, 8 * d + i + 1)
                    nc.scalar.activation(r_hi[:, bass.ds(2 * i, 2), :], qkn[:], ACT.Square, scale=0.5
                                         ).then_inc(r_hi_ready, 1)

                c = [(U_UP[d] + j + 2) // 2 + SLOT for j in range(2)]
                with act.Fori(0, 4) as t:
                    for j in range(2):
                        unit(2 * t + j, j, c[j] + t)

            mlp_up(0)
            split_units(U_DOWN[0] + 2, 8)
            mlp_up(1)
            with act.Fori(0, 4) as t:
                for j in range(2):
                    u = U_DOWN[1] + 2 + j
                    norm_square(2, 24, 2 * t + j, j)
                    h_hi(FILL_KV, 24, 2 * t + j)
                    split(u // 2 + SLOT + t, u + 2 * t, u % 2)

            act.wait_ge(hank_landed, 16)
            act.wait_ge(w_used, U_KV)
            nc.scalar.activation(hk_hi[:], hank[:], ACT.Copy).then_inc(s_hank, 1)

            def query_hi(c):
                if c < KC - 1:
                    act.wait_ge(s_kv, c + 1)
                else:
                    act.wait_ge(w_used, U_KV + 1)
                h_hi(FILL_Q, 24, c)

            for c in range(4):
                query_hi(c)
            norm_rstd(2)
            for c in range(4, KC):
                query_hi(c)

            def swa_square(m, raw):
                act.wait_ge(s_raw, m + 1)
                after(act, s_refined, 2 * m)
                nc.scalar.activation(sqt[:, 0, :], raw, ACT.Square, scale=0.5).then_inc(s_sq, 1)

            def swa_rstd(m):
                act.wait_ge(s_sum, m + 1)
                after(act, s_qn, m)
                nc.scalar.activation(q_rst[:], ps[:, 1, :], ACT.Ln, bias=EPS).then_inc(s_ln, 1)
                act.wait_ge(s_ln, 2 * m + 1)
                nc.scalar.activation(q_rst[:], q_rst[:], ACT.Exp, scale=-0.5).then_inc(s_ln, 1)
                act.wait_ge(s_ln, 2 * m + 2)
                nc.scalar.activation(sqt[:, 0, :], q_rst[:], ACT.Square).then_inc(s_rs, 1)

            def swa_hi(i):
                act.wait_ge(s_qn, i + 2)
                after(act, s_st, 2 * i)
                nc.scalar.activation(sq_hi[:], qkn[:, 0, :], ACT.Copy).then_inc(s_hi, 1)

            def swa_exp(j, e):
                act.wait_ge(s_st, 2 * j + e + 1)
                after(act, s_o, 2 * j - 1 + e)
                after(act, s_den, 2 * j - 1 + e)
                b = 2 + 2 * e
                nc.scalar.activation(psink[e][:], ps[:, 6 + e, :], ACT.Exp, bias=sinkb[:, 2 * j + e:2 * j + e + 1])
                nc.scalar.activation(sp_[:, e, 0:512], ps[:, b, :], ACT.Exp)
                nc.scalar.activation(sp_[:, e, 512:896], ps[:, b + 1, 0:384], ACT.Exp).then_inc(s_p, 1)

            def split_q(v):
                u = U_Q + v
                split(u // 2 + SLOT, u, u % 2)

            swa_square(0, qkn[:, 1, :])
            split_q(1)
            swa_rstd(0)
            act.wait_ge(s_qn, 1)
            for g in range(2):
                for half in range(2):
                    ins = nc.scalar.activation(kd_hi[64 * half:64 * half + 64, g, :], qkn[64 * g:64 * g + 64, 1, :],
                                               ACT.Copy)
            ins.then_inc(s_hi, 1)
            swa_square(1, q_raw[:, 0, :])
            swa_rstd(1)
            swa_hi(0)
            swa_square(2, q_raw[:, 1, :])
            split_q(2)
            for j in range(PAIRS - 1):
                swa_rstd(j + 2)
                if j + 2 < PAIRS:
                    swa_square(j + 3, q_raw[:, j % 2, :])
                swa_exp(j, 0)
                swa_exp(j, 1)
                swa_hi(j + 1)
                if j % 2 == 1:
                    split_q(3 + j // 2)
            for c in range(2):
                out_hi(1, s_ot, c)
            swa_exp(7, 0)
            for c in range(2, 4):
                out_hi(1, s_ot, c)
            swa_exp(7, 1)
            for c in range(4, KC):
                out_hi(1, s_ot, c)
            out_units(1, 3, FILL_MLP1, 32)

            mlp_up(2)
            split_units(U_DOWN[2] + 2, 8)
            mlp_up(3)
            for n in range(KC):
                if n + 2 < KC:
                    u = U_DOWN[3] + n + 2
                    split(u // 2 + SLOT, u, u % 2)
                if n >= 1:
                    turn_out = n - 1
                    act.wait_ge(fin_turned, turn_out + 1)
                    after(act, out_stored[turn_out % 2], 16 * (turn_out // 2))
                    nc.scalar.activation(out_sb[:, turn_out % 2], ps[:, 6 + turn_out % 2, :].rearrange(
                        "p (b n) -> p b n", b=TB), ACT.Copy).then_inc(out_copied, 1)
            act.wait_ge(fin_turned, KC)
            act.wait_ge(out_stored[1], 16 * (KC // 2 - 1))
            nc.scalar.activation(out_sb[:, 1], ps[:, 7, :].rearrange("p (b n) -> p b n", b=TB),
                                 ACT.Copy).then_inc(out_copied, 1)

        @block.vector
        def _(dve):
            V = nc.vector

            nc.vector.memset(bf[:], 0.0).then_inc(wf_zero, 1)

            def acc_zero():
                V.memset(acc, 0.0).then_inc(acc_added, 1)

            def norm_add(q, c, slot):
                dve.wait_ge(sq_ready, KC * q + c + 1)
                dve.wait_ge(acc_added, 9 * q + c + 1)
                V.tensor_tensor(acc, acc, sqt[:, slot, :], ALU.add).then_inc(acc_added, 1)

            def newton(square, mean_square, y, refined, count):
                V.scalar_tensor_tensor(out=square, in0=mean_square, scalar=EPS, in1=square, op0=ALU.add,
                                       op1=ALU.mult).then_inc(refined, 1)
                dve.wait_ge(refined, count - 1)
                V.scalar_tensor_tensor(out=y, in0=square, scalar=-3.0, in1=y, op0=ALU.add,
                                       op1=ALU.mult).then_inc(refined, 1)
                dve.wait_ge(refined, count)

            def norm_refine(q):
                dve.wait_ge(rstd_ready, q + 1)
                newton(sqt[:, 0, :], ps[:, 7, :], rst[:, 0, :], n_refined, 2 * q + 2)

            acc_zero()
            for c in range(KC):
                dve.wait_ge(x_turned, c + 1)
                V.tensor_copy(hT[:, c, :], ps[:, c % 4, :]).then_inc(h_written, 1)
                if c >= 1:
                    norm_add(0, c - 1, (c - 1) % 2)
            norm_add(0, KC - 1, (KC - 1) % 2)
            dve.wait_ge(gains_t, 1)
            V.tensor_copy(gains[:], ps[:, 6, 0:44]).then_inc(prep, 1)
            dve.wait_ge(prep, 1)
            for n, scale in enumerate((-0.5 * float(HD) ** -0.5, -0.5, 0.25 * float(HD) ** -0.5, 0.25)):
                V.tensor_scalar(half_gains[:, n:n + 1], gains[:, 40 + n:41 + n], scale, None, ALU.mult)
            V.tensor_scalar(nsink[:], sinkb[:], -1.0, None, ALU.mult).then_inc(prep, 1)

            def x_hat_chunk(c):
                V.scalar_tensor_tensor(out=x_hat[:, c, :], in0=hT[:, c, :], scalar=-0.5, in1=rst[:, 0, :],
                                       op0=ALU.mult, op1=ALU.mult).then_inc(xhat_ready, 1)

            def fill_norm():
                x_hat_chunk(0)
                x_hat_chunk(1)
                for c in range(KC):
                    dve.wait_ge(xhat_ready, c + 1)
                    dve.wait_ge(xn_hi_ready, c + 1)
                    V.scalar_tensor_tensor(out=xn_lo[:, c, :], in0=x_hat[:, c, :], scalar=gains[:, c:c + 1],
                                           in1=xn_hi[:, c, :].bitcast(F32), op0=ALU.mult, op1=ALU.subtract
                                           ).then_inc(xn_ready, 1)
                    if c + 2 < KC:
                        x_hat_chunk(c + 2)

            def h_lo(fill, c):
                dve.wait_ge(xn_hi_ready, KC * fill + c + 1)
                one = [t[:, bass.ds(c, 1), :].rearrange("p a n -> p (a n)") for t in (hT, xn_hi, xn_lo)]
                V.scalar_tensor_tensor(out=one[2], in0=one[0], scalar=gains[:, bass.ds(8 * GAIN[fill] + c, 1)],
                                       in1=one[1].bitcast(F32), op0=ALU.mult, op1=ALU.subtract).then_inc(xn_ready, 1)

            def out_lo(which, fill, c):
                dve.wait_ge(xn_hi_ready, KC * fill + c + 1)
                V.tensor_tensor(o_lo[which][:, c, :], o_t[:, c, :], o_hi[which][:, c, :].bitcast(F32),
                                ALU.subtract).then_inc(xn_ready, 1)

            norm_refine(0)
            fill_norm()
            dve.wait_ge(wf_landed, 32)
            V.tensor_copy(wf_hi[:], wf[:]).then_inc(wf_split, 1)
            dve.wait_ge(wf_split, 1)
            V.tensor_tensor(wf_lo[:], wf[:], wf_hi[:].bitcast(F32), ALU.subtract).then_inc(wf_split, 1)
            V.memset(vx[:, :, HD:2 * HD], 1.0).then_inc(f_ones, 1)
            for v in range(4):
                dve.wait_ge(w_used, U_V + v + 1)
                b = 4 * (v % 2)
                V.tensor_copy(v_all[:, :, 256 * v:256 * v + 256], ps[:, b:b + 4, 0:256]).then_inc(v_stored, 1)
                if v == 0:
                    dve.wait_ge(ctemp_landed, 16)
                    for dst, src in ((ident_r, ident), (anti_r, C_ANTI), (ones_r, C_ONES), (maskA_r, C_MASKA),
                                     (maskT_r, C_MASKT)):
                        if isinstance(src, int):
                            src = ctemp[:, src - C_TEMP:src - C_TEMP + P]
                        ins = V.tensor_copy(dst[:], src)
                    for e in range(2):
                        V.tensor_copy(qk_hi[64 - 64 * e:128 - 64 * e, 0, e, :].rearrange("p (b n) -> p b n", b=TB),
                                      ctemp[64 - 64 * e:128 - 64 * e, None, C_ONES - C_TEMP:C_ONES - C_TEMP + P
                                            ].to_broadcast([64, TB, P]))
                    V.tensor_tensor(pick[:], ident[0:64, 0:HEADS], ident[0:64, 32:32 + HEADS], ALU.add).then_inc(prep, 1)
                if v == 1:
                    dve.wait_ge(ext_ps, 1)
                    V.tensor_tensor(ext_sb[:], ps[0:HEADS, 2, 0:384], ctemp[0:HEADS, C_NEG - C_TEMP:C_NEG - C_TEMP + 384],
                                    ALU.add).then_inc(ext_ready, 1)
            dve.wait_ge(ext_stored, 16)
            V.memset(ct[:, 3, :], 1.0).then_inc(gate_dve, 1)
            dve.wait_ge(gate_step, 4)
            V.scalar_tensor_tensor(out=ct[:, 1, :], in0=ct[:, 0, :], scalar=0.0, in1=ct[:, 1, :],
                                   op0=ALU.min, op1=ALU.subtract).then_inc(gate_dve, 1)
            dve.wait_ge(gate_dve, 2)
            V.tensor_tensor_scan(out=ct[:, 2, :], data0=ct[:, 3, :], data1=ct[:, 1, :], initial=0.0,
                                 op0=ALU.mult, op1=ALU.subtract).then_inc(gate_dve, 1)
            dve.wait_ge(gate_dve, 3)
            V.tensor_copy(c_split[0:32, :], ct[0:32, 2, :]).then_inc(gate_dve, 1)
            dve.wait_ge(gate_dve, 4)
            V.tensor_tensor(c_split[32:64, :], ct[0:32, 2, :], c_split[0:32, :].bitcast(F32),
                            ALU.subtract).then_inc(gate_dve, 1)
            dve.wait_ge(gate_dve, 5)

            def fox_c(i):
                for e in range(2):
                    after(dve, f_st, 2 * i - 1 + e)
                    V.tensor_scalar(qk_hi[64 - 64 * e:128 - 64 * e, 1, e, :], c_split[:].bitcast(F32),
                                    pick[:, bass.ds(2 * i + e, 1)], None, ALU.mult).then_inc(f_c, 1)

            def fox_vx(i):
                after(dve, f_o, 2 * i)
                for e in range(2):
                    ins = V.tensor_copy(vx[:, :, 2 * HD * e:2 * HD * e + HD], v_all[:, :, bass.ds(i * P + HD * e, HD)])
                ins.then_inc(f_vx, 1)

            def fox_norm(i, t):
                dve.wait_ge(f_rs, 2 * i + t + 1)
                newton(sqt[:, t, :], ps[:, t, :], rst[:, t, :], f_refined, 4 * i + 2 * t + 2)
                after(dve, f_lo, 2 * i)
                V.scalar_tensor_tensor(out=qkn[:, t, :], in0=raw[:, t, :], scalar=half_gains[:, t:t + 1],
                                       in1=rst[:, t, :], op0=ALU.mult, op1=ALU.mult).then_inc(f_qkn, 1)

            def fox_lo(i):
                for e in range(2):
                    dve.wait_ge(f_hi, 2 * i + e + 1)
                    own = slice(64 * e, 64 * e + 64)
                    V.tensor_tensor(qk_lo[own], qkn[own], qk_hi[own, :, e, :].bitcast(F32),
                                    ALU.subtract).then_inc(f_lo, 1)

            def fox_max(j):
                for e in range(2):
                    dve.wait_ge(f_sa, 2 * j + e + 1)
                    after(dve, f_diag, 2 * j - 1 + e)
                    b0, b1, b2 = SCORE_BANKS[e]
                    for qb, bank, c0, n in ((3, b0, 0, 512), (2, b1, 0, 384), (0, b1, 384, 128), (1, b2, 0, 256)):
                        ins = V.tensor_reduce(nm[:, e, qb:qb + 1], ps[:, bank, c0:c0 + n], AX_X, ALU.max, negate=True)
                    ins.then_inc(f_nm, 1)
                    dve.wait_ge(f_nm, 2 * j + e + 1)
                    after(dve, f_st, 2 * j - 1 + e)
                    V.tensor_tensor(diag[:, e, :].rearrange("p (b n) -> p b n", b=TB),
                                    ident[:, None, :].to_broadcast([P, TB, P]),
                                    nm[:, e, :, None].to_broadcast([P, TB, P]), ALU.mult).then_inc(f_diag, 1)

            def fox_out(j):
                dve.wait_ge(f_den, j + 1)
                V.reciprocal(ct[:, 3, :], ct[:, 3, :]).then_inc(f_rec, 1)
                dve.wait_ge(f_rec, j + 1)
                for e in range(2):
                    own = slice(64 * e, 64 * e + 64)
                    dst = o_t[own, bass.ds(j, 1), :].rearrange("p a n -> p (a n)")
                    V.tensor_tensor(dst, ps[own, 4 + 3 * e, :], ct[own, 3, :], ALU.mult).then_inc(f_ot, 1)

            def fox_step(i):
                fox_max(i - 1)
                fox_norm(i, 0)
                fox_norm(i, 1)
                fox_c(i)
                fox_lo(i)
                fox_out(i - 1)
                fox_vx(i)

            fox_c(0)
            fox_vx(0)
            fox_norm(0, 0)
            fox_norm(0, 1)
            fox_lo(0)
            fox_step(1)
            with dve.Fori(1, 4) as t:
                fox_step(2 * t)
                fox_step(2 * t + 1)
            for c in range(2):
                out_lo(0, FILL_OUT_A, c)
            fox_max(7)
            for c in range(2, KC - 1):
                out_lo(0, FILL_OUT_A, c)
            fox_out(7)
            out_lo(0, FILL_OUT_A, KC - 1)

            def add_chunk(bank, c):
                dst = hT[:, bass.ds(c, 1), :].rearrange("p a n -> p (a n)")
                V.tensor_tensor(dst, dst, ps[:, bank, :], ALU.add).then_inc(h_written, 1)

            def add_out(which, q, fill):
                acc_zero()
                with dve.Fori(0, 2) as t:
                    for j in range(2):
                        dve.wait_ge(w_used, U_OUT[which] + 2 * t + j + 1)
                        for n in range(2):
                            add_chunk(2 * j + n, 4 * t + 2 * j + n)
                        for n in range(2):
                            norm_add(q, 4 * t + 2 * j + n, n)
                            h_lo(fill, 4 * t + 2 * j + n)
                norm_refine(q)

            def mlp_up(d):
                scale = rst[:, 0:1, :].to_broadcast([P, 2, T])
                with dve.Fori(0, 4) as t:
                    for j in range(2):
                        i = 2 * t + j
                        dve.wait_ge(w_used, U_UP[d] + i + 1)
                        V.scalar_tensor_tensor(out=qkn[:], in0=ps[:, 2 * j:2 * j + 2, :], scalar=0.0, in1=scale,
                                               op0=ALU.max, op1=ALU.mult).then_inc(u_ready, 1)
                        dve.wait_ge(u_ready, 8 * d + i + 1)
                        V.scalar_tensor_tensor(out=sqt[:], in0=qkn[:], scalar=0.25, in1=qkn[:], op0=ALU.mult,
                                               op1=ALU.mult).then_inc(sqf_done, 1)
                        dve.wait_ge(sqf_done, 8 * d + i + 1)
                        dve.wait_ge(r_hi_ready, 8 * d + i + 1)
                        V.tensor_tensor(r_lo[:, bass.ds(2 * i, 2), :], sqt[:],
                                        r_hi[:, bass.ds(2 * i, 2), :].bitcast(F32), ALU.subtract).then_inc(r_ready, 1)
                        dve.wait_ge(r_ready, 8 * d + i + 1)

            def mlp_down(d, q=None, fill=None):
                if q is not None:
                    acc_zero()
                with dve.Fori(0, 4) as t:
                    for j in range(2):
                        dve.wait_ge(w_used, U_DOWN[d] + 2 * t + j + 1)
                        add_chunk(4 + j, 2 * t + j)
                        if q is not None:
                            norm_add(q, 2 * t + j, j)
                            h_lo(fill, 2 * t + j)

            add_out(0, 1, FILL_MLP0)
            mlp_up(0)
            mlp_down(0)
            mlp_up(1)
            mlp_down(1, 2, FILL_KV)

            dve.wait_ge(s_hank, 1)
            V.tensor_tensor(hk_lo[:], hank[:], hk_hi[:].bitcast(F32), ALU.subtract).then_inc(s_hank_read, 1)
            for c in range(4):
                h_lo(FILL_Q, c)
            norm_refine(2)
            for c in range(4, KC - 1):
                h_lo(FILL_Q, c)

            def swa_raw(m, bank, dst):
                V.tensor_tensor(dst, ps[:, bank, :], rst[:, 0, :], ALU.mult).then_inc(s_raw, 1)

            def swa_query_raw(i):
                if i % 2 == 0:
                    dve.wait_ge(s_q, i // 2 + 1)
                else:
                    dve.wait_ge(w_used, U_Q + i // 2 + 1)
                swa_raw(i + 1, 0, q_raw[:, i % 2, :])

            def swa_norm(m, raw, dst, gain):
                dve.wait_ge(s_rs, m + 1)
                newton(sqt[:, 0, :], ps[:, 1, :], q_rst[:], s_refined, 2 * m + 2)
                V.scalar_tensor_tensor(out=dst, in0=raw, scalar=half_gains[:, gain:gain + 1], in1=q_rst[:],
                                       op0=ALU.mult, op1=ALU.mult).then_inc(s_qn, 1)

            def swa_lo(i):
                dve.wait_ge(s_hi, i + 2)
                after(dve, s_st, 2 * i)
                V.tensor_tensor(sq_lo[:], qkn[:, 0, :], sq_hi[:].bitcast(F32), ALU.subtract).then_inc(s_lo, 1)

            dve.wait_ge(w_used, U_KV + 1)
            swa_raw(0, 1, qkn[:, 1, :])
            h_lo(FILL_Q, KC - 1)
            dve.wait_ge(s_vps, 1)
            V.tensor_scalar(v_rst[:], ps[:, 6, 0:TB], -0.5, None, ALU.mult).then_inc(s_v, 1)
            V.memset(svx[:, :, :, HD:2 * HD], 1.0)
            dve.wait_ge(s_v, 1)
            for g in range(2):
                for half in range(2):
                    ins = V.tensor_tensor(svx[:, g, :, 2 * HD * half:2 * HD * half + HD],
                                          ps[:, 2, :].rearrange("p (b n) -> p b n", b=TB)[:, :, HD * g:HD * g + HD],
                                          v_rst[:, :, None].to_broadcast([P, TB, HD]), ALU.mult)
            ins.then_inc(s_v, 1)
            swa_norm(0, qkn[:, 1, :], qkn[:, 1, :], 3)
            swa_query_raw(0)
            dve.wait_ge(s_hi, 1)
            dve.wait_ge(s_qn, 1)
            for g in range(2):
                for half in range(2):
                    ins = V.tensor_tensor(kd_lo[64 * half:64 * half + 64, g, :], qkn[64 * g:64 * g + 64, 1, :],
                                          kd_hi[64 * g:64 * g + 64, g, :].bitcast(F32), ALU.subtract)
            ins.then_inc(s_lo, 1)
            swa_norm(1, q_raw[:, 0, :], qkn[:, 0, :], 2)
            swa_query_raw(1)
            swa_lo(0)

            def swa_max(j):
                for e in range(2):
                    dve.wait_ge(s_sa, 2 * j + e + 1)
                    after(dve, s_diag, 2 * j - 1 + e)
                    b = 2 + 2 * e
                    V.tensor_reduce(nm[:, e, 1:3], ps[:, b, :].rearrange("p (b n) -> p b n", b=2), AX_X, ALU.max,
                                    negate=True)
                    V.tensor_reduce(nm[:, e, 3:4], ps[:, b + 1, 0:256], AX_X, ALU.max, negate=True)
                    V.tensor_reduce(nm[:, e, 0:1], ps[:, b + 1, 256:384], AX_X, ALU.max, negate=True).then_inc(s_nm, 1)
                    dve.wait_ge(s_nm, 2 * j + e + 1)
                    V.tensor_scalar(nm[:, e, :], nm[:, e, :], nsink[:, bass.ds(2 * j + e, 1)], None,
                                    ALU.min).then_inc(s_nms, 1)
                    dve.wait_ge(s_nms, 2 * j + e + 1)
                    after(dve, s_st, 2 * j - 1 + e)
                    V.tensor_tensor(sdiag[:, e, :].rearrange("p (b n) -> p b n", b=TB),
                                    ident[:, None, :].to_broadcast([P, TB, P]),
                                    nm[:, e, :, None].to_broadcast([P, TB, P]), ALU.mult).then_inc(s_diag, 1)

            def swa_out(j):
                for e in range(2):
                    dve.wait_ge(s_o, 2 * j + e + 1)
                    own, other = slice(64 * e, 64 * e + 64), slice(64 - 64 * e, 128 - 64 * e)
                    V.tensor_tensor(qkn[own, 1, :], ps[other, 6 + e, :], psink[e][other, :], ALU.add).then_inc(s_den, 1)
                dve.wait_ge(s_den, 2 * j + 2)
                V.reciprocal(qkn[:, 1, :], qkn[:, 1, :]).then_inc(s_rec, 1)
                dve.wait_ge(s_rec, j + 1)
                for e in range(2):
                    own = slice(64 * e, 64 * e + 64)
                    V.tensor_tensor(o_t[own, j, :], ps[own, 6 + e, :], qkn[own, 1, :], ALU.mult).then_inc(s_ot, 1)

            for j in range(PAIRS - 1):
                swa_max(j)
                swa_norm(j + 2, q_raw[:, (j + 1) % 2, :], qkn[:, 0, :], 2)
                if j + 2 < PAIRS:
                    swa_query_raw(j + 2)
                swa_lo(j + 1)
                swa_out(j)
            for c in range(2):
                out_lo(1, FILL_OUT_B, c)
            swa_max(7)
            for c in range(2, KC - 1):
                out_lo(1, FILL_OUT_B, c)
            swa_out(7)
            out_lo(1, FILL_OUT_B, KC - 1)
            add_out(1, 3, FILL_MLP1)
            mlp_up(2)
            mlp_down(2)
            mlp_up(3)
            for n in range(KC):
                dve.wait_ge(w_used, U_DOWN[3] + n + 1)
                after(dve, fin_turned, n - 1)
                V.tensor_tensor(qkn[:, n % 2, :], hT[:, n, :], ps[:, 4 + n % 2, :], ALU.add).then_inc(fin_ready, 1)

        @block.tensor
        def _(pe):
            mm = nc.tensor.matmul

            def three(out_, s_hi, s_lo, m_hi, m_lo, start, stop):
                mm(out_, s_hi, m_hi, start=start, stop=False)
                mm(out_, s_hi, m_lo, start=False, stop=False)
                return mm(out_, s_lo, m_hi, start=False, stop=stop)

            pe.wait_ge(consts_landed, 16)
            for b in range(TB):
                pe.wait_ge(x_landed[b], 16)
            for c in range(KC):
                after(pe, h_written, c - 3)
                for b in range(TB):
                    ins = nc.tensor.transpose(ps[:, c % 4, b * P:(b + 1) * P], x_in[:, b, c * P:(c + 1) * P], ident)
                ins.then_inc(x_turned, 1)
            pe.wait_ge(small_landed, 16 * 15)
            nc.tensor.transpose(ps[:, 6, 0:44], g_in[:], ident[0:44, 0:44]).then_inc(gains_t, 1)

            def norm_sum(q):
                pe.wait_ge(acc_added, 9 * q + 9)
                mm(ps[:, 7, :], ones_d, acc, start=True, stop=True).then_inc(sum_added, 1)

            norm_sum(0)

            pe.wait_ge(h_written, KC)
            for v in range(4):
                u = U_V + v
                s = u % 2
                pe.wait_ge(w_lo_ready, u + 1)
                after(pe, v_stored, v - 1)
                if v == 1:
                    pe.wait_ge(prep, 2)
                if v == 2:
                    pe.wait_ge(ctemp_landed, 16)
                    mm(ps[0:HEADS, 2, 0:384], rel[0:N_BUCKETS, :], ctemp[0:N_BUCKETS, C_HOT - C_TEMP:C_HOT - C_TEMP + 384],
                       start=True, stop=True).then_inc(ext_ps, 1)
                    pe.wait_ge(ext_ready, 1)
                wh = w_hi[:, s, :].rearrange("p (k n) -> p k n", k=KC)
                wl = w_lo[:, s, :].rearrange("p (k n) -> p k n", k=KC)
                for k in range(KC):
                    if v == 0:
                        pe.wait_ge(xn_ready, k + 1)
                    for b in range(TB):
                        o = ps[:, 4 * (v % 2) + b, 0:256]
                        xs = slice(b * P, (b + 1) * P)
                        ins = three(o, xn_hi[:, k, xs], xn_lo[:, k, xs], wh[:, k, :], wl[:, k, :], k == 0, k == KC - 1)
                ins.then_inc(w_used, 1)

            def chunk(bank, wh, wl, k_of, m_hi, m_lo, kc):
                for k in range(kc):
                    ins = three(ps[:, bank, :], k_of(wh, k), k_of(wl, k), m_hi[:, k, :], m_lo[:, k, :], k == 0, k == kc - 1)
                return ins

            pe.wait_ge(v_stored, 4)
            pe.wait_ge(wf_split, 2)
            chunk(6, wf_hi, wf_lo, lambda w, k: w[:, k, :], xn_hi, xn_lo, KC).then_inc(gate_ps, 1)

            def proj_pair(i, s, t):
                if t == 0:
                    pe.wait_ge(w_lo_ready, U_PAIR + i + 1)
                after(pe, f_refined, 4 * i - 3 + 2 * t)
                wh = w_hi[:, s, :].rearrange("p (t k n) -> p t k n", t=2, k=KC)
                wl = w_lo[:, s, :].rearrange("p (t k n) -> p t k n", t=2, k=KC)
                ins = chunk(t, wh[:, t], wl[:, t], lambda w, k: w[:, k, :], xn_hi, xn_lo, KC)
                ins.then_inc(w_used if t else f_proj, 1)

            def fox_sum(i, t):
                pe.wait_ge(f_sq, 2 * i + t + 1)
                mm(ps[:, t, :], blk, sqt[:, t, :], start=True, stop=True).then_inc(f_sum, 1)

            def fox_max_scores(j):
                tiles = [(e, tile) for e in range(2) for tile in ((3, 0, 0), (2, 1, 0), (0, 1, 384))]
                for e, (qb, bank, c0) in tiles + [(0, (1, 2, 0)), (1, (1, 2, 0))]:
                    if qb == 3:
                        pe.wait_ge(f_hi, 2 * j + e + 1)
                        pe.wait_ge(f_c, 2 * j + e + 1)
                    if bank == 2:
                        after(pe, f_ot, 2 * j - 1 + e)
                    n = (qb + 1) * P
                    bank = SCORE_BANKS[e][bank]
                    o = ps[:, bank, c0:c0 + n]
                    mm(o, qk_hi[:, 0, e, qb * P:(qb + 1) * P], qk_hi[:, 1, e, 0:n], start=True, stop=False)
                    ins = mm(ps[:, bank, c0 + qb * P:c0 + n], ident_r[:], maskA_r[:], start=False, stop=True)
                    if qb == 1:
                        ins.then_inc(f_sa, 1)

            def fox_scores(j, between=None):
                pe.wait_ge(f_lo, 2 * j + 2)
                for e in range(2):
                    if e == 1 and between is not None:
                        fox_sum(between, 1)
                    pe.wait_ge(f_diag, 2 * j + e + 1)
                    b0, b1, b2 = SCORE_BANKS[e]
                    h = slice(64 * e, 64 * e + 64)
                    for kb, bank, c0 in ((0, b0, 0), (1, b1, 0), (3, b1, 384), (2, b2, 0)):
                        n = (TB - kb) * P
                        o = ps[:, bank, c0:c0 + n]
                        ks, qs = slice(kb * P, (kb + 1) * P), slice(kb * P, T)
                        mm(o, qk_hi[:, 1, e, ks], qk_hi[:, 0, e, qs], start=True, stop=False)
                        mm(o, qk_hi[h, 1, e, ks], qk_lo[h, 0, qs], start=False, stop=False)
                        mm(o, qk_lo[h, 1, ks], qk_hi[h, 0, e, qs], start=False, stop=False)
                        mm(o, ones_r[:], diag[:, e, qs], start=False, stop=False)
                        ins = mm(ps[:, bank, c0:c0 + P], ident_r[:], maskT_r[:], start=False, stop=True)
                    ins.then_inc(f_st, 1)

            def fox_pv(j):
                pe.wait_ge(f_vx, j + 1)
                for e in range(2):
                    pe.wait_ge(f_p, 2 * j + e + 1)
                    for kb, src in ((0, 0), (1, 512), (2, 1024), (3, 896)):
                        n = (TB - kb) * P
                        ins = mm(ps[:, 4 + 3 * e, kb * P:T], vx[:, kb, HD * e:HD * e + P], pT[:, e, src:src + n],
                                 start=(kb == 0), stop=(kb == TB - 1))
                    ins.then_inc(f_o, 1)

            pe.wait_ge(f_ones, 1)
            proj_pair(0, 0, 0)
            fox_sum(0, 0)
            proj_pair(0, 0, 1)
            fox_sum(0, 1)

            def fox_step(i, s):
                proj_pair(i, s, 0)
                fox_max_scores(i - 1)
                fox_sum(i, 0)
                proj_pair(i, s, 1)
                fox_scores(i - 1, i)
                fox_pv(i - 1)

            fox_step(1, 1)
            with pe.Fori(1, 4) as t:
                fox_step(2 * t, 0)
                fox_step(2 * t + 1, 1)
            def unit_d(u, s, banks, fill=None, k_waits=False, m=(xn_hi, xn_lo)):
                pe.wait_ge(w_lo_ready, u + 1)
                wh = w_hi[:, s, :].rearrange("p (k n) -> p k n", k=KC)
                wl = w_lo[:, s, :].rearrange("p (k n) -> p k n", k=KC)
                for k in range(KC):
                    if k_waits:
                        pe.wait_ge(xn_ready, KC * fill + k + 1)
                    for n in range(2):
                        ins = three(ps[:, banks + n, :], wh[:, k, n * P:(n + 1) * P], wl[:, k, n * P:(n + 1) * P],
                                    m[0][:, k, :], m[1][:, k, :], k == 0, k == KC - 1)
                ins.then_inc(w_used, 1)

            def out_piece(which, fill, ks):
                u = U_OUT[which]
                if ks[0] == 0:
                    pe.wait_ge(w_lo_ready, u + 1)
                wh = w_hi[:, u % 2, :].rearrange("p (k n) -> p k n", k=KC)
                wl = w_lo[:, u % 2, :].rearrange("p (k n) -> p k n", k=KC)
                for k in ks:
                    pe.wait_ge(xn_ready, KC * fill + k + 1)
                    for n in range(2):
                        ins = three(ps[:, n, :], wh[:, k, n * P:(n + 1) * P], wl[:, k, n * P:(n + 1) * P],
                                    o_hi[which][:, k, :], o_lo[which][:, k, :], k == 0, k == KC - 1)
                if ks[-1] == KC - 1:
                    ins.then_inc(w_used, 1)

            def last_pair(which, fill, max_scores, scores, pv):
                max_scores(PAIRS - 1)
                out_piece(which, fill, (0, 1))
                scores(PAIRS - 1)
                pv(PAIRS - 1)
                out_piece(which, fill, range(2, KC))

            def proj_out(which):
                h_base = [8, 32][which]
                u = U_OUT[which]
                m = (o_hi[which], o_lo[which])
                unit_d(u + 1, (u + 1) % 2, 2, m=m)
                for j in range(2, 4):
                    pe.wait_ge(h_written, h_base + 2 * (j - 1))
                    unit_d(u + j, (u + j) % 2, 2 * (j % 2), m=m)

            def mlp_up(d, fill, k_waits, q=None):
                u = U_UP[d]
                pe.wait_ge(h_written, [14, 24, 38, 48][d])
                unit_d(u, u % 2, 0, fill, k_waits)
                if q is not None:
                    norm_sum(q)
                    pe.wait_ge(h_written, 8 * FILL_MLP0 if d == 0 else 40)
                unit_d(u + 1, (u + 1) % 2, 2)
                with pe.Fori(1, 4) as t:
                    for j in range(2):
                        pe.wait_ge(u_ready, 8 * d + 2 * t + j - 1)
                        unit_d(u + j + 2 * t, (u + j) % 2, 2 * j)

            def down_unit(u, s, bank, d=None):
                pe.wait_ge(w_lo_ready, u + 1)
                wh = w_hi[:, s, :].rearrange("p (k n) -> p k n", k=FH)
                wl = w_lo[:, s, :].rearrange("p (k n) -> p k n", k=FH)
                for k in range(FH):
                    if d is not None and k % 2 == 0:
                        pe.wait_ge(r_ready, 8 * d + k // 2 + 1)
                    ins = three(ps[:, bank, :], wh[:, k, :], wl[:, k, :], r_hi[:, k, :], r_lo[:, k, :],
                                k == 0, k == FH - 1)
                ins.then_inc(w_used, 1)

            H_BASE = [16, 24, 40, 48]

            def mlp_down(d):
                u = U_DOWN[d]
                pe.wait_ge(h_written, H_BASE[d])
                down_unit(u, u % 2, 4, d)
                down_unit(u + 1, (u + 1) % 2, 5)
                with pe.Fori(1, 4) as t:
                    for j in range(2):
                        pe.wait_ge(h_written, H_BASE[d] + 2 * t + j - 1)
                        down_unit(u + j + 2 * t, (u + j) % 2, 4 + j)

            last_pair(0, FILL_OUT_A, fox_max_scores, fox_scores, fox_pv)
            proj_out(0)
            mlp_up(0, FILL_MLP0, True, 1)
            mlp_down(0)
            mlp_up(1, FILL_MLP0, False)
            mlp_down(1)

            s = U_KV % 2
            pe.wait_ge(w_lo_ready, U_KV + 1)
            wh = w_hi[:, s, :].rearrange("p (k n) -> p k n", k=KC)
            wl = w_lo[:, s, :].rearrange("p (k n) -> p k n", k=KC)
            for k in range(KC):
                if k == 4:
                    norm_sum(2)
                pe.wait_ge(xn_ready, KC * FILL_KV + k + 1)
                three(ps[:, 1, :], wh[:, k, 0:P], wl[:, k, 0:P], xn_hi[:, k, :], xn_lo[:, k, :], k == 0, k == KC - 1)
                for b in range(TB):
                    xs = slice(b * P, (b + 1) * P)
                    ins = three(ps[:, 2, xs], xn_hi[:, k, xs], xn_lo[:, k, xs], wh[:, k, P:2 * P],
                                wl[:, k, P:2 * P], k == 0 and b == 0, k == KC - 1 and b == TB - 1)
                ins.then_inc(s_kv if k < KC - 1 else w_used, 1)
            pe.wait_ge(n_refined, 6)
            for b in range(TB):
                ins = mm(ps[:, 6, b:b + 1], rst[:, 0, b * P:(b + 1) * P], ident[:, 0:1], start=True, stop=True)
            ins.then_inc(s_vps, 1)

            def swa_proj(i, k_waits=False, sum_at_2=None):
                v, n = i // 2, i % 2
                u = U_Q + v
                s = u % 2
                if n == 0:
                    pe.wait_ge(w_lo_ready, u + 1)
                after(pe, s_raw, i + 1 if i else 0)
                wh = w_hi[:, s, :].rearrange("p (k n) -> p k n", k=KC)
                wl = w_lo[:, s, :].rearrange("p (k n) -> p k n", k=KC)
                for k in range(KC):
                    if k_waits:
                        pe.wait_ge(xn_ready, KC * FILL_Q + k + 1)
                    if k == 2 and sum_at_2 is not None:
                        swa_sum(sum_at_2)
                    ins = three(ps[:, 0, :], wh[:, k, n * P:(n + 1) * P], wl[:, k, n * P:(n + 1) * P],
                                xn_hi[:, k, :], xn_lo[:, k, :], k == 0, k == KC - 1)
                ins.then_inc(w_used if n else s_q, 1)

            def swa_sum(m):
                pe.wait_ge(s_sq, m + 1)
                if m == 0:
                    pe.wait_ge(s_raw, 1)
                after(pe, s_refined, 2 * m - 1)
                mm(ps[:, 1, :], blk, sqt[:, 0, :], start=True, stop=True).then_inc(s_sum, 1)

            def swa_max_scores(j):
                g = j // (PAIRS // 2)
                pe.wait_ge(s_hi, j + 2)
                for e in range(2):
                    b = 2 + 2 * e
                    h = slice(64 * e, 64 * e + 64)
                    bias = hk_hi[:, 2 * j + e, :]
                    for qb, bank, c0 in ((1, b, 0), (2, b, 256), (3, b + 1, 0), (0, b + 1, 256)):
                        n = 2 * P if qb else P
                        k0 = max(qb - 1, 0) * P
                        mm(ps[:, bank, c0:c0 + n], sq_hi[h, qb * P:(qb + 1) * P], kd_hi[h, g, k0:k0 + n],
                           start=True, stop=False)
                        if qb:
                            mm(ps[:, bank, c0:c0 + P], bias[:, P:2 * P], anti_r[:], start=False, stop=False)
                        ins = mm(ps[:, bank, c0 + n - P:c0 + n], bias[:, 0:P], anti_r[:], start=False, stop=True)
                    ins.then_inc(s_sa, 1)

            def swa_scores(j):
                g = j // (PAIRS // 2)
                pe.wait_ge(s_lo, j + 2)
                for e in range(2):
                    pe.wait_ge(s_diag, 2 * j + e + 1)
                    after(pe, s_ot, 2 * j - 1 + e)
                    b = 2 + 2 * e
                    h = slice(64 * e, 64 * e + 64)
                    mm(ps[:, 6 + e, :], ones_r[:], sdiag[:, e, :], start=True, stop=True)
                    for kb, bank, c0 in ((0, b, 0), (1, b, 256), (2, b + 1, 0), (3, b + 1, 256)):
                        n = 2 * P if kb < TB - 1 else P
                        o = ps[:, bank, c0:c0 + n]
                        ks, qs = slice(kb * P, (kb + 1) * P), slice(kb * P, kb * P + n)
                        mm(o, kd_hi[h, g, ks], sq_hi[h, qs], start=True, stop=False)
                        mm(o, kd_hi[h, g, ks], sq_lo[h, qs], start=False, stop=False)
                        mm(o, kd_lo[h, g, ks], sq_hi[h, qs], start=False, stop=False)
                        mm(o, ones_r[:], sdiag[:, e, qs], start=False, stop=False)
                        mm(o, anti_r[:], hk_lo[:, 2 * j + e, 0:n], start=False, stop=False)
                        ins = mm(o, anti_r[:], hk_hi[:, 2 * j + e, 0:n], start=False, stop=True)
                    ins.then_inc(s_st, 1)

            def swa_pv(j):
                g = j // (PAIRS // 2)
                for e in range(2):
                    pe.wait_ge(s_p, 2 * j + e + 1)
                    for qb in range(TB):
                        for kb in range(max(qb - 1, 0), qb + 1):
                            src = 256 * kb + P * (qb - kb)
                            ins = mm(ps[:, 6 + e, qb * P:(qb + 1) * P], svx[:, g, kb, HD * e:HD * e + P],
                                     sp_[:, e, src:src + P], start=(kb == max(qb - 1, 0)), stop=(kb == qb))
                    ins.then_inc(s_o, 1)

            swa_proj(0, True, 0)
            swa_proj(1, False, 1)
            pe.wait_ge(s_v, 2)
            pe.wait_ge(s_hank_read, 1)
            for j in range(PAIRS - 1):
                swa_max_scores(j)
                swa_sum(j + 2)
                if j + 2 < PAIRS:
                    swa_proj(j + 2)
                swa_scores(j)
                swa_pv(j)
            last_pair(1, FILL_OUT_B, swa_max_scores, swa_scores, swa_pv)
            proj_out(1)
            mlp_up(2, FILL_MLP1, True, 3)
            mlp_down(2)
            mlp_up(3, FILL_MLP1, False)
            pe.wait_ge(h_written, H_BASE[3])

            def turn_out(n):
                pe.wait_ge(fin_ready, n + 1)
                after(pe, out_copied, n - 1)
                for b in range(TB):
                    ins = nc.tensor.transpose(ps[:, 6 + n % 2, b * P:(b + 1) * P], qkn[:, n % 2, b * P:(b + 1) * P], ident)
                ins.then_inc(fin_turned, 1)

            for n in range(KC):
                after(pe, fin_ready, n - 1)
                down_unit(U_DOWN[3] + n, (U_DOWN[3] + n) % 2, 4 + n % 2, 3 if n == 0 else None)
                if n >= 1:
                    turn_out(n - 1)
            turn_out(KC - 1)


_INS = ["x", "g_attn", "g_mlp", "w_in_a", "b_f", "gq_a", "gk_a", "w_out_a", "g_kv", "w_kv", "gk_b",
        "w_q_b", "gq_b", "sinks", "rel_bias", "w_out_b", "w_up", "w_down"]


def kernel(**inputs):
    import numpy as _np
    import concourse.bacc as _bacc
    from concourse import mybir as _mybir
    from concourse.bass_utils import run_bass_kernel_spmd as _run

    nc = _bacc.Bacc("TRN2", target_bir_lowering=False, num_devices=1)
    arrays, args = {}, []
    for name in _INS + ["shape_consts"]:
        a = shape_constants() if name == "shape_consts" else _np.ascontiguousarray(inputs[name])
        arrays[f"in_{name}"] = a
        args.append(nc.dram_tensor(f"in_{name}", a.shape, _mybir.dt.from_np(a.dtype), kind="ExternalInput").ap())
    out = nc.dram_tensor("out", (1, T, D), _mybir.dt.float32, kind="ExternalOutput").ap()
    build(nc, *args, out)
    r = _run(nc, [arrays], core_ids=[0])
    return r.results[0]["out"]
```

```python
from contextlib import ExitStack

import numpy as np

import concourse.bass as bass
from concourse import mybir

ALU = mybir.AluOpType
ACT = mybir.ActivationFunctionType
F32 = mybir.dt.float32
F32R = mybir.dt.float32r
AX_X = mybir.AxisListType.X

P = 128
D = 1024
T = 512
HD = 64
HEADS = 16
PAIRS = HEADS // 2
F = 4 * D
KC = D // P
TB = T // P
FH = F // 2 // P
WINDOW = 128
N_BUCKETS = 32
REL_MAX_DIST = 128
EPS = 1e-6
NEG = -1e30
UNIT = 2048

U_V = 0
U_PAIR = 4
U_OUT = [12, 53]
U_UP = [16, 32, 57, 73]
U_DOWN = [24, 40, 65, 81]
U_KV = 48
U_Q = 49
N_UNITS = 89

FILL_V, FILL_ATTN0, FILL_OUT_A, FILL_MLP0, FILL_KV, FILL_Q, FILL_OUT_B, FILL_MLP1 = range(8)
GAIN = {FILL_V: 0, FILL_ATTN0: 0, FILL_Q: 1, FILL_MLP0: 2, FILL_MLP1: 3, FILL_KV: 4}

C_IDENT, C_BLK, C_OND = 0, 128, 256
C_TEMP = 384
C_ANTI, C_ONES, C_MASKA, C_MASKT, C_HOT, C_NEG = 384, 512, 640, 768, 896, 1280
C_ALL = 1664


def shape_constants():
    c = np.zeros((P, C_ALL), np.float32)
    c[:, C_IDENT:C_IDENT + P] = np.eye(P)
    for b in range(2):
        c[64 * b:64 * b + 64, C_BLK + 64 * b:C_BLK + 64 * b + 64] = 1.0 / HD
    c[:, C_OND:C_OND + P] = 1.0 / D
    c[:, C_ANTI:C_ANTI + P] = np.eye(P)[::-1]
    c[:, C_ONES:C_ONES + P] = 1.0
    r = np.arange(P)
    c[:, C_MASKA:C_MASKA + P] = np.where(r[None, :] > r[:, None], NEG, 0.0)
    c[:, C_MASKT:C_MASKT + P] = np.where(r[:, None] > r[None, :], NEG, 0.0)
    d = np.arange(WINDOW)
    exact = N_BUCKETS // 2
    large = exact + (np.log(np.maximum(d, 1) / exact) / np.log(REL_MAX_DIST / exact)
                     * (N_BUCKETS - exact)).astype(np.int32)
    bucket = np.where(d < exact, d, np.minimum(large, N_BUCKETS - 1))
    c[:, C_NEG:C_NEG + 384] = NEG
    for dist in range(WINDOW):
        c[bucket[dist], C_HOT + 127 + dist] = 1.0
        c[:, C_NEG + 127 + dist] = 0.0
    return c


def build(nc, x, g_attn, g_mlp, w_in_a, b_f, gq_a, gk_a, w_out_a, g_kv, w_kv, gk_b,
          w_q_b, gq_b, sinks, rel_bias, w_out_b, w_up, w_down, consts, out):
    with ExitStack() as ctx:
        base = nc.sbuf_base
        room = (nc.sbuf_bytes_remaining // 32) * 32
        ctx.enter_context(nc.sbuf_tensor("arena", [P, room // 4 - 8], F32))
        cursor = [(base + 31) // 32 * 32]
        limit = base + room - 32

        def at(name, shape, dt, offset):
            assert offset + 4 * int(np.prod(shape[1:])) <= limit, (name, offset, limit)
            return nc.alloc_sbuf_tensor_at(name, shape, dt, offset=offset)

        def sb(name, shape, dt=F32):
            t = at(name, shape, dt, cursor[0])
            cursor[0] += (4 * int(np.prod(shape[1:])) + 31) // 32 * 32
            return t

        def sem(name):
            return ctx.enter_context(nc.semaphore(name))

        hT = sb("hT", [P, KC, T])
        xn_hi = sb("xn_hi", [P, KC, T], F32R)
        xn_lo = sb("xn_lo", [P, KC, T], F32R)
        stage = sb("stage", [P, 2, UNIT])
        w_hi = sb("w_hi", [P, 2, UNIT], F32R)
        w_lo = sb("w_lo", [P, 2, UNIT], F32R)
        sq_off = cursor[0]
        sqt = sb("sqt", [P, 2, T])
        rst_off = cursor[0]
        rst = sb("rst", [P, 2, T])
        acc = rst[:, 1, :]
        qkn = sb("qkn", [P, 2, T])
        kept = sb("kept", [P, C_TEMP])
        ident_r = sb("ident_r", [P, P], F32R)
        blk_r = sb("blk_r", [P, P], F32R)
        ones_r = sb("ones_r", [P, P], F32R)
        anti_r = sb("anti_r", [P, P], F32R)
        maskA_r = sb("maskA_r", [P, P], F32R)
        maskT_r = sb("maskT_r", [P, P], F32R)
        gains = sb("gains", [P, 44])
        half_gains = sb("half_gains", [P, 4])
        bf = sb("bf", [P, 1])
        sinkb = sb("sinkb", [P, HEADS])
        nsink = sb("nsink", [P, HEADS])
        nm = sb("nm", [P, 2, TB])
        rel = sb("rel", [P, HEADS])
        v_rst = sb("v_rst", [P, TB])
        area = cursor[0]
        KB = 1024

        o_t = at("o_t", [P, KC, T], F32, area + 78 * KB)
        hank = at("hank", [P, HEADS, 2 * WINDOW], F32, area + 78 * KB)
        x_hat = at("x_hat", [P, KC, T], F32, area + 30 * KB)
        o_hi = [at("oa_hi", [P, KC, T], F32R, area), at("ob_hi", [P, KC, T], F32R, area)]
        o_lo = [at("oa_lo", [P, KC, T], F32R, area + 54 * KB), at("ob_lo", [P, KC, T], F32R, area + 16 * KB)]
        r_hi = at("r_hi", [P, FH, T], F32R, area)
        r_lo = at("r_lo", [P, FH, T], F32R, area + 32 * KB)
        out_sb = at("out_sb", [P, 2, TB, P], F32, area + 64 * KB)
        x_in = at("x_in", [P, TB, D], F32, area)
        ctemp = at("ctemp", [P, C_ALL - C_TEMP], F32, area + 16 * KB)
        g_in = at("g_in", [16, P], F32, area + 25 * KB)
        g_in2 = at("g_in2", [28, P], F32, area + 26 * KB)
        ext_sb = at("ext_sb", [HEADS, 384], F32, area + 46 * KB)
        v_all = at("v_all", [P, PAIRS, TB, P], F32, area)
        pT = at("pT", [P, 2, 1280], F32, area + 16 * KB)
        vx = at("vx", [P, TB, 192], F32, area + 27 * KB)
        qk_hi = at("qk_hi", [P, 2, 2, T], F32R, area + 30 * KB)
        qk_x = at("qk_x", [P, 2, 2, T], F32R, area + 38 * KB)
        c_split = at("c_split", [64, T], F32R, area + 74 * KB)
        pick = at("pick", [64, HEADS], F32, area + 76 * KB)
        ct = at("ct", [P, 4, T], F32, area + 46 * KB)
        diag = at("diag", [P, 2, T], F32R, area + 46 * KB)
        raw = at("raw", [P, 2, T], F32, area + 70 * KB)
        fox_sq_hi = at("fox_sq_hi", [P, T], F32R, area + 66 * KB)
        fox_sq_lo = at("fox_sq_lo", [P, T], F32R, area + 68 * KB)
        wf = at("wf", [P, KC, P], F32, area + 54 * KB)
        wf_hi = at("wf_hi", [P, KC, P], F32R, area + 58 * KB)
        wf_lo = at("wf_lo", [P, KC, P], F32R, area + 62 * KB)
        hk_hi = at("hk_hi", [P, HEADS, 2 * WINDOW], F32R, area)
        hk_lo = at("hk_lo", [P, HEADS, 2 * WINDOW], F32R, area + 16 * KB)
        v_t = at("v_t", [P, T], F32, area + 44 * KB)
        q_rst = at("q_rst", [P, T], F32, area + 32 * KB)
        swa_sq_hi = at("swa_sq_hi", [P, T], F32R, area + 40 * KB)
        swa_sq_lo = at("swa_sq_lo", [P, T], F32R, area + 42 * KB)
        q_rec = at("q_rec", [P, T], F32, area + 38 * KB)
        q_raw = at("q_raw", [P, 2, T], F32, area + 34 * KB)
        swa_p = at("swa_p", [P, 2, 896], F32, area + 48 * KB)
        swa_vx = at("swa_vx", [P, 2, TB, 192], F32, area + 55 * KB)
        q_hl = at("q_hl", [P, 2, T], F32R, area + 61 * KB)
        kd_hi = at("kd_hi", [P, 2, T], F32R, area + 65 * KB)
        kd_lo = at("kd_lo", [P, 2, T], F32R, area + 69 * KB)
        swa_diag = at("swa_diag", [P, 2, T], F32R, area + 73 * KB)
        psink = [at("psink0", [P, T], F32, sq_off + 2 * KB), at("psink1", [P, T], F32, rst_off + 2 * KB)]

        ident = kept[:, C_IDENT:C_IDENT + P]
        blk = kept[:, C_BLK:C_BLK + P]
        ones_d = kept[:, C_OND:C_OND + P]

        ps = ctx.enter_context(nc.psum_tensor("ps", [P, 8, T], F32))
        ext = nc.dram_tensor("ext", [HEADS, 384], F32, kind="Internal").ap()

        x_landed = [sem(f"x_landed{b}") for b in range(TB)]
        consts_landed = sem("consts_landed")
        ctemp_landed = sem("ctemp_landed")
        gain_landed = sem("gain_landed")
        small_landed = sem("small_landed")
        landed = [sem("landed0"), sem("landed1")]
        w_hi_ready = sem("w_hi_ready")
        w_lo_ready = sem("w_lo_ready")
        w_used = sem("w_used")
        constants_ready = sem("constants_ready")
        gains_turned = sem("gains_turned")
        bias_row_made = sem("bias_row_made")
        bias_row_ready = sem("bias_row_ready")
        bias_row_stored = sem("bias_row_stored")
        hank_landed = sem("hank_landed")
        x_turned = sem("x_turned")
        h_written = sem("h_written")
        norm_squared = sem("norm_squared")
        norm_accumulated = sem("norm_accumulated")
        norm_summed = sem("norm_summed")
        norm_refined = sem("norm_refined")
        norm_ln_step = sem("norm_ln_step")
        norm_rstd_ready = sem("norm_rstd_ready")
        xhat_ready = sem("xhat_ready")
        xn_hi_ready = sem("xn_hi_ready")
        xn_ready = sem("xn_ready")
        v_rstd_turned = sem("v_rstd_turned")
        v_rstd_ready = sem("v_rstd_ready")
        v_chunk_used = sem("v_chunk_used")
        v_stored = sem("v_stored")
        wf_zero = sem("wf_zero")
        wf_landed = sem("wf_landed")
        wf_split = sem("wf_split")
        gate_projected = sem("gate_projected")
        gate_scalar_step = sem("gate_scalar_step")
        gate_vector_step = sem("gate_vector_step")
        fox_squared = sem("fox_squared")
        fox_squares_split = sem("fox_squares_split")
        fox_summed = sem("fox_summed")
        fox_ln_step = sem("fox_ln_step")
        fox_rstd_ready = sem("fox_rstd_ready")
        fox_rstd_refined = sem("fox_rstd_refined")
        fox_q_projected = sem("fox_q_projected")
        fox_den_ready = sem("fox_den_ready")
        fox_normed = sem("fox_normed")
        fox_hi_ready = sem("fox_hi_ready")
        fox_lo_ready = sem("fox_lo_ready")
        fox_cross_ready = sem("fox_cross_ready")
        fox_c_ready = sem("fox_c_ready")
        fox_v_ready = sem("fox_v_ready")
        ones_ready = sem("ones_ready")
        fox_max_scores_done = sem("fox_max_scores_done")
        fox_max_ready = sem("fox_max_ready")
        fox_diag_ready = sem("fox_diag_ready")
        fox_scores_done = sem("fox_scores_done")
        fox_probs_ready = sem("fox_probs_ready")
        fox_out_done = sem("fox_out_done")
        fox_recip_step = sem("fox_recip_step")
        fox_recip_refined = sem("fox_recip_refined")
        fox_out_stored = sem("fox_out_stored")
        hankel_hi_ready = sem("hankel_hi_ready")
        hankel_lo_ready = sem("hankel_lo_ready")
        kv_chunk_used = sem("kv_chunk_used")
        swa_raw_ready = sem("swa_raw_ready")
        v_turned = sem("v_turned")
        v_t_ready = sem("v_t_ready")
        swa_squared = sem("swa_squared")
        swa_squares_split = sem("swa_squares_split")
        swa_summed = sem("swa_summed")
        swa_ln_step = sem("swa_ln_step")
        swa_rstd_ready = sem("swa_rstd_ready")
        swa_rstd_refined = sem("swa_rstd_refined")
        swa_normed = sem("swa_normed")
        swa_hi_ready = sem("swa_hi_ready")
        swa_lo_ready = sem("swa_lo_ready")
        swa_q_projected = sem("swa_q_projected")
        swa_max_scores_done = sem("swa_max_scores_done")
        swa_max_found = sem("swa_max_found")
        swa_max_ready = sem("swa_max_ready")
        swa_diag_ready = sem("swa_diag_ready")
        swa_scores_done = sem("swa_scores_done")
        swa_probs_ready = sem("swa_probs_ready")
        swa_out_done = sem("swa_out_done")
        swa_den_ready = sem("swa_den_ready")
        swa_recip_step = sem("swa_recip_step")
        swa_recip_refined = sem("swa_recip_refined")
        swa_v_ready = sem("swa_v_ready")
        swa_out_stored = sem("swa_out_stored")
        u_ready = sem("u_ready")
        r_made = sem("r_made")
        r_hi_ready = sem("r_hi_ready")
        r_lo_ready = sem("r_lo_ready")
        fin_ready = sem("fin_ready")
        fin_turned = sem("fin_turned")
        out_copied = sem("out_copied")
        out_stored = [sem("out_stored0"), sem("out_stored1")]

        def after(eng, s, count):
            if not (isinstance(count, int) and count <= 0):
                eng.wait_ge(s, count)

        SCORE_BANKS = ((2, 3, 4), (5, 6, 7))

        V_BANKS = (0, 2, 4, 0)
        Q_BANKS = (0, 4, 0, 0, 0, 0, 0, 0)

        block = ctx.enter_context(nc.Block())

        @block.sync
        def _(sp):
            def slot_free(u):
                after(sp, w_lo_ready, u - 1)

            def load(u, s, src, **shape):
                slot_free(u)
                dst = stage[:, s, :].rearrange("p (k n) -> p k n", **shape)
                sp.dma_start(dst, src).then_inc(landed[s], 16)

            sp.dma_start(kept[:], consts[:, 0:C_TEMP]).then_inc(consts_landed, 16)
            w_in = w_in_a[0].rearrange("(k p) n -> p k n", p=P)
            for v in range(4):
                if v == 2:
                    sp.dma_start(ctemp[:], consts[:, C_TEMP:C_ALL]).then_inc(ctemp_landed, 16)
                load(U_V + v, (U_V + v) % 2, w_in[:, :, 2 * D + 256 * v:2 * D + 256 * v + 256], k=KC)
                if v == 0:
                    for b in range(TB):
                        sp.dma_start(x_in[:, b, :], x[0, b * P:(b + 1) * P, :]).then_inc(x_landed[b], 16)
                if v == 1:
                    sp.dma_start(rel[0:N_BUCKETS, :], rel_bias).then_inc(small_landed, 16)
                    sp.dma_start(sinkb[:], sinks[0].partition_broadcast(P)).then_inc(small_landed, 16)
                    sp.dma_start(g_in2[0:16, :], g_mlp.rearrange("l (k p) -> (l k) p", p=P)).then_inc(small_landed, 16)
                    sp.dma_start(g_in2[16:24, :], g_kv.rearrange("(k p) -> k p", p=P)).then_inc(small_landed, 16)
                    for n, g in enumerate((gq_a[0], gk_a[0], gq_b[0], gk_b)):
                        sp.dma_start(g_in2[24 + n:25 + n, :].rearrange("o (t d) -> o t d", t=2),
                                     g[None, None, :].to_broadcast([1, 2, HD])).then_inc(small_landed, 16)
                    sp.wait_ge(wf_zero, 2)
                    sp.dma_start(bf[0:HEADS, :], b_f[0].rearrange("(h o) -> h o", o=1)).then_inc(wf_landed, 16)
                    sp.dma_start(wf[:, :, 0:HEADS], w_in[:, :, 3 * D:3 * D + HEADS]).then_inc(wf_landed, 16)

            def load_pair(i, s):
                slot_free(U_PAIR + i)
                dst = stage[:, s, :].rearrange("p (t k n) -> p t k n", t=2, k=KC)
                for t in range(2):
                    sp.dma_start(dst[:, t], w_in[:, :, bass.ds(i * P + t * D, P)]).then_inc(landed[s], 16)

            with sp.Fori(0, PAIRS // 2) as i:
                for j in range(2):
                    load_pair(2 * i + j, (U_PAIR + j) % 2)

            def load_out(which, w):
                src = w.rearrange("(k p) n -> p k n", p=P)
                with sp.Fori(0, 2) as i:
                    for j in range(2):
                        u = U_OUT[which] + j
                        load(u + 2 * i, u % 2, src[:, :, bass.ds(i * 512 + 256 * j, 256)], k=KC)

            def load_mlp(d):
                layer, half = d // 2, d % 2
                up = w_up[layer].rearrange("(k p) n -> p k n", p=P)
                with sp.Fori(0, 4) as i:
                    for j in range(2):
                        u = U_UP[d] + j
                        load(u + 2 * i, u % 2, up[:, :, bass.ds(i * 512 + 256 * j + half * (F // 2), 256)], k=KC)
                down = w_down[layer, half * (F // 2):(half + 1) * (F // 2), :].rearrange("(k p) n -> p k n", p=P)
                with sp.Fori(0, 4) as i:
                    for j in range(2):
                        u = U_DOWN[d] + j
                        load(u + 2 * i, u % 2, down[:, :, bass.ds(i * 256 + 128 * j, P)], k=FH)

            load_out(0, w_out_a[0])
            load_mlp(0)
            sp.wait_ge(xn_ready, KC * (FILL_OUT_A + 1))
            sp.wait_ge(bias_row_stored, 16)
            hank_src = bass.AP(ext.tensor, 0, [[1, P], [384, HEADS], [1, 2 * WINDOW]])
            sp.dma_start(hank[:], hank_src).then_inc(hank_landed, 16)
            load_mlp(1)
            load(U_KV, U_KV % 2, w_kv.rearrange("(k p) n -> p k n", p=P), k=KC)
            wq = w_q_b[0].rearrange("(k p) n -> p k n", p=P)
            for v in range(4):
                load(U_Q + v, (U_Q + v) % 2, wq[:, :, 256 * v:256 * v + 256], k=KC)
            load_out(1, w_out_b[0])
            load_mlp(2)
            load_mlp(3)
            dst = out[0].rearrange("(b p) n -> p b n", p=P)
            for n in range(KC):
                sp.wait_ge(out_copied, n + 1)
                sp.dma_start(dst[:, :, n * P:(n + 1) * P], out_sb[:, n % 2]).then_inc(out_stored[n % 2], 16)
            for s in range(2):
                sp.wait_ge(out_stored[s], 16 * KC // 2)

        @block.gpsimd
        def _(pool):
            nc.gpsimd.memset(wf[:], 0.0).then_inc(wf_zero, 1)

            def low(u, s):
                pool.wait_ge(w_hi_ready, u + 1)
                for q in range(4):
                    c = slice(q * UNIT // 4, (q + 1) * UNIT // 4)
                    ins = nc.gpsimd.tensor_tensor(w_lo[:, s, c], stage[:, s, c], w_hi[:, s, c].bitcast(F32),
                                                  ALU.subtract)
                ins.then_inc(w_lo_ready, 1)

            def low_squares(lo, hi, t, ready, count, split):
                pool.wait_ge(ready, count)
                nc.gpsimd.tensor_tensor(lo[:], sqt[:, t, :], hi[:].bitcast(F32), ALU.subtract).then_inc(split, 1)

            def fox_squares(i, t):
                low_squares(fox_sq_lo, fox_sq_hi, t, fox_squared, 2 * i + t + 1, fox_squares_split)

            with pool.Fori(0, U_PAIR // 2 + 1) as i:
                low(2 * i, 0)
                low(2 * i + 1, 1)
            def fox_step(i, s):
                fox_squares(i, 0)
                low(U_PAIR + i + 1, s)
                fox_squares(i, 1)

            fox_step(1, 0)
            with pool.Fori(1, PAIRS // 2) as t:
                fox_step(2 * t, 1)
                fox_step(2 * t + 1, 0)
            low(U_PAIR + PAIRS + 1, 1)
            with pool.Fori((U_PAIR + PAIRS + 2) // 2, (U_Q + 1) // 2) as i:
                low(2 * i, 0)
                low(2 * i + 1, 1)
            low(U_Q + 1, (U_Q + 1) % 2)
            pool.wait_ge(hankel_hi_ready, 1)
            for half in range(2):
                heads = slice(half * HEADS // 2, (half + 1) * HEADS // 2)
                nc.gpsimd.tensor_tensor(hk_lo[:, heads, :], hank[:, heads, :], hk_hi[:, heads, :].bitcast(F32),
                                        ALU.subtract).then_inc(hankel_lo_ready, 1)
                if half == 0:
                    low(U_Q + 2, (U_Q + 2) % 2)
            for j in range(PAIRS - 2):
                low_squares(swa_sq_lo, swa_sq_hi, 0, swa_squared, j + 4, swa_squares_split)
                if j % 2 == 1:
                    u = U_Q + 3 + j // 2
                    low(u, u % 2)
            u = U_Q + PAIRS // 2 + 2
            low(u, u % 2)
            assert (u + 1) % 2 == 0
            with pool.Fori((u + 1) // 2, N_UNITS // 2) as i:
                low(2 * i, 0)
                low(2 * i + 1, 1)
            low(N_UNITS - 1, 0)

        @block.scalar
        def _(act):
            def split(count, u, s):
                act.wait_ge(landed[s], 16 * count)
                after(act, w_used, u - 1)
                nc.scalar.activation(w_hi[:, s, :], stage[:, s, :], ACT.Copy).then_inc(w_hi_ready, 1)

            act.preload_act_table_set("natural_log_exp_and_others")
            act.dma_start(g_in[:], g_attn.rearrange("l (k p) -> (l k) p", p=P)).then_inc(gain_landed, 16)

            def norm_square(q, h_base, c, slot):
                act.wait_ge(h_written, h_base + c + 1)
                after(act, norm_accumulated, 9 * q + c if not (q == 0 and isinstance(c, int) and c < 2) else 0)
                src = hT[:, bass.ds(c, 1), :].rearrange("p a n -> p (a n)")
                nc.scalar.activation(sqt[:, slot, :], src, ACT.Square).then_inc(norm_squared, 1)

            def norm_rstd(q):
                act.wait_ge(norm_summed, q + 1)
                nc.scalar.activation(rst[:, 0, :], ps[:, 7, :], ACT.Ln, bias=EPS).then_inc(norm_ln_step, 1)
                act.wait_ge(norm_ln_step, 2 * q + 1)
                nc.scalar.activation(rst[:, 0, :], rst[:, 0, :], ACT.Exp, scale=-0.5).then_inc(norm_ln_step, 1)
                act.wait_ge(norm_ln_step, 2 * q + 2)
                nc.scalar.activation(sqt[:, 0, :], rst[:, 0, :], ACT.Square).then_inc(norm_rstd_ready, 1)

            def fill_hi():
                for c in range(KC):
                    act.wait_ge(xhat_ready, c + 1)
                    if c < KC - 1:
                        act.wait_ge(v_chunk_used, c + 1)
                    else:
                        act.wait_ge(w_used, U_V + 4)
                    nc.scalar.activation(xn_hi[:, c, :], x_hat[:, c, :], ACT.Identity,
                                         scale=gains[:, c:c + 1]).then_inc(xn_hi_ready, 1)

            def h_hi(fill, h_base, c):
                act.wait_ge(h_written, h_base + c + 1)
                src = hT[:, bass.ds(c, 1), :].rearrange("p a n -> p (a n)")
                dst = xn_hi[:, bass.ds(c, 1), :].rearrange("p a n -> p (a n)")
                nc.scalar.activation(dst, src, ACT.Identity,
                                     scale=gains[:, bass.ds(8 * GAIN[fill] + c, 1)]).then_inc(xn_hi_ready, 1)

            split(1, 0, 0)
            act.wait_ge(constants_ready, 1)
            for c in range(KC):
                h_hi(FILL_V, 0, c)
                if 2 <= c < 6:
                    if c == 2:
                        act.wait_ge(landed[1], 16)
                    quarter = slice((c - 2) * UNIT // 4, (c - 1) * UNIT // 4)
                    ins = nc.scalar.activation(w_hi[:, 1, quarter], stage[:, 1, quarter], ACT.Copy)
                    if c == 5:
                        ins.then_inc(w_hi_ready, 1)
            for c in range(KC):
                norm_square(0, 0, c, c % 2)
                if c == 3:
                    split(2, 2, 0)
            norm_rstd(0)
            split(2, 3, 1)
            act.wait_ge(bias_row_ready, 1)
            act.dma_start(ext, ext_sb[:]).then_inc(bias_row_stored, 16)
            split(2 + 2, 4, 0)
            fill_hi()
            split(2 + 2, 5, 1)

            act.wait_ge(gate_projected, 1)
            act.wait_ge(bias_row_stored, 16)
            nc.scalar.activation(ct[:, 0, :], ps[:, 6, :], ACT.Identity, bias=bf[:, 0:1]).then_inc(gate_scalar_step, 1)
            act.wait_ge(gate_scalar_step, 1)
            nc.scalar.activation(ct[:, 1, :], ct[:, 0, :], ACT.Abs).then_inc(gate_scalar_step, 1)
            act.wait_ge(gate_scalar_step, 2)
            nc.scalar.activation(ct[:, 1, :], ct[:, 1, :], ACT.Exp, scale=-1.0).then_inc(gate_scalar_step, 1)
            act.wait_ge(gate_scalar_step, 3)
            nc.scalar.activation(ct[:, 1, :], ct[:, 1, :], ACT.Ln, bias=1.0).then_inc(gate_scalar_step, 1)

            def fox_square(i, t):
                if t == 0:
                    act.wait_ge(fox_q_projected, i + 1)
                else:
                    act.wait_ge(w_used, U_PAIR + i + 1)
                after(act, fox_normed, 2 * i - 1 + t)
                nc.scalar.activation(raw[:, t, :], ps[:, t, :], ACT.Copy)
                ins = nc.scalar.activation(sqt[:, t, :], ps[:, t, :], ACT.Square)
                if not (isinstance(i, int) and i == 0):
                    after(act, fox_summed, 2 * i + t)
                    ins = nc.scalar.activation(fox_sq_hi[:], ps[:, t, :], ACT.Square)
                ins.then_inc(fox_squared, 1)

            def fox_rstd(i, t):
                act.wait_ge(fox_summed, 2 * i + t + 1)
                nc.scalar.activation(rst[:, t, :], ps[:, t, :], ACT.Ln, bias=EPS).then_inc(fox_ln_step, 1)
                act.wait_ge(fox_ln_step, 4 * i + 2 * t + 1)
                nc.scalar.activation(rst[:, t, :], rst[:, t, :], ACT.Exp, scale=-0.5).then_inc(fox_ln_step, 1)
                act.wait_ge(fox_ln_step, 4 * i + 2 * t + 2)
                nc.scalar.activation(sqt[:, t, :], rst[:, t, :], ACT.Square).then_inc(fox_rstd_ready, 1)

            def fox_hi(i):
                act.wait_ge(fox_normed, 2 * i + 2)
                for e in range(2):
                    after(act, fox_scores_done, 2 * i - 1 + e)
                    own = slice(64 * e, 64 * e + 64)
                    nc.scalar.activation(qk_hi[own, :, e, :], qkn[own], ACT.Copy).then_inc(fox_hi_ready, 1)

            def fox_cross(i):
                for e in range(2):
                    own, other = slice(64 * e, 64 * e + 64), slice(64 - 64 * e, 128 - 64 * e)
                    nc.scalar.activation(qk_x[own, 0, e, :], qkn[own, 0, :], ACT.Copy)
                    nc.scalar.activation(qk_x[other, 1, e, :], qkn[own, 1, :], ACT.Copy).then_inc(fox_cross_ready, 1)

            def fox_exp(j, e):
                act.wait_ge(fox_scores_done, 2 * j + e + 1)
                after(act, fox_out_done, 2 * j - 1 + e)
                b0, b1, b2 = SCORE_BANKS[e]
                for bank, n, dst in ((b0, 512, 0), (b1, 512, 512), (b2, 256, 1024)):
                    ins = nc.scalar.activation(pT[:, e, dst:dst + n], ps[:, bank, 0:n], ACT.Exp)
                ins.then_inc(fox_probs_ready, 1)

            for t in range(2):
                fox_square(0, t)
                fox_rstd(0, t)
            fox_hi(0)

            def reciprocal(dst, den, done, n):
                nc.scalar.activation(dst, den, ACT.Ln).then_inc(done, 1)
                act.wait_ge(done, 2 * n + 1)
                nc.scalar.activation(dst, dst, ACT.Exp, scale=-1.0).then_inc(done, 1)

            def fox_den(j):
                for e in range(2):
                    act.wait_ge(fox_out_done, 2 * j + e + 1)
                    own, other = slice(64 * e, 64 * e + 64), slice(64 - 64 * e, 128 - 64 * e)
                    after(act, fox_out_stored, 2 * j)
                    ins = nc.scalar.activation(ct[own, 3, :], ps[other, 4 + 3 * e, :], ACT.Copy)
                ins.then_inc(fox_den_ready, 1)
                act.wait_ge(fox_den_ready, j + 1)
                reciprocal(ct[:, 2, :], ct[:, 3, :], fox_recip_step, j)

            def fox_step(i, landed_count, s):
                fox_square(i, 0)
                split(landed_count, U_PAIR + i + 1, s)
                if isinstance(i, int) and i == 1:
                    fox_cross(0)
                fox_rstd(i, 0)
                if isinstance(i, int) and i == 7:
                    for c in range(5):
                        out_hi(0, fox_out_stored, c)
                fox_square(i, 1)
                fox_exp(i - 1, 0)
                fox_exp(i - 1, 1)
                fox_rstd(i, 1)
                fox_den(i - 1)
                fox_hi(i)
                fox_cross(i)

            def out_hi(which, ready, c):
                act.wait_ge(ready, 2 * c + 2)
                nc.scalar.activation(o_hi[which][:, c, :], o_t[:, c, :], ACT.Copy).then_inc(xn_hi_ready, 1)

            fox_step(1, 2 + 4, 0)
            with act.Fori(1, 3) as t:
                fox_step(2 * t, 2 + 2 + 2 * t, 1)
                fox_step(2 * t + 1, 2 + 4 + 2 * t, 0)
            fox_step(6, 2 + 8, 1)
            fox_step(7, 2 + 8 + 1, 0)
            split(2 + 8 + 1, U_PAIR + 9, 1)
            SLOT = 5

            def split_units(u0, n):
                with act.Fori(0, n // 2) as t:
                    for j in range(2):
                        u = u0 + j
                        split(u // 2 + SLOT + t, u + 2 * t, u % 2)

            fox_exp(7, 0)
            out_hi(0, fox_out_stored, 5)
            fox_exp(7, 1)
            out_hi(0, fox_out_stored, 6)
            fox_den(7)
            act.wait_ge(fox_v_ready, PAIRS)
            out_hi(0, fox_out_stored, KC - 1)

            def out_units(which, q, fill, h_base):
                with act.Fori(0, 2) as t:
                    for j in range(2):
                        u = U_OUT[which] + 2 + j
                        split(u // 2 + SLOT + t, u + 2 * t, u % 2)
                        for n in range(2):
                            c = 4 * t + 2 * j + n
                            norm_square(q, h_base, c, n)
                            h_hi(fill, h_base, c)
                norm_rstd(q)

            out_units(0, 1, FILL_MLP0, 8)

            def mlp_up(d):
                def unit(i, s, count):
                    split(count, U_UP[d] + i + 2, (U_UP[d] + s) % 2)
                    act.wait_ge(u_ready, 8 * d + i + 1)
                    nc.scalar.activation(r_hi[:, bass.ds(2 * i, 2), :], qkn[:], ACT.Square, scale=0.5
                                         ).then_inc(r_hi_ready, 1)

                c = [(U_UP[d] + j + 2) // 2 + SLOT for j in range(2)]
                with act.Fori(0, 4) as t:
                    for j in range(2):
                        unit(2 * t + j, j, c[j] + t)

            mlp_up(0)
            split_units(U_DOWN[0] + 2, 8)
            mlp_up(1)
            with act.Fori(0, 4) as t:
                for j in range(2):
                    u = U_DOWN[1] + 2 + j
                    norm_square(2, 24, 2 * t + j, j)
                    h_hi(FILL_KV, 24, 2 * t + j)
                    split(u // 2 + SLOT + t, u + 2 * t, u % 2)

            def query_hi(c):
                if c < KC - 1:
                    act.wait_ge(kv_chunk_used, c + 1)
                else:
                    act.wait_ge(w_used, U_KV + 1)
                h_hi(FILL_Q, 24, c)

            for c in range(2):
                query_hi(c)
            norm_rstd(2)
            for c in range(2, KC):
                query_hi(c)

            def swa_square(m, raw):
                act.wait_ge(swa_raw_ready, m + 1)
                after(act, swa_rstd_refined, 2 * m)
                ins = nc.scalar.activation(sqt[:, 0, :], raw, ACT.Square, scale=0.5)
                if m >= 3:
                    ins = nc.scalar.activation(swa_sq_hi[:], raw, ACT.Square, scale=0.5)
                ins.then_inc(swa_squared, 1)

            def swa_rstd(m):
                act.wait_ge(swa_summed, m + 1)
                after(act, swa_normed, m)
                nc.scalar.activation(q_rst[:], ps[:, 1, :], ACT.Ln, bias=EPS).then_inc(swa_ln_step, 1)
                act.wait_ge(swa_ln_step, 2 * m + 1)
                nc.scalar.activation(q_rst[:], q_rst[:], ACT.Exp, scale=-0.5).then_inc(swa_ln_step, 1)
                act.wait_ge(swa_ln_step, 2 * m + 2)
                nc.scalar.activation(sqt[:, 0, :], q_rst[:], ACT.Square).then_inc(swa_rstd_ready, 1)

            def swa_hi(i):
                act.wait_ge(swa_normed, i + 2)
                for e in range(2):
                    own = slice(64 * e, 64 * e + 64)
                    after(act, swa_scores_done, 2 * i - 1 + e)
                    ins = nc.scalar.activation(q_hl[own, e, :], qkn[own, 0, :], ACT.Copy)
                ins.then_inc(swa_hi_ready, 1)

            def swa_exp(j, e):
                act.wait_ge(swa_scores_done, 2 * j + e + 1)
                after(act, swa_out_done, 2 * j - 1 + e)
                b = 2 + 2 * e
                nc.scalar.activation(swa_p[:, e, 0:512], ps[:, b, :], ACT.Exp)
                nc.scalar.activation(swa_p[:, e, 512:896], ps[:, b + 1, 0:384], ACT.Exp)
                nc.scalar.activation(psink[e][:], ps[:, 6 + e, :], ACT.Exp, bias=sinkb[:, 2 * j + e:2 * j + e + 1]
                                     ).then_inc(swa_probs_ready, 1)

            def swa_rec(j):
                act.wait_ge(swa_den_ready, 2 * j + 2)
                after(act, swa_out_stored, 2 * j)
                reciprocal(q_rec[:], qkn[:, 1, :], swa_recip_step, j)

            def split_q(v):
                u = U_Q + v
                split(u // 2 + SLOT, u, u % 2)

            swa_square(0, qkn[:, 1, :])
            split_q(1)
            swa_rstd(0)
            act.wait_ge(hank_landed, 16)
            nc.scalar.activation(hk_hi[:], hank[:], ACT.Copy).then_inc(hankel_hi_ready, 1)
            swa_square(1, q_raw[:, 0, :])
            act.wait_ge(swa_normed, 1)
            for g in range(2):
                for half in range(2):
                    ins = nc.scalar.activation(kd_hi[64 * half:64 * half + 64, g, :], qkn[64 * g:64 * g + 64, 1, :],
                                               ACT.Copy)
            ins.then_inc(swa_hi_ready, 1)
            swa_rstd(1)
            swa_hi(0)
            swa_square(2, q_raw[:, 1, :])
            split_q(2)
            for j in range(PAIRS - 1):
                swa_rstd(j + 2)
                if j == 5:
                    for c in range(4):
                        out_hi(1, swa_out_stored, c)
                swa_exp(j, 0)
                swa_exp(j, 1)
                swa_hi(j + 1)
                if j + 2 < PAIRS:
                    swa_square(j + 3, q_raw[:, j % 2, :])
                swa_rec(j)
                if j % 2 == 1:
                    split_q(3 + j // 2)
            for c in range(4, 6):
                out_hi(1, swa_out_stored, c)
            swa_exp(7, 0)
            swa_exp(7, 1)
            out_hi(1, swa_out_stored, 6)
            swa_rec(7)
            out_hi(1, swa_out_stored, 7)
            out_units(1, 3, FILL_MLP1, 32)

            mlp_up(2)
            split_units(U_DOWN[2] + 2, 8)
            mlp_up(3)
            for n in range(KC):
                if n + 2 < KC:
                    u = U_DOWN[3] + n + 2
                    split(u // 2 + SLOT, u, u % 2)
                if n >= 1:
                    turn_out = n - 1
                    act.wait_ge(fin_turned, turn_out + 1)
                    after(act, out_stored[turn_out % 2], 16 * (turn_out // 2))
                    nc.scalar.activation(out_sb[:, turn_out % 2], ps[:, 6 + turn_out % 2, :].rearrange(
                        "p (b n) -> p b n", b=TB), ACT.Copy).then_inc(out_copied, 1)
            act.wait_ge(fin_turned, KC)
            act.wait_ge(out_stored[1], 16 * (KC // 2 - 1))
            nc.scalar.activation(out_sb[:, 1], ps[:, 7, :].rearrange("p (b n) -> p b n", b=TB),
                                 ACT.Copy).then_inc(out_copied, 1)

        @block.vector
        def _(dve):
            V = nc.vector

            nc.vector.memset(bf[:], 0.0).then_inc(wf_zero, 1)

            def acc_zero():
                V.memset(acc, 0.0).then_inc(norm_accumulated, 1)

            def norm_add(q, c, slot):
                dve.wait_ge(norm_squared, KC * q + c + 1)
                dve.wait_ge(norm_accumulated, 9 * q + c + 1)
                V.tensor_tensor(acc, acc, sqt[:, slot, :], ALU.add).then_inc(norm_accumulated, 1)

            def newton(square, mean_square, y, refined, count):
                V.scalar_tensor_tensor(out=square, in0=mean_square, scalar=EPS, in1=square, op0=ALU.add,
                                       op1=ALU.mult).then_inc(refined, 1)
                dve.wait_ge(refined, count - 1)
                V.scalar_tensor_tensor(out=y, in0=square, scalar=-3.0, in1=y, op0=ALU.add,
                                       op1=ALU.mult).then_inc(refined, 1)
                dve.wait_ge(refined, count)

            def norm_refine(q):
                dve.wait_ge(norm_rstd_ready, q + 1)
                newton(sqt[:, 0, :], ps[:, 7, :], rst[:, 0, :], norm_refined, 2 * q + 2)

            dve.wait_ge(gains_turned, 1)
            V.tensor_copy(gains[:, 0:16], ps[:, 7, 0:16]).then_inc(constants_ready, 1)
            acc_zero()

            def x_hat_chunk(c):
                V.scalar_tensor_tensor(out=x_hat[:, c, :], in0=hT[:, c, :], scalar=-0.5, in1=rst[:, 0, :],
                                       op0=ALU.mult, op1=ALU.mult).then_inc(xhat_ready, 1)

            def h_lo(fill, c):
                dve.wait_ge(xn_hi_ready, KC * fill + c + 1)
                one = [t[:, bass.ds(c, 1), :].rearrange("p a n -> p (a n)") for t in (hT, xn_hi, xn_lo)]
                V.scalar_tensor_tensor(out=one[2], in0=one[0], scalar=gains[:, bass.ds(8 * GAIN[fill] + c, 1)],
                                       in1=one[1].bitcast(F32), op0=ALU.mult, op1=ALU.subtract).then_inc(xn_ready, 1)

            def out_lo(which, fill, c):
                dve.wait_ge(xn_hi_ready, KC * fill + c + 1)
                V.tensor_tensor(o_lo[which][:, c, :], o_t[:, c, :], o_hi[which][:, c, :].bitcast(F32),
                                ALU.subtract).then_inc(xn_ready, 1)

            for c in range(KC):
                dve.wait_ge(x_turned, c + 1)
                V.tensor_copy(hT[:, c, :], ps[:, c, :]).then_inc(h_written, 1)
                if c >= 1:
                    h_lo(FILL_V, c - 1)
            h_lo(FILL_V, KC - 1)
            for c in range(KC):
                norm_add(0, c, c % 2)
            dve.wait_ge(bias_row_made, 1)
            V.tensor_tensor(ext_sb[:], ps[0:HEADS, 6, 0:384], ctemp[0:HEADS, C_NEG - C_TEMP:C_NEG - C_TEMP + 384],
                            ALU.add).then_inc(bias_row_ready, 1)
            norm_refine(0)
            for c in range(KC):
                x_hat_chunk(c)
            dve.wait_ge(gains_turned, 2)
            V.tensor_copy(gains[:, 16:44], ps[:, 6, 0:28]).then_inc(constants_ready, 1)
            dve.wait_ge(constants_ready, 2)
            for n, scale in enumerate((-0.5 * float(HD) ** -0.5, -0.5, 0.25 * float(HD) ** -0.5, 0.25)):
                V.tensor_scalar(half_gains[:, n:n + 1], gains[:, 40 + n:41 + n], scale, None, ALU.mult)
            V.tensor_scalar(nsink[:], sinkb[:], -1.0, None, ALU.mult).then_inc(constants_ready, 1)
            dve.wait_ge(wf_landed, 32)
            V.tensor_copy(wf_hi[:], wf[:]).then_inc(wf_split, 1)
            dve.wait_ge(wf_split, 1)
            V.tensor_tensor(wf_lo[:], wf[:], wf_hi[:].bitcast(F32), ALU.subtract).then_inc(wf_split, 1)
            dve.wait_ge(ctemp_landed, 16)
            for dst, src in ((ident_r, ident), (blk_r, blk), (anti_r, C_ANTI), (ones_r, C_ONES), (maskA_r, C_MASKA), (maskT_r, C_MASKT)):
                if isinstance(src, int):
                    src = ctemp[:, src - C_TEMP:src - C_TEMP + P]
                V.tensor_copy(dst[:], src)
            V.tensor_tensor(pick[:], ident[0:64, 0:HEADS], ident[0:64, 32:32 + HEADS], ALU.add)
            V.memset(vx[:, :, HD:2 * HD], 1.0).then_inc(ones_ready, 1)
            dve.wait_ge(v_rstd_turned, 1)
            V.tensor_scalar(v_rst[:], ps[:, 7, 0:TB], -0.5, None, ALU.mult).then_inc(v_rstd_ready, 1)
            dve.wait_ge(v_rstd_ready, 1)

            def v_out(v):
                dve.wait_ge(w_used, U_V + v + 1)
                bank = V_BANKS[v]
                for half in range(2):
                    src = ps[:, bank:bank + 2, :].rearrange("p a (b n) -> p (a b) n", b=2)[:, :, half * P:(half + 1) * P]
                    ins = V.tensor_tensor(v_all[:, 2 * v + half], src, v_rst[:, :, None].to_broadcast([P, TB, P]), ALU.mult)
                ins.then_inc(v_stored, 1)

            for v in range(3):
                v_out(v)
            for c in range(KC):
                dve.wait_ge(xn_hi_ready, KC * FILL_ATTN0 + c + 1)
                V.scalar_tensor_tensor(out=xn_lo[:, c, :], in0=x_hat[:, c, :], scalar=gains[:, c:c + 1],
                                       in1=xn_hi[:, c, :].bitcast(F32), op0=ALU.mult, op1=ALU.subtract
                                       ).then_inc(xn_ready, 1)
            v_out(3)
            dve.wait_ge(xn_ready, KC * FILL_ATTN0 + KC)
            for e in range(2):
                rows = slice(64 - 64 * e, 128 - 64 * e)
                ins = V.tensor_copy(qk_hi[rows, 0, e, :].rearrange("p (b n) -> p b n", b=TB),
                                    ctemp[rows, None, C_ONES - C_TEMP:C_ONES - C_TEMP + P].to_broadcast([64, TB, P]))
            ins.then_inc(ones_ready, 1)
            dve.wait_ge(bias_row_stored, 16)
            V.memset(ct[:, 3, :], 1.0).then_inc(gate_vector_step, 1)
            dve.wait_ge(gate_scalar_step, 4)
            V.scalar_tensor_tensor(out=ct[:, 1, :], in0=ct[:, 0, :], scalar=0.0, in1=ct[:, 1, :],
                                   op0=ALU.min, op1=ALU.subtract).then_inc(gate_vector_step, 1)
            dve.wait_ge(gate_vector_step, 2)
            V.tensor_tensor_scan(out=ct[:, 2, :], data0=ct[:, 3, :], data1=ct[:, 1, :], initial=0.0,
                                 op0=ALU.mult, op1=ALU.subtract).then_inc(gate_vector_step, 1)
            dve.wait_ge(gate_vector_step, 3)
            V.tensor_copy(c_split[0:32, :], ct[0:32, 2, :]).then_inc(gate_vector_step, 1)
            dve.wait_ge(gate_vector_step, 4)
            V.tensor_tensor(c_split[32:64, :], ct[0:32, 2, :], c_split[0:32, :].bitcast(F32),
                            ALU.subtract).then_inc(gate_vector_step, 1)
            dve.wait_ge(gate_vector_step, 5)

            def fox_c(i):
                for e in range(2):
                    after(dve, fox_scores_done, 2 * i - 1 + e)
                    V.tensor_scalar(qk_hi[64 - 64 * e:128 - 64 * e, 1, e, :], c_split[:].bitcast(F32),
                                    pick[:, bass.ds(2 * i + e, 1)], None, ALU.mult).then_inc(fox_c_ready, 1)

            def fox_vx(i):
                after(dve, fox_out_done, 2 * i)
                for e in range(2):
                    src = v_all[:, bass.ds(i, 1), :, HD * e:HD * e + HD].rearrange("p a b n -> p (a b) n")
                    ins = V.tensor_copy(vx[:, :, 2 * HD * e:2 * HD * e + HD], src)
                ins.then_inc(fox_v_ready, 1)

            def fox_norm(i, t):
                dve.wait_ge(fox_rstd_ready, 2 * i + t + 1)
                newton(sqt[:, t, :], ps[:, t, :], rst[:, t, :], fox_rstd_refined, 4 * i + 2 * t + 2)
                after(dve, fox_cross_ready, 2 * i)
                V.scalar_tensor_tensor(out=qkn[:, t, :], in0=raw[:, t, :], scalar=half_gains[:, t:t + 1],
                                       in1=rst[:, t, :], op0=ALU.mult, op1=ALU.mult).then_inc(fox_normed, 1)

            def fox_lo(i):
                for e in range(2):
                    dve.wait_ge(fox_hi_ready, 2 * i + e + 1)
                    own, other = slice(64 * e, 64 * e + 64), slice(64 - 64 * e, 128 - 64 * e)
                    V.tensor_tensor(qk_x[other, 0, e, :], qkn[own, 0, :], qk_hi[own, 0, e, :].bitcast(F32), ALU.subtract)
                    V.tensor_tensor(qk_x[own, 1, e, :], qkn[own, 1, :], qk_hi[own, 1, e, :].bitcast(F32),
                                    ALU.subtract).then_inc(fox_lo_ready, 1)

            def fox_max(j):
                for e in range(2):
                    dve.wait_ge(fox_max_scores_done, 2 * j + e + 1)
                    after(dve, fox_diag_ready, 2 * j - 1 + e)
                    b0, b1, b2 = SCORE_BANKS[e]
                    for qb, bank, c0, n in ((3, b0, 0, 512), (2, b1, 0, 384), (0, b1, 384, 128), (1, b2, 0, 256)):
                        ins = V.tensor_reduce(nm[:, e, qb:qb + 1], ps[:, bank, c0:c0 + n], AX_X, ALU.max, negate=True)
                    ins.then_inc(fox_max_ready, 1)
                    dve.wait_ge(fox_max_ready, 2 * j + e + 1)
                    after(dve, fox_scores_done, 2 * j - 1 + e)
                    V.tensor_tensor(diag[:, e, :].rearrange("p (b n) -> p b n", b=TB),
                                    ident[:, None, :].to_broadcast([P, TB, P]),
                                    nm[:, e, :, None].to_broadcast([P, TB, P]), ALU.mult).then_inc(fox_diag_ready, 1)

            def reciprocal(y, den, refined, n):
                V.scalar_tensor_tensor(out=den, in0=den, scalar=-1.0, in1=y, op0=ALU.mult, op1=ALU.mult
                                       ).then_inc(refined, 1)
                dve.wait_ge(refined, 2 * n + 1)
                V.scalar_tensor_tensor(out=y, in0=den, scalar=2.0, in1=y, op0=ALU.add, op1=ALU.mult).then_inc(refined, 1)
                dve.wait_ge(refined, 2 * n + 2)

            def fox_out(j):
                dve.wait_ge(fox_recip_step, 2 * j + 2)
                reciprocal(ct[:, 2, :], ct[:, 3, :], fox_recip_refined, j)
                for e in range(2):
                    own = slice(64 * e, 64 * e + 64)
                    dst = o_t[own, bass.ds(j, 1), :].rearrange("p a n -> p (a n)")
                    V.tensor_tensor(dst, ps[own, 4 + 3 * e, :], ct[own, 2, :], ALU.mult).then_inc(fox_out_stored, 1)

            def fox_step(i):
                fox_max(i - 1)
                fox_norm(i, 0)
                if isinstance(i, int) and i == 7:
                    for c in range(5):
                        out_lo(0, FILL_OUT_A, c)
                fox_norm(i, 1)
                fox_c(i)
                fox_out(i - 1)
                fox_vx(i)
                fox_lo(i)

            fox_c(0)
            fox_vx(0)
            fox_norm(0, 0)
            fox_norm(0, 1)
            fox_lo(0)
            fox_step(1)
            with dve.Fori(1, 3) as t:
                fox_step(2 * t)
                fox_step(2 * t + 1)
            fox_step(6)
            fox_step(7)
            fox_max(7)
            for c in range(5, KC - 1):
                out_lo(0, FILL_OUT_A, c)
            fox_out(7)
            out_lo(0, FILL_OUT_A, KC - 1)

            def add_chunk(bank, c):
                dst = hT[:, bass.ds(c, 1), :].rearrange("p a n -> p (a n)")
                V.tensor_tensor(dst, dst, ps[:, bank, :], ALU.add).then_inc(h_written, 1)

            def add_out(which, q, fill):
                acc_zero()
                with dve.Fori(0, 2) as t:
                    for j in range(2):
                        dve.wait_ge(w_used, U_OUT[which] + 2 * t + j + 1)
                        for n in range(2):
                            add_chunk(2 * j + n, 4 * t + 2 * j + n)
                        for n in range(2):
                            norm_add(q, 4 * t + 2 * j + n, n)
                            h_lo(fill, 4 * t + 2 * j + n)
                norm_refine(q)

            def mlp_up(d):
                scale = rst[:, 0:1, :].to_broadcast([P, 2, T])
                with dve.Fori(0, 4) as t:
                    for j in range(2):
                        i = 2 * t + j
                        dve.wait_ge(w_used, U_UP[d] + i + 1)
                        V.scalar_tensor_tensor(out=qkn[:], in0=ps[:, 2 * j:2 * j + 2, :], scalar=0.0, in1=scale,
                                               op0=ALU.max, op1=ALU.mult).then_inc(u_ready, 1)
                        dve.wait_ge(u_ready, 8 * d + i + 1)
                        V.scalar_tensor_tensor(out=sqt[:], in0=qkn[:], scalar=0.25, in1=qkn[:], op0=ALU.mult,
                                               op1=ALU.mult).then_inc(r_made, 1)
                        dve.wait_ge(r_made, 8 * d + i + 1)
                        dve.wait_ge(r_hi_ready, 8 * d + i + 1)
                        V.tensor_tensor(r_lo[:, bass.ds(2 * i, 2), :], sqt[:],
                                        r_hi[:, bass.ds(2 * i, 2), :].bitcast(F32), ALU.subtract).then_inc(r_lo_ready, 1)
                        dve.wait_ge(r_lo_ready, 8 * d + i + 1)

            def mlp_down(d, q=None, fill=None):
                if q is not None:
                    acc_zero()
                with dve.Fori(0, 4) as t:
                    for j in range(2):
                        dve.wait_ge(w_used, U_DOWN[d] + 2 * t + j + 1)
                        add_chunk(4 + j, 2 * t + j)
                        if q is not None:
                            norm_add(q, 2 * t + j, j)
                            h_lo(fill, 2 * t + j)

            add_out(0, 1, FILL_MLP0)
            mlp_up(0)
            mlp_down(0)
            mlp_up(1)
            mlp_down(1, 2, FILL_KV)

            for c in range(2):
                h_lo(FILL_Q, c)
            norm_refine(2)
            for c in range(2, 5):
                h_lo(FILL_Q, c)

            def swa_raw(m, bank, dst):
                V.tensor_tensor(dst, ps[:, bank, :], rst[:, 0, :], ALU.mult).then_inc(swa_raw_ready, 1)

            def swa_query_raw(i):
                if i % 2 == 0:
                    dve.wait_ge(swa_q_projected, i // 2 + 1)
                else:
                    dve.wait_ge(w_used, U_Q + i // 2 + 1)
                swa_raw(i + 1, Q_BANKS[i], q_raw[:, i % 2, :])

            def swa_norm(m, raw, dst, gain):
                dve.wait_ge(swa_rstd_ready, m + 1)
                newton(sqt[:, 0, :], ps[:, 1, :], q_rst[:], swa_rstd_refined, 2 * m + 2)
                V.scalar_tensor_tensor(out=dst, in0=raw, scalar=half_gains[:, gain:gain + 1], in1=q_rst[:],
                                       op0=ALU.mult, op1=ALU.mult).then_inc(swa_normed, 1)

            def swa_lo(i):
                dve.wait_ge(swa_hi_ready, i + 2)
                after(dve, swa_scores_done, 2 * i)
                for e in range(2):
                    own, other = slice(64 * e, 64 * e + 64), slice(64 - 64 * e, 128 - 64 * e)
                    ins = V.tensor_tensor(q_hl[other, e, :], qkn[own, 0, :], q_hl[own, e, :].bitcast(F32), ALU.subtract)
                ins.then_inc(swa_lo_ready, 1)

            dve.wait_ge(w_used, U_KV + 1)
            swa_raw(0, 1, qkn[:, 1, :])
            for c in range(5, KC):
                h_lo(FILL_Q, c)
            V.tensor_tensor(v_t[:], ps[:, 2, :], rst[:, 0, :], ALU.mult).then_inc(v_t_ready, 1)
            V.memset(swa_vx[:, :, :, HD:2 * HD], 1.0)
            swa_norm(0, qkn[:, 1, :], qkn[:, 1, :], 3)
            swa_query_raw(0)
            swa_norm(1, q_raw[:, 0, :], qkn[:, 0, :], 2)
            swa_query_raw(1)
            dve.wait_ge(swa_hi_ready, 1)
            for g in range(2):
                for half in range(2):
                    ins = V.tensor_tensor(kd_lo[64 * half:64 * half + 64, g, :], qkn[64 * g:64 * g + 64, 1, :],
                                          kd_hi[64 * g:64 * g + 64, g, :].bitcast(F32), ALU.subtract)
            ins.then_inc(swa_lo_ready, 1)
            swa_lo(0)
            dve.wait_ge(v_turned, 1)
            for g in range(2):
                src = ps[:, 7, :].rearrange("p (b n) -> p b n", b=TB)[:, :, HD * g:HD * g + HD]
                for half in range(2):
                    ins = V.tensor_scalar(swa_vx[:, g, :, 2 * HD * half:2 * HD * half + HD], src, -0.5, None, ALU.mult)
            ins.then_inc(swa_v_ready, 1)

            def swa_max(j):
                for e in range(2):
                    dve.wait_ge(swa_max_scores_done, 2 * j + e + 1)
                    after(dve, swa_diag_ready, 2 * j - 1 + e)
                    b = 2 + 2 * e
                    V.tensor_reduce(nm[:, e, 1:3], ps[:, b, :].rearrange("p (b n) -> p b n", b=2), AX_X, ALU.max,
                                    negate=True)
                    V.tensor_reduce(nm[:, e, 3:4], ps[:, b + 1, 0:256], AX_X, ALU.max, negate=True)
                    V.tensor_reduce(nm[:, e, 0:1], ps[:, b + 1, 256:384], AX_X, ALU.max, negate=True).then_inc(swa_max_found, 1)
                    dve.wait_ge(swa_max_found, 2 * j + e + 1)
                    V.tensor_scalar(nm[:, e, :], nm[:, e, :], nsink[:, bass.ds(2 * j + e, 1)], None,
                                    ALU.min).then_inc(swa_max_ready, 1)
                    dve.wait_ge(swa_max_ready, 2 * j + e + 1)
                    after(dve, swa_scores_done, 2 * j - 1 + e)
                    V.tensor_tensor(swa_diag[:, e, :].rearrange("p (b n) -> p b n", b=TB),
                                    ident[:, None, :].to_broadcast([P, TB, P]),
                                    nm[:, e, :, None].to_broadcast([P, TB, P]), ALU.mult).then_inc(swa_diag_ready, 1)

            def swa_den(j):
                for e in range(2):
                    dve.wait_ge(swa_out_done, 2 * j + e + 1)
                    own, other = slice(64 * e, 64 * e + 64), slice(64 - 64 * e, 128 - 64 * e)
                    V.tensor_tensor(qkn[own, 1, :], ps[other, 6 + e, :], psink[e][other, :], ALU.add).then_inc(swa_den_ready, 1)

            def swa_out(j):
                dve.wait_ge(swa_recip_step, 2 * j + 2)
                reciprocal(q_rec[:], qkn[:, 1, :], swa_recip_refined, j)
                for e in range(2):
                    own = slice(64 * e, 64 * e + 64)
                    V.tensor_tensor(o_t[own, j, :], ps[own, 6 + e, :], q_rec[own, :], ALU.mult).then_inc(swa_out_stored, 1)

            for j in range(PAIRS - 1):
                swa_max(j)
                if j:
                    swa_out(j - 1)
                swa_norm(j + 2, q_raw[:, (j + 1) % 2, :], qkn[:, 0, :], 2)
                if j + 2 < PAIRS:
                    swa_query_raw(j + 2)
                if j == 5:
                    for c in range(4):
                        out_lo(1, FILL_OUT_B, c)
                swa_lo(j + 1)
                swa_den(j)
            swa_max(7)
            swa_out(6)
            for c in range(4, 7):
                out_lo(1, FILL_OUT_B, c)
            swa_den(7)
            swa_out(7)
            out_lo(1, FILL_OUT_B, KC - 1)
            add_out(1, 3, FILL_MLP1)
            mlp_up(2)
            mlp_down(2)
            mlp_up(3)
            for n in range(KC):
                dve.wait_ge(w_used, U_DOWN[3] + n + 1)
                after(dve, fin_turned, n - 1)
                V.tensor_tensor(qkn[:, n % 2, :], hT[:, n, :], ps[:, 4 + n % 2, :], ALU.add).then_inc(fin_ready, 1)

        @block.tensor
        def _(pe):
            mm = nc.tensor.matmul

            def three(out_, st_hi, st_lo, mv_hi, mv_lo, start, stop):
                mm(out_, st_hi, mv_hi, start=start, stop=False)
                mm(out_, st_hi, mv_lo, start=False, stop=False)
                return mm(out_, st_lo, mv_hi, start=False, stop=stop)

            pe.wait_ge(consts_landed, 16)
            pe.wait_ge(gain_landed, 16)
            nc.tensor.transpose(ps[:, 7, 0:16], g_in[:], ident[0:16, 0:16]).then_inc(gains_turned, 1)
            for b in range(TB):
                pe.wait_ge(x_landed[b], 16)
                for c in range(KC):
                    if b == 0 and c == KC - 1:
                        pe.wait_ge(constants_ready, 1)
                    ins = nc.tensor.transpose(ps[:, c, b * P:(b + 1) * P], x_in[:, b, c * P:(c + 1) * P], ident)
                    if b == TB - 1:
                        ins.then_inc(x_turned, 1)

            def norm_sum(q):
                pe.wait_ge(norm_accumulated, 9 * q + 9)
                mm(ps[:, 7, :], ones_d, acc, start=True, stop=True).then_inc(norm_summed, 1)

            pe.wait_ge(h_written, 2)
            for v in range(4):
                u = U_V + v
                s = u % 2
                pe.wait_ge(w_lo_ready, u + 1)
                if v == 3:
                    pe.wait_ge(v_stored, 1)
                wh = w_hi[:, s, :].rearrange("p (k n) -> p k n", k=KC)
                wl = w_lo[:, s, :].rearrange("p (k n) -> p k n", k=KC)
                for k in range(KC):
                    if v == 0:
                        pe.wait_ge(xn_ready, k + 1)
                    if (v, k) == (1, 5):
                        pe.wait_ge(ctemp_landed, 16)
                        pe.wait_ge(small_landed, 16 * 8)
                        mm(ps[0:HEADS, 6, 0:384], rel[0:N_BUCKETS, :],
                           ctemp[0:N_BUCKETS, C_HOT - C_TEMP:C_HOT - C_TEMP + 384], start=True, stop=True).then_inc(bias_row_made, 1)
                    if (v, k) == (1, 6):
                        norm_sum(0)
                    if (v, k) == (2, 3):
                        pe.wait_ge(norm_refined, 2)
                        for b in range(TB):
                            ins = mm(ps[:, 7, b:b + 1], rst[:, 0, b * P:(b + 1) * P], ident[:, 0:1], start=True, stop=True)
                        ins.then_inc(v_rstd_turned, 1)
                        pe.wait_ge(bias_row_ready, 1)
                        nc.tensor.transpose(ps[:, 6, 0:28], g_in2[:], ident[0:28, 0:28]).then_inc(gains_turned, 1)
                    for b in range(TB):
                        o = ps[:, V_BANKS[v] + b // 2, 256 * (b % 2):256 * (b % 2) + 256]
                        xs = slice(b * P, (b + 1) * P)
                        ins = three(o, xn_hi[:, k, xs], xn_lo[:, k, xs], wh[:, k, :], wl[:, k, :],
                                    k == 0 and b % 2 == 0, k == KC - 1 and b % 2 == 1)
                    if v == 3 and k < KC - 1:
                        ins.then_inc(v_chunk_used, 1)
                ins.then_inc(w_used, 1)

            pe.wait_ge(wf_split, 2)
            pe.wait_ge(constants_ready, 3)
            for k in range(KC):
                pe.wait_ge(xn_ready, KC * FILL_ATTN0 + k + 1)
                ins = three(ps[:, 6, :], wf_hi[:, k, :], wf_lo[:, k, :], xn_hi[:, k, :], xn_lo[:, k, :],
                            k == 0, k == KC - 1)
            ins.then_inc(gate_projected, 1)
            pe.wait_ge(v_stored, 4)

            def proj_pair(i, s, t, sum_before=None):
                if t == 0:
                    pe.wait_ge(w_lo_ready, U_PAIR + i + 1)
                after(pe, fox_rstd_refined, 4 * i - 3 + 2 * t)
                wh = w_hi[:, s, :].rearrange("p (t k n) -> p t k n", t=2, k=KC)
                wl = w_lo[:, s, :].rearrange("p (t k n) -> p t k n", t=2, k=KC)
                for k in range(KC):
                    if k == 2 and sum_before is not None:
                        fox_sum(*sum_before)
                    ins = three(ps[:, t, :], wh[:, t, k], wl[:, t, k], xn_hi[:, k, :], xn_lo[:, k, :], k == 0, k == KC - 1)
                ins.then_inc(w_used if t else fox_q_projected, 1)

            def fox_sum(i, t):
                if isinstance(i, int) and i == 0:
                    pe.wait_ge(fox_squared, t + 1)
                    mm(ps[:, t, :], blk, sqt[:, t, :], start=True, stop=True).then_inc(fox_summed, 1)
                else:
                    pe.wait_ge(fox_squares_split, 2 * i + t - 1)
                    mm(ps[:, t, :], blk_r[:], fox_sq_hi[:], start=True, stop=False)
                    mm(ps[:, t, :], blk_r[:], fox_sq_lo[:], start=False, stop=True).then_inc(fox_summed, 1)

            def fox_max_scores(j):
                def tile(e, qb, bank, c0, start=True):
                    n = (qb + 1) * P
                    mm(ps[:, bank, c0:c0 + n], qk_hi[:, 0, e, qb * P:(qb + 1) * P], qk_hi[:, 1, e, 0:n],
                       start=start, stop=False)

                for e in range(2):
                    b0, b1, b2 = SCORE_BANKS[e]
                    pe.wait_ge(fox_hi_ready, 2 * j + e + 1)
                    pe.wait_ge(fox_c_ready, 2 * j + e + 1)
                    tile(e, 3, b0, 0)
                    mm(ps[:, b0, 3 * P:], ident_r[:], maskA_r[:], start=False, stop=True)
                    tile(e, 2, b1, 0)
                    tile(e, 0, b1, 3 * P, False)
                    mm(ps[:, b1, 2 * P:].rearrange("p (a n) -> p a n", a=2), ident_r[:],
                       maskA_r[:, None, :].to_broadcast([P, 2, P]), start=False, stop=True)
                for e in range(2):
                    b2 = SCORE_BANKS[e][2]
                    after(pe, fox_out_stored, 2 * j - 1 + e)
                    tile(e, 1, b2, 0)
                    mm(ps[:, b2, P:2 * P], ident_r[:], maskA_r[:], start=False, stop=True).then_inc(fox_max_scores_done, 1)

            def fox_scores(j):
                pe.wait_ge(fox_lo_ready, 2 * j + 2)
                pe.wait_ge(fox_cross_ready, 2 * j + 2)
                for e in range(2):
                    pe.wait_ge(fox_diag_ready, 2 * j + e + 1)
                    b0, b1, b2 = SCORE_BANKS[e]
                    for kb, bank, c0, start in ((0, b0, 0, True), (3, b1, 0, True), (1, b1, P, False), (2, b2, 0, True)):
                        n = (TB - kb) * P
                        o = ps[:, bank, c0:c0 + n]
                        ks, qs = slice(kb * P, (kb + 1) * P), slice(kb * P, T)
                        mm(o, qk_hi[:, 1, e, ks], qk_hi[:, 0, e, qs], start=start, stop=False)
                        mm(o, qk_x[:, 1, e, ks], qk_x[:, 0, e, qs], start=False, stop=False)
                        mm(o, ones_r[:], diag[:, e, qs], start=False, stop=False)
                        if kb in (0, 2):
                            ins = mm(ps[:, bank, 0:P], ident_r[:], maskT_r[:], start=False, stop=True)
                        if kb == 1:
                            mm(ps[:, bank, 0:2 * P].rearrange("p (a n) -> p a n", a=2), ident_r[:],
                               maskT_r[:, None, :].to_broadcast([P, 2, P]), start=False, stop=True)
                    ins.then_inc(fox_scores_done, 1)

            def fox_pv(j):
                pe.wait_ge(fox_v_ready, j + 1)
                for e in range(2):
                    pe.wait_ge(fox_probs_ready, 2 * j + e + 1)
                    for kb, src in ((0, 0), (1, 640), (2, 1024), (3, 512)):
                        n = (TB - kb) * P
                        ins = mm(ps[:, 4 + 3 * e, kb * P:T], vx[:, kb, HD * e:HD * e + P], pT[:, e, src:src + n],
                                 start=(kb == 0), stop=(kb == TB - 1))
                    ins.then_inc(fox_out_done, 1)

            pe.wait_ge(ones_ready, 2)
            proj_pair(0, 0, 0)
            proj_pair(0, 0, 1, (0, 0))

            def fox_step(i, s):
                proj_pair(i, s, 0, (0, 1) if isinstance(i, int) and i == 1 else None)
                fox_max_scores(i - 1)
                proj_pair(i, s, 1, (i, 0))
                fox_scores(i - 1)
                fox_sum(i, 1)
                fox_pv(i - 1)

            fox_step(1, 1)
            with pe.Fori(1, 4) as t:
                fox_step(2 * t, 0)
                fox_step(2 * t + 1, 1)
            def unit_d(u, s, banks, fill=None, k_waits=False, m=(xn_hi, xn_lo)):
                pe.wait_ge(w_lo_ready, u + 1)
                wh = w_hi[:, s, :].rearrange("p (k n) -> p k n", k=KC)
                wl = w_lo[:, s, :].rearrange("p (k n) -> p k n", k=KC)
                for k in range(KC):
                    if k_waits:
                        pe.wait_ge(xn_ready, KC * fill + k + 1)
                    for n in range(2):
                        ins = three(ps[:, banks + n, :], wh[:, k, n * P:(n + 1) * P], wl[:, k, n * P:(n + 1) * P],
                                    m[0][:, k, :], m[1][:, k, :], k == 0, k == KC - 1)
                ins.then_inc(w_used, 1)

            def out_piece(which, j, halves, steps):
                u = U_OUT[which] + j
                fill = [FILL_OUT_A, FILL_OUT_B][which]
                wh = w_hi[:, u % 2, :].rearrange("p (k n) -> p k n", k=KC)
                wl = w_lo[:, u % 2, :].rearrange("p (k n) -> p k n", k=KC)
                for k in steps:
                    pe.wait_ge(w_lo_ready, u + 1)
                    pe.wait_ge(xn_ready, KC * fill + k + 1)
                    for n in halves:
                        ins = three(ps[:, 2 * j + n, :], wh[:, k, n * P:(n + 1) * P], wl[:, k, n * P:(n + 1) * P],
                                    o_hi[which][:, k, :], o_lo[which][:, k, :], k == 0, k == KC - 1)
                if steps[-1] == KC - 1:
                    ins.then_inc(w_used, 1)

            def proj_out_rest(which):
                h_base = [8, 32][which]
                u = U_OUT[which]
                for j in range(2, 4):
                    pe.wait_ge(h_written, h_base + 2 * (j - 1))
                    unit_d(u + j, (u + j) % 2, 2 * (j % 2), m=(o_hi[which], o_lo[which]))

            def mlp_up(d, fill, k_waits, q=None):
                u = U_UP[d]
                if q is not None:
                    pe.wait_ge(h_written, 14 if d == 0 else 38)
                unit_d(u, u % 2, 0, fill, k_waits)
                if q is not None:
                    norm_sum(q)
                    pe.wait_ge(h_written, 16 if d == 0 else 40)
                unit_d(u + 1, (u + 1) % 2, 2)
                with pe.Fori(1, 4) as t:
                    for j in range(2):
                        pe.wait_ge(u_ready, 8 * d + 2 * t + j - 1)
                        unit_d(u + j + 2 * t, (u + j) % 2, 2 * j)

            def down_unit(u, s, bank, d=None):
                pe.wait_ge(w_lo_ready, u + 1)
                wh = w_hi[:, s, :].rearrange("p (k n) -> p k n", k=FH)
                wl = w_lo[:, s, :].rearrange("p (k n) -> p k n", k=FH)
                for k in range(FH):
                    if d is not None and k % 2 == 0:
                        pe.wait_ge(r_lo_ready, 8 * d + k // 2 + 1)
                    ins = three(ps[:, bank, :], wh[:, k, :], wl[:, k, :], r_hi[:, k, :], r_lo[:, k, :],
                                k == 0, k == FH - 1)
                ins.then_inc(w_used, 1)

            H_BASE = [16, 24, 40, 48]

            def mlp_down(d):
                u = U_DOWN[d]
                pe.wait_ge(h_written, H_BASE[d])
                down_unit(u, u % 2, 4, d)
                down_unit(u + 1, (u + 1) % 2, 5)
                with pe.Fori(1, 4) as t:
                    for j in range(2):
                        pe.wait_ge(h_written, H_BASE[d] + 2 * t + j - 1)
                        down_unit(u + j + 2 * t, (u + j) % 2, 4 + j)

            both = range(2)
            pe.wait_ge(fox_rstd_refined, 4 * PAIRS - 1)
            out_piece(0, 0, both, range(0, 3))
            fox_max_scores(PAIRS - 1)
            out_piece(0, 0, both, range(3, 5))
            fox_scores(PAIRS - 1)
            fox_pv(PAIRS - 1)
            out_piece(0, 0, both, range(5, 7))
            out_piece(0, 1, both, range(0, 3))
            out_piece(0, 0, both, range(7, 8))
            out_piece(0, 1, both, range(3, 8))
            proj_out_rest(0)
            mlp_up(0, FILL_MLP0, True, 1)
            mlp_down(0)
            mlp_up(1, FILL_MLP0, False)
            mlp_down(1)

            s = U_KV % 2
            pe.wait_ge(w_lo_ready, U_KV + 1)
            wh = w_hi[:, s, :].rearrange("p (k n) -> p k n", k=KC)
            wl = w_lo[:, s, :].rearrange("p (k n) -> p k n", k=KC)
            for k in range(KC):
                if k == 3:
                    norm_sum(2)
                pe.wait_ge(xn_ready, KC * FILL_KV + k + 1)
                three(ps[:, 1, :], wh[:, k, 0:P], wl[:, k, 0:P], xn_hi[:, k, :], xn_lo[:, k, :], k == 0, k == KC - 1)
                ins = three(ps[:, 2, :], wh[:, k, P:2 * P], wl[:, k, P:2 * P], xn_hi[:, k, :], xn_lo[:, k, :],
                            k == 0, k == KC - 1)
                ins.then_inc(kv_chunk_used if k < KC - 1 else w_used, 1)
            def swa_proj(i, k_waits=False, sum_before=None, ks=range(KC)):
                v, n = i // 2, i % 2
                u = U_Q + v
                s = u % 2
                if n == 0:
                    pe.wait_ge(w_lo_ready, u + 1)
                if i != 1:
                    after(pe, swa_raw_ready, {0: 0, 2: 2}.get(i, i + 1))
                bank = Q_BANKS[i]
                wh = w_hi[:, s, :].rearrange("p (k n) -> p k n", k=KC)
                wl = w_lo[:, s, :].rearrange("p (k n) -> p k n", k=KC)
                for k in ks:
                    if k_waits:
                        pe.wait_ge(xn_ready, KC * FILL_Q + k + 1)
                    if sum_before is not None and k == sum_before[1]:
                        swa_sum(sum_before[0])
                    ins = three(ps[:, bank, :], wh[:, k, n * P:(n + 1) * P], wl[:, k, n * P:(n + 1) * P],
                                xn_hi[:, k, :], xn_lo[:, k, :], k == 0, k == KC - 1)
                if ks[-1] == KC - 1:
                    ins.then_inc(w_used if n else swa_q_projected, 1)

            def swa_sum(m):
                pe.wait_ge(swa_squared, m + 1)
                if m == 0:
                    pe.wait_ge(swa_raw_ready, 1)
                after(pe, swa_rstd_refined, 2 * m - 1)
                if m < 3:
                    mm(ps[:, 1, :], blk, sqt[:, 0, :], start=True, stop=True).then_inc(swa_summed, 1)
                else:
                    pe.wait_ge(swa_squares_split, m - 2)
                    mm(ps[:, 1, :], blk_r[:], swa_sq_hi[:], start=True, stop=False)
                    mm(ps[:, 1, :], blk_r[:], swa_sq_lo[:], start=False, stop=True).then_inc(swa_summed, 1)

            def swa_max_scores(j):
                g = j // (PAIRS // 2)
                pe.wait_ge(swa_hi_ready, j + 2)
                for e in range(2):
                    b = 2 + 2 * e
                    h = slice(64 * e, 64 * e + 64)
                    same, before = hk_hi[:, 2 * j + e, 0:P], hk_hi[:, 2 * j + e, P:2 * P]
                    twice = anti_r[:, None, :].to_broadcast([P, 2, P])
                    for qb, bank, c0, start in ((1, b, 0, True), (2, b, 256, False), (3, b + 1, 0, True),
                                                (0, b + 1, 256, False)):
                        n = 2 * P if qb else P
                        k0 = max(qb - 1, 0) * P
                        mm(ps[:, bank, c0:c0 + n], q_hl[h, e, qb * P:(qb + 1) * P], kd_hi[h, g, k0:k0 + n],
                           start=start, stop=False)
                    of_b = ps[:, b, :].rearrange("p (t s n) -> p t s n", t=2, s=2)
                    mm(of_b[:, :, 0, :], before, twice, start=False, stop=False)
                    mm(of_b[:, :, 1, :], same, twice, start=False, stop=True)
                    mm(ps[:, b + 1, 0:P], before, anti_r[:], start=False, stop=False)
                    mm(ps[:, b + 1, P:3 * P].rearrange("p (a n) -> p a n", a=2), same, twice,
                       start=False, stop=True).then_inc(swa_max_scores_done, 1)

            def swa_scores(j):
                g = j // (PAIRS // 2)
                pe.wait_ge(swa_lo_ready, j + 2)
                for e in range(2):
                    pe.wait_ge(swa_diag_ready, 2 * j + e + 1)
                    b = 2 + 2 * e
                    h = slice(64 * e, 64 * e + 64)
                    for kb, bank, c0 in ((0, b, 0), (1, b, 256), (2, b + 1, 0), (3, b + 1, 256)):
                        n = 2 * P if kb < TB - 1 else P
                        o = ps[:, bank, c0:c0 + n]
                        ks, qs = slice(kb * P, (kb + 1) * P), slice(kb * P, kb * P + n)
                        mm(o, kd_hi[:, g, ks], q_hl[:, e, qs], start=True, stop=False)
                        mm(o, kd_lo[h, g, ks], q_hl[h, e, qs], start=False, stop=False)
                        mm(o, ones_r[:], swa_diag[:, e, qs], start=False, stop=False)
                        mm(o, anti_r[:], hk_lo[:, 2 * j + e, 0:n], start=False, stop=False)
                        mm(o, anti_r[:], hk_hi[:, 2 * j + e, 0:n], start=False, stop=True)
                    after(pe, swa_out_stored, 2 * j - 1 + e)
                    mm(ps[:, 6 + e, :], ones_r[:], swa_diag[:, e, :], start=True, stop=True).then_inc(swa_scores_done, 1)

            def swa_pv(j):
                g = j // (PAIRS // 2)
                for e in range(2):
                    pe.wait_ge(swa_probs_ready, 2 * j + e + 1)
                    for qb in range(TB):
                        for kb in range(max(qb - 1, 0), qb + 1):
                            src = 256 * kb + P * (qb - kb)
                            ins = mm(ps[:, 6 + e, qb * P:(qb + 1) * P], swa_vx[:, g, kb, HD * e:HD * e + P],
                                     swa_p[:, e, src:src + P], start=(kb == max(qb - 1, 0)), stop=(kb == qb))
                    ins.then_inc(swa_out_done, 1)

            swa_proj(0, True, (0, 2))
            pe.wait_ge(v_t_ready, 1)
            for b in range(TB):
                ins = nc.tensor.transpose(ps[:, 7, b * P:(b + 1) * P], v_t[:, b * P:(b + 1) * P], ident)
            ins.then_inc(v_turned, 1)
            swa_proj(1, False, (1, 2))
            swa_proj(2, ks=range(4))
            pe.wait_ge(swa_raw_ready, 3)
            for j in range(PAIRS - 1):
                swa_max_scores(j)
                if j == 0:
                    swa_proj(2, False, (2, 6), range(4, KC))
                elif j + 2 < PAIRS:
                    swa_proj(j + 2, False, (j + 2, 2))
                if j == 6:
                    pe.wait_ge(swa_raw_ready, PAIRS + 1)
                    out_piece(1, 0, range(1), range(0, 4))
                    swa_sum(PAIRS)
                if j == 0:
                    pe.wait_ge(swa_v_ready, 1)
                    pe.wait_ge(hankel_lo_ready, 1)
                if j == PAIRS // 2:
                    pe.wait_ge(hankel_lo_ready, 2)
                swa_scores(j)
                swa_pv(j)
            swa_max_scores(PAIRS - 1)
            pe.wait_ge(swa_rstd_refined, 2 * PAIRS + 1)
            out_piece(1, 0, range(1, 2), range(0, 4))
            swa_scores(PAIRS - 1)
            swa_pv(PAIRS - 1)
            out_piece(1, 0, both, range(4, 7))
            out_piece(1, 1, both, range(0, 3))
            out_piece(1, 0, both, range(7, 8))
            out_piece(1, 1, both, range(3, 8))
            proj_out_rest(1)
            mlp_up(2, FILL_MLP1, True, 3)
            mlp_down(2)
            mlp_up(3, FILL_MLP1, False)
            pe.wait_ge(h_written, H_BASE[3])

            def turn_out(n):
                pe.wait_ge(fin_ready, n + 1)
                after(pe, out_copied, n - 1)
                for b in range(TB):
                    ins = nc.tensor.transpose(ps[:, 6 + n % 2, b * P:(b + 1) * P], qkn[:, n % 2, b * P:(b + 1) * P], ident)
                ins.then_inc(fin_turned, 1)

            for n in range(KC):
                after(pe, fin_ready, n - 1)
                down_unit(U_DOWN[3] + n, (U_DOWN[3] + n) % 2, 4 + n % 2, 3 if n == 0 else None)
                if n >= 1:
                    turn_out(n - 1)
            turn_out(KC - 1)


_INS = ["x", "g_attn", "g_mlp", "w_in_a", "b_f", "gq_a", "gk_a", "w_out_a", "g_kv", "w_kv", "gk_b",
        "w_q_b", "gq_b", "sinks", "rel_bias", "w_out_b", "w_up", "w_down"]


def kernel(**inputs):
    import numpy as _np
    import concourse.bacc as _bacc
    from concourse import mybir as _mybir
    from concourse.bass_utils import run_bass_kernel_spmd as _run

    nc = _bacc.Bacc("TRN2", target_bir_lowering=False, num_devices=1)
    arrays, args = {}, []
    for name in _INS + ["shape_consts"]:
        a = shape_constants() if name == "shape_consts" else _np.ascontiguousarray(inputs[name])
        arrays[f"in_{name}"] = a
        args.append(nc.dram_tensor(f"in_{name}", a.shape, _mybir.dt.from_np(a.dtype), kind="ExternalInput").ap())
    out = nc.dram_tensor("out", (1, T, D), _mybir.dt.float32, kind="ExternalOutput").ap()
    build(nc, *args, out)
    r = _run(nc, [arrays], core_ids=[0])
    return r.results[0]["out"]
```
